# Optimizing a Trainium2 kernel written in Bass

```python
import math
import jax, jax.numpy as jnp
from jax import lax
import numpy as np

D_MODEL = 1024
BATCH = 1
SEQ = 512
DEPTH = 2

CHUNK = 64
N_EVEN = (DEPTH + 1) // 2
N_ODD = DEPTH // 2
N_VRES = max(N_ODD - 1, 0)
A_HEADS = D_MODEL // 256
A_DIM = 64
A_VDIM = 2 * A_DIM
ROPE_DIM = A_DIM // 4
ROPE_THETA = 500000.0
Q_BLOCK = 128
SUBLN_EPS = 1e-5
B_HEADS = D_MODEL // 128
B_DIM = 64
B_CHUNKS_BACK = 8
REL_CLIP = 128
A_QK_WIDTH = A_HEADS * 2 * A_DIM
A_V_WIDTH = A_HEADS * A_VDIM
B_WIDTH = B_HEADS * B_DIM
IN_WIDTH = 2 * A_QK_WIDTH + A_V_WIDTH + 3 * B_WIDTH
MIX_WIDTH = A_V_WIDTH + B_WIDTH
C_DIM = 64
C_HEADS = D_MODEL // C_DIM
LORA_W = max(32, round(1.8 * D_MODEL ** 0.5 / 32) * 32)
LORA_A = max(32, round(1.8 * D_MODEL ** 0.5 / 32) * 32)
LORA_V = max(32, round(1.3 * D_MODEL ** 0.5 / 32) * 32)
LORA_G = max(32, round(0.6 * D_MODEL ** 0.8 / 32) * 32)
LNX_EPS = 1e-5 * C_DIM
N_EXPERTS = 32
N_GROUPS = 4
EXPERTS_PER_GROUP = N_EXPERTS // N_GROUPS
TOP_K = 2
D_EXPERT = D_MODEL // 2
MOE_BLOCK = 256
LN_EPS = 1e-5
ALPHA = (2 * DEPTH) ** 0.25
BETA = (8 * DEPTH) ** -0.25
NEG_INF = -1e30

kernel_name = 'hybrid_diffattn_chunkattn_rwkv7_grouped_moe'

def layer_norm(x, g, b):
    xf = x.astype(jnp.float32)
    mu = xf.mean(-1, keepdims=True)
    var = jnp.square(xf - mu).mean(-1, keepdims=True)
    return ((xf - mu) * lax.rsqrt(var + LN_EPS) * g + b).astype(x.dtype)

def partial_rotary(t, pos):
    half = ROPE_DIM // 2
    inv = ROPE_THETA ** (-jnp.arange(half, dtype=jnp.float32) / half)
    ang = pos.astype(jnp.float32)[:, None] * inv
    cos = jnp.cos(ang)[:, None, None, :]
    sin = jnp.sin(ang)[:, None, None, :]
    tr = t[..., :ROPE_DIM].astype(jnp.float32)
    x1, x2 = tr[..., :half], tr[..., half:]
    rot = jnp.concatenate([x1 * cos - x2 * sin, x2 * cos + x1 * sin], axis=-1).astype(t.dtype)
    return jnp.concatenate([rot, t[..., ROPE_DIM:]], axis=-1)

def diff_attention(q, k, v, lam, lam_init, subln_g):
    bn, s_len = q.shape[0], q.shape[1]
    n_blk = s_len // Q_BLOCK
    scale = A_DIM ** -0.5
    key_chunk = jnp.arange(s_len) // CHUNK
    qb = q.reshape(bn, n_blk, Q_BLOCK, A_HEADS, 2, A_DIM).transpose(1, 0, 2, 3, 4, 5)

    def block(args):
        qi, i = args
        s = jnp.einsum('bqhcd,bkhcd->bhcqk', qi, k).astype(jnp.float32) * scale
        q_chunk = (i * Q_BLOCK + jnp.arange(Q_BLOCK)) // CHUNK
        mask = key_chunk[None, :] <= q_chunk[:, None]
        p = jax.nn.softmax(jnp.where(mask, s, NEG_INF), axis=-1)
        pd = p[:, :, 0] - lam * p[:, :, 1]
        o = jnp.einsum('bhqk,bkhe->bqhe', pd.astype(v.dtype), v).astype(jnp.float32)
        o = o * lax.rsqrt(jnp.mean(jnp.square(o), -1, keepdims=True) + SUBLN_EPS) * subln_g * (1.0 - lam_init)
        return o.astype(v.dtype)

    o = lax.map(block, (qb, jnp.arange(n_blk)))
    return o.transpose(1, 0, 2, 3, 4).reshape(bn, s_len, A_V_WIDTH)

def chunk_rel_attention(q, k, v, rel_bias):
    bn, s_len = q.shape[0], q.shape[1]
    n_chunks = s_len // CHUNK
    back = B_CHUNKS_BACK * CHUNK
    band = back + CHUNK
    scale = B_DIM ** -0.5
    kp = jnp.pad(k, ((0, 0), (back, 0), (0, 0), (0, 0)))
    vp = jnp.pad(v, ((0, 0), (back, 0), (0, 0), (0, 0)))
    rel = jnp.clip(jnp.arange(CHUNK)[:, None] + back - jnp.arange(band)[None, :], -REL_CLIP, REL_CLIP) + REL_CLIP
    bias = rel_bias[:, rel].astype(jnp.float32)

    def chunk(c):
        start = c * CHUNK
        qc = lax.dynamic_slice_in_dim(q, start, CHUNK, axis=1)
        kc = lax.dynamic_slice_in_dim(kp, start, band, axis=1)
        vc = lax.dynamic_slice_in_dim(vp, start, band, axis=1)
        s = jnp.einsum('bqhd,bkhd->bhqk', qc, kc).astype(jnp.float32) * scale + bias
        valid = (start - back + jnp.arange(band)) >= 0
        p = jax.nn.softmax(jnp.where(valid, s, NEG_INF), axis=-1)
        return jnp.einsum('bhqk,bkhd->bqhd', p.astype(v.dtype), vc)

    o = lax.map(chunk, jnp.arange(n_chunks))
    return o.transpose(1, 0, 2, 3, 4).reshape(bn, s_len, B_WIDTH)

def even_mixer(x, pos, w_in, w_out, lam_p, subln_g, rel_bias, lam_init):
    bn, s_len, _ = x.shape
    proj = x @ w_in
    cuts = [A_QK_WIDTH, 2 * A_QK_WIDTH, 2 * A_QK_WIDTH + A_V_WIDTH,
            2 * A_QK_WIDTH + A_V_WIDTH + B_WIDTH, 2 * A_QK_WIDTH + A_V_WIDTH + 2 * B_WIDTH]
    aq, ak, av, bq, bk, bv = jnp.split(proj, cuts, axis=-1)
    aq = partial_rotary(aq.reshape(bn, s_len, A_HEADS, 2, A_DIM), pos)
    ak = partial_rotary(ak.reshape(bn, s_len, A_HEADS, 2, A_DIM), pos)
    av = av.reshape(bn, s_len, A_HEADS, A_VDIM)
    lp = lam_p.astype(jnp.float32)
    lam = jnp.exp(jnp.sum(lp[0] * lp[1])) - jnp.exp(jnp.sum(lp[2] * lp[3])) + lam_init
    ya = diff_attention(aq, ak, av, lam, lam_init, subln_g)
    yb = chunk_rel_attention(bq.reshape(bn, s_len, B_HEADS, B_DIM), bk.reshape(bn, s_len, B_HEADS, B_DIM),
                             bv.reshape(bn, s_len, B_HEADS, B_DIM), rel_bias)
    return jnp.concatenate([ya, yb], axis=-1) @ w_out

def wkv7_scan(r, w, k, v, a, b):
    bn = r.shape[0]
    seq_first = lambda t: jnp.moveaxis(t.astype(jnp.float32), 1, 0)
    s0 = jnp.zeros((bn, C_HEADS, C_DIM, C_DIM), jnp.float32)

    def step(state, inp):
        rt, wt, kt, vt, at, bt = inp
        sa = jnp.einsum('bhvk,bhk->bhv', state, at)
        state = state * wt[:, :, None, :] + sa[..., None] * bt[:, :, None, :] + vt[..., None] * kt[:, :, None, :]
        return state, jnp.einsum('bhvk,bhk->bhv', state, rt)

    _, y = lax.scan(step, s0, (seq_first(r), seq_first(w), seq_first(k), seq_first(v), seq_first(a), seq_first(b)))
    return jnp.moveaxis(y, 0, 1)

def rwkv7_mixer(x, v_first, mix, w_rkv, w0, w1, w2, a0, a1, a2, g1, g2, k_k, k_a, r_k, lnx_g, lnx_b, w_out, vres):
    bn, s_len, d = x.shape
    hs = (bn, s_len, C_HEADS, C_DIM)
    xx = jnp.pad(x, ((0, 0), (1, 0), (0, 0)))[:, :-1] - x
    xr, xw, xk, xv, xa, xg = [x + xx * mix[i] for i in range(6)]
    r = xr @ w_rkv[0]
    k = xk @ w_rkv[1]
    v = xv @ w_rkv[2]
    w = -jax.nn.softplus(-(w0 + jnp.tanh(xw @ w1) @ w2).astype(jnp.float32)) - 0.5
    decay = jnp.exp(-jnp.exp(w))
    if vres is None:
        v_first = v
    else:
        v0, v1, v2 = vres
        v = v + (v_first - v) * jax.nn.sigmoid(v0 + (xv @ v1) @ v2)
    a = jax.nn.sigmoid(a0 + (xa @ a1) @ a2)
    g = jax.nn.sigmoid(xg @ g1) @ g2
    kk = (k * k_k).reshape(hs).astype(jnp.float32)
    kk = kk / jnp.maximum(jnp.sqrt(jnp.sum(jnp.square(kk), -1, keepdims=True)), 1e-12)
    k = k * (1.0 + (a - 1.0) * k_a)
    rh, kh, vh, ah = r.reshape(hs), k.reshape(hs), v.reshape(hs), a.reshape(hs)
    y = wkv7_scan(rh, decay.reshape(hs), kh, vh, -kk, kk * ah.astype(jnp.float32))
    mu = y.mean(-1, keepdims=True)
    var = jnp.square(y - mu).mean(-1, keepdims=True)
    y = ((y - mu) * lax.rsqrt(var + LNX_EPS)).reshape(bn, s_len, d) * lnx_g + lnx_b
    bonus = jnp.sum(rh * kh * r_k, -1, keepdims=True) * vh
    y = y.astype(x.dtype) + bonus.reshape(bn, s_len, d)
    return (y * g) @ w_out, v_first

def route(h2, router_w, router_b):
    n = h2.shape[0]
    scores = jax.nn.sigmoid((h2 @ router_w).astype(jnp.float32))
    sel = scores + router_b.astype(jnp.float32)
    grp_score = lax.top_k(sel.reshape(n, N_GROUPS, EXPERTS_PER_GROUP), 2)[0].sum(-1)
    best = jnp.argmax(grp_score, axis=-1)
    in_group = (jnp.arange(N_EXPERTS) // EXPERTS_PER_GROUP)[None, :] == best[:, None]
    _, idx = lax.top_k(jnp.where(in_group, sel, -jnp.inf), TOP_K)
    gate = jnp.take_along_axis(scores, idx, axis=-1)
    return gate / gate.sum(-1, keepdims=True), idx

def moe_ffn(h, router_w, router_b, w_gate, w_up, w_down):
    bn, s_len, d = h.shape
    n = bn * s_len
    h2 = h.reshape(n, d)
    gate, idx = route(h2, router_w, router_b)
    n_rows = n * TOP_K
    flat_e = idx.reshape(-1)
    flat_tok = jnp.arange(n_rows) // TOP_K
    flat_gate = gate.reshape(-1)
    order = jnp.argsort(flat_e)
    e_sorted = flat_e[order]
    counts = jnp.bincount(flat_e, length=N_EXPERTS)
    padded = (counts + MOE_BLOCK - 1) // MOE_BLOCK * MOE_BLOCK
    pad_end = jnp.cumsum(padded)
    pad_start = pad_end - padded
    start = jnp.cumsum(counts) - counts
    dest = pad_start[e_sorted] + jnp.arange(n_rows) - start[e_sorted]
    cap = n_rows + N_EXPERTS * MOE_BLOCK
    n_blocks = cap // MOE_BLOCK
    row_tok = jnp.full((cap,), n, jnp.int32).at[dest].set(flat_tok[order])
    row_gate = jnp.zeros((cap,), jnp.float32).at[dest].set(flat_gate[order])
    block_e = jnp.minimum(jnp.searchsorted(pad_end, jnp.arange(n_blocks) * MOE_BLOCK, side='right'), N_EXPERTS - 1)
    xb = jnp.concatenate([h2, jnp.zeros((1, d), h2.dtype)], axis=0)[row_tok].reshape(n_blocks, MOE_BLOCK, d)

    def expert_block(args):
        xe, e = args
        u = jax.nn.silu(xe @ w_gate[e]) * (xe @ w_up[e])
        return u @ w_down[e]

    yb = lax.map(expert_block, (xb, block_e)).reshape(cap, d)
    yb = yb * row_gate[:, None].astype(yb.dtype)
    out = jax.ops.segment_sum(yb, row_tok, num_segments=n + 1)[:n]
    return out.reshape(bn, s_len, d)

def setup_inputs(seed: int = 0) -> dict:
    key = jax.random.key(seed)
    ks = iter(jax.random.split(key, 40))
    f32 = jnp.float32
    nrm = lambda shape, scale: jax.random.normal(next(ks), shape, f32) * scale
    uni = lambda shape, lo, hi: jax.random.uniform(next(ks), shape, f32, lo, hi)
    D = D_MODEL
    return {
        'x': nrm((BATCH, SEQ, D), 1.0),
        'ln_g': 1.0 + nrm((DEPTH, 2, D), 0.02),
        'ln_b': nrm((DEPTH, 2, D), 0.02),
        'even_w_in': nrm((N_EVEN, D, IN_WIDTH), D ** -0.5),
        'even_w_out': nrm((N_EVEN, MIX_WIDTH, D), MIX_WIDTH ** -0.5 * BETA),
        'even_lambda': nrm((N_EVEN, 4, A_DIM), 0.1),
        'even_subln_g': 1.0 + nrm((N_EVEN, A_VDIM), 0.02),
        'even_rel_bias': nrm((N_EVEN, B_HEADS, 2 * REL_CLIP + 1), 0.2),
        'odd_mix': uni((N_ODD, 6, D), 0.0, 1.0),
        'odd_w_rkv': nrm((N_ODD, 3, D, D), D ** -0.5),
        'odd_w0': uni((N_ODD, D), -6.0, 1.0),
        'odd_w1': nrm((N_ODD, D, LORA_W), D ** -0.5),
        'odd_w2': nrm((N_ODD, LORA_W, D), 0.5 * LORA_W ** -0.5),
        'odd_a0': nrm((N_ODD, D), 0.1),
        'odd_a1': nrm((N_ODD, D, LORA_A), D ** -0.5),
        'odd_a2': nrm((N_ODD, LORA_A, D), 0.5 * LORA_A ** -0.5),
        'odd_g1': nrm((N_ODD, D, LORA_G), D ** -0.5),
        'odd_g2': nrm((N_ODD, LORA_G, D), LORA_G ** -0.5),
        'odd_k_k': 0.85 + nrm((N_ODD, D), 0.05),
        'odd_k_a': 1.0 + nrm((N_ODD, D), 0.05),
        'odd_r_k': nrm((N_ODD, C_HEADS, C_DIM), 0.1),
        'odd_lnx_g': 1.0 + nrm((N_ODD, D), 0.02),
        'odd_lnx_b': nrm((N_ODD, D), 0.02),
        'odd_w_out': nrm((N_ODD, D, D), D ** -0.5 * BETA),
        'vres_v0': 1.0 + nrm((N_VRES, D), 0.1),
        'vres_v1': nrm((N_VRES, D, LORA_V), D ** -0.5),
        'vres_v2': nrm((N_VRES, LORA_V, D), 0.5 * LORA_V ** -0.5),
        'router_w': nrm((D, N_EXPERTS), D ** -0.5),
        'router_b': nrm((N_EXPERTS,), 0.01),
        'moe_w_gate': nrm((DEPTH, N_EXPERTS, D, D_EXPERT), D ** -0.5),
        'moe_w_up': nrm((DEPTH, N_EXPERTS, D, D_EXPERT), D ** -0.5),
        'moe_w_down': nrm((DEPTH, N_EXPERTS, D_EXPERT, D), D_EXPERT ** -0.5 * BETA),
    }

def reference(x, ln_g, ln_b, even_w_in, even_w_out, even_lambda, even_subln_g, even_rel_bias,
              odd_mix, odd_w_rkv, odd_w0, odd_w1, odd_w2, odd_a0, odd_a1, odd_a2, odd_g1, odd_g2,
              odd_k_k, odd_k_a, odd_r_k, odd_lnx_g, odd_lnx_b, odd_w_out, vres_v0, vres_v1, vres_v2,
              router_w, router_b, moe_w_gate, moe_w_up, moe_w_down):
    pos = jnp.arange(x.shape[1])
    v_first = None
    for layer in range(DEPTH):
        if layer % 2 == 0:
            e = layer // 2
            lam_init = 0.8 - 0.6 * math.exp(-0.3 * layer)
            mix_out = even_mixer(x, pos, even_w_in[e], even_w_out[e], even_lambda[e], even_subln_g[e],
                                 even_rel_bias[e], lam_init)
        else:
            o = layer // 2
            vres = None if o == 0 else (vres_v0[o - 1], vres_v1[o - 1], vres_v2[o - 1])
            mix_out, v_first = rwkv7_mixer(x, v_first, odd_mix[o], odd_w_rkv[o], odd_w0[o], odd_w1[o], odd_w2[o],
                                           odd_a0[o], odd_a1[o], odd_a2[o], odd_g1[o], odd_g2[o], odd_k_k[o],
                                           odd_k_a[o], odd_r_k[o], odd_lnx_g[o], odd_lnx_b[o], odd_w_out[o], vres)
        h = layer_norm(ALPHA * x + mix_out, ln_g[layer, 0], ln_b[layer, 0])
        ffn = moe_ffn(h, router_w, router_b, moe_w_gate[layer], moe_w_up[layer], moe_w_down[layer])
        x = layer_norm(ALPHA * h + ffn, ln_g[layer, 1], ln_b[layer, 1])
    return x


_drawn_inputs = setup_inputs


def setup_inputs(seed=0):
    import zlib

    import numpy as np

    out = dict(_drawn_inputs(seed))
    spreads = {}
    factors = {'even_subln_g': 2.698,
     'even_rel_bias': 4.135,
     'odd_w1': 3.953,
     'odd_w2': 4.149,
     'odd_a0': 3.906,
     'odd_lnx_g': 4.064,
     'odd_lnx_b': 6.888}
    for name, (base, spread) in spreads.items():
        noise = np.random.default_rng([zlib.crc32(name.encode()), seed]).standard_normal(out[name].shape)
        drawn = base * np.exp(spread * noise) if base else spread * noise
        out[name] = __import__('jax').numpy.asarray(drawn.astype(out[name].dtype))
    for name, factor in factors.items():
        out[name] = (out[name] * factor).astype(out[name].dtype)
    return out
```

```python
import math
from contextlib import ExitStack

import numpy as np

import concourse.bass as bass
from concourse import mybir

F32 = mybir.dt.float32
F32R = mybir.dt.float32r
U32 = mybir.dt.uint32
I32 = mybir.dt.int32
ALU = mybir.AluOpType
ACT = mybir.ActivationFunctionType
AX = mybir.AxisListType

P = 128
D_MODEL, SEQ, DEPTH = 1024, 512, 2
KD = D_MODEL // P
NT = SEQ // P
CHUNK = 64
N_EXPERTS, N_GROUPS, TOP_K = 32, 4, 2
PER_GROUP = N_EXPERTS // N_GROUPS
D_EXPERT = D_MODEL // 2
KE = D_EXPERT // P
SLOTS = 128
PIECE = KD * D_EXPERT // 2
UNROLL = 4
AHEAD = 2
TURNS = N_EXPERTS // UNROLL
LN_EPS = 1e-5
ALPHA = (2 * DEPTH) ** 0.25
BIG = 3e38
NOWHERE = 1 << 20
A_HEADS, A_DIM, B_HEADS = D_MODEL // 256, 64, D_MODEL // 128
ROPE_DIM, ROPE_THETA, SUBLN_EPS, REL_CLIP = A_DIM // 4, 500000.0, 1e-5, 128
LAMBDA_INIT = 0.8 - 0.6 * math.exp(-0.3 * 0)
NEG_INF = -1e30
N_CHUNKS, PAIRS = SEQ // CHUNK, D_MODEL // 128
LORA_W, LORA_A, LORA_G = 64, 64, 160
LNX_EPS = 1e-5 * CHUNK
PARAM = {"mix": 0, "a0": 6, "k_k": 7, "k_a": 8, "r_k": 9, "lnx_g": 10, "lnx_b": 11}
LEVELS = 6
MASK_IDENT, MASK_BEFORE, MASK_UP_TO, MASK_FIRST_T, MASK_LEVEL = 0, 1, 2, 3, 4
N_MASKS = MASK_LEVEL + LEVELS


class Shared:

    def __init__(self, a, out):
        self.a, self.out = a, out


def shape_constants():
    i = np.arange(P)
    c = {
        "ident": np.eye(P, dtype=np.float32),
        "earlier": (i[:, None] < i[None, :]).astype(np.float32),
        "ones": np.ones((P, P), np.float32),
    }
    e = np.arange(N_EXPERTS)
    c["expert_iota"] = np.tile(e, (P, 1)).astype(np.float32)
    c["group_iota"] = np.tile(e // PER_GROUP, (P, 1)).astype(np.float32)
    c["expert_base"] = np.tile(e * SEQ, (P, 1)).astype(np.float32)
    token = np.arange(SEQ).reshape(NT, P).T
    c["entries"] = np.stack([np.stack([token, TOP_K * token + k], -1) for k in range(TOP_K)], 2).astype(np.uint32)
    c["nowhere"] = np.full((P, 2 * N_EXPERTS * SEQ // P), NOWHERE, np.uint32)
    half = ROPE_DIM // 2
    inv = np.float32(ROPE_THETA) ** (-np.arange(half, dtype=np.float32) / half)
    angle = np.arange(SEQ, dtype=np.float32)[None, :] * inv.astype(np.float32)[:, None]
    cos, sin = np.ones((A_DIM, SEQ), np.float32), np.zeros((A_DIM, SEQ), np.float32)
    cos[:ROPE_DIM], sin[:ROPE_DIM] = np.tile(np.cos(angle), (2, 1)), np.tile(np.sin(angle), (2, 1))
    c["rot_cos"], c["rot_sin"] = np.tile(cos, (2, 1)), np.tile(sin, (2, 1))
    swap = np.zeros((P, P), np.float32)
    for base in (0, A_DIM):
        for d in range(half):
            swap[base + half + d, base + d] = -1.0
            swap[base + d, base + half + d] = 1.0
    c["rot_swap"] = swap
    c["mask_q"] = (i < CHUNK).astype(np.float32)[None, :]
    c["mask_k"] = np.where(i >= CHUNK, np.float32(NEG_INF), np.float32(0.0)).astype(np.float32)[None, :]
    same = i[:, None] // CHUNK == i[None, :] // CHUNK
    c["sum_decay"] = np.where(same & (i[:, None] <= i[None, :]), np.float32(-math.exp(-0.5)), np.float32(0.0)).astype(np.float32)
    c["pair_ones"] = same.astype(np.float32)
    c["pair_mean"] = (same / CHUNK).astype(np.float32)
    r, q = np.arange(CHUNK)[:, None], np.arange(CHUNK)[None, :]
    masks = [r == q, r < q, r <= q, (r % 2 == 0) & (q == r + 1)]
    for level in range(LEVELS):
        size = 2 ** level
        masks.append((r // (2 * size) == q // (2 * size)) & (r // size == q // size + 1))
    c["scan_masks"] = np.tile(np.stack(masks, 1).astype(np.float32), (2, 1, 1))
    return c


def laid_out(inputs):
    query, key = np.arange(P)[:, None] + SEQ - P, np.arange(SEQ)[None, :]
    distance = np.clip(query - key, -REL_CLIP, REL_CLIP) + REL_CLIP
    vectors = [*np.asarray(inputs["odd_mix"])[0]]
    vectors += [np.asarray(inputs[name])[0].reshape(-1) for name in ("odd_a0", "odd_k_k", "odd_k_a", "odd_r_k", "odd_lnx_g", "odd_lnx_b")]
    return {
        "params": np.ascontiguousarray(np.stack(vectors).reshape(len(vectors), KD, P).transpose(2, 0, 1)),
        "x_T": np.ascontiguousarray(np.asarray(inputs["x"])[0].T),
        "rel_bias_rows": np.ascontiguousarray(np.asarray(inputs["even_rel_bias"])[0][:, distance].transpose(1, 0, 2)),
    }


class Chain:

    def __init__(self, engine, steps_done):
        self.engine, self.steps_done = engine, steps_done
        self.count, self.ahead = 0, 0

    def link(self, instruction):
        self.mark(instruction)
        self.wait()

    def mark(self, instruction):
        instruction.then_inc(self.steps_done, 1)
        self.count += 1

    def wait(self):
        self.engine.wait_ge(self.steps_done, self.ahead + self.count)


def norm_moments(nc, chain, pre, stats, moments, var_ready):
    for half in range(2):
        chain.mark(nc.vector.bn_stats(stats[:, half, :], pre[:, half * 512:(half + 1) * 512]))
    chain.wait()
    nc.vector.bn_aggr(moments[:, 0:2], stats[:, :, :]).then_inc(var_ready, 1)


def roots(nc, act, moments, eps, tiles, var_ready, root_ready):
    for t in range(tiles):
        act.wait_ge(var_ready, t + 1)
        nc.scalar.activation(moments[:, t, 2:3], moments[:, t, 1:2], ACT.Sqrt, bias=eps).then_inc(root_ready, 1)


def norm_apply(nc, chain, pre, moments, gain, bias, out):
    chain.link(nc.vector.reciprocal(moments[:, 2:3], moments[:, 2:3]))
    chain.link(nc.vector.tensor_scalar(pre, pre, moments[:, 0:1], moments[:, 2:3], ALU.subtract, ALU.mult))
    chain.link(nc.vector.tensor_tensor(pre, pre, gain, ALU.mult))
    return nc.vector.tensor_tensor(out, pre, bias, ALU.add)


def clear_semaphores(nc, semaphores):
    with nc.Block() as block:
        @block.gpsimd
        def _(pool):
            for s in semaphores:
                pool.sem_clear(s)


def moe_route(nc, m, layer):
    with ExitStack() as ctx:
        def sb(name, shape, dt=F32):
            return ctx.enter_context(nc.sbuf_tensor(f"{name}_r{layer}", shape, dt))

        hidden_T = sb("hidden_T", [P, KD, SEQ])
        scores = sb("scores", [P, NT, N_EXPERTS])
        select = sb("select", [P, NT, N_EXPERTS])
        group_top = sb("group_top", [P, NT, N_GROUPS, 8])
        group_score = sb("group_score", [P, NT, 8])
        group_best = sb("group_best", [P, NT, 8])
        group_index = sb("group_index", [P, NT, 8], U32)
        group_of_token = sb("group_of_token", [P, NT])
        penalty = sb("penalty", [P, NT, N_EXPERTS])
        expert_best = sb("expert_best", [P, NT, 8])
        expert_index = sb("expert_index", [P, NT, 8], U32)
        expert_of_token = sb("expert_of_token", [P, NT, TOP_K])
        chosen = sb("chosen", [P, NT, TOP_K, N_EXPERTS])
        product = sb("product", [P, NT, TOP_K, N_EXPERTS])
        chosen_any = sb("chosen_any", [P, NT, N_EXPERTS])
        slot_value = sb("slot_value", [P, NT, N_EXPERTS])
        gate_raw = sb("gate_raw", [P, NT, TOP_K])
        gate_sum = sb("gate_sum", [P, NT])
        slot_f = sb("slot_f", [P, NT, TOP_K])
        slot_u = sb("slot_u", [P, NT, TOP_K], U32)
        most_f = sb("most_f", [1, 1])
        psum_T = [ctx.enter_context(nc.psum_tensor(f"psum_T{i}_r{layer}", [P, 512], F32)) for i in range(4)]
        psum_logits = ctx.enter_context(nc.psum_tensor(f"psum_logits_r{layer}", [P, NT, N_EXPERTS], F32))
        psum_rank = ctx.enter_context(nc.psum_tensor(f"psum_rank_r{layer}", [P, NT + 1, N_EXPERTS], F32))
        table_entry = m.table_entry[layer]
        nowhere = sb("nowhere", [P, 2 * N_EXPERTS * SEQ // P], U32)
        router_w, router_b = sb("router_w", [P, KD, N_EXPERTS]), sb("router_b", [P, N_EXPERTS])
        names = ("hidden_stored", "table_empty", "transposed", "copied_act", "copied_dve", "logits", "scores", "chosen", "rank", "slots",
                 "dve_steps", "router_loaded", "nowhere_loaded")
        S = [ctx.enter_context(nc.semaphore(f"{name}_r{layer}")) for name in names]
        (hidden_stored, table_empty, transposed, copied_act, copied_dve, logits_ready,
         scores_ready, chosen_ready, rank_ready, slots_ready, dve_steps, router_loaded, nowhere_loaded) = S
        block = ctx.enter_context(nc.Block())

        @block.sync
        def _(sp):
            sp.dma_start(router_w[:], m.a["router_w"].rearrange("(k p) e -> p k e", p=P)).then_inc(router_loaded, 16)
            sp.dma_start(router_b[:], m.a["router_b"].partition_broadcast(P)).then_inc(router_loaded, 16)
            sp.dma_start(nowhere[:], m.a["nowhere"]).then_inc(nowhere_loaded, 16)
            sp.wait_ge(nowhere_loaded, 16)
            sp.dma_start(m.table.rearrange("(p n) c -> p (n c)", p=P), nowhere[:]).then_inc(table_empty, 16)
            sp.dma_start(m.h_dram.rearrange("(t p) d -> p t d", p=P), m.stream[:]).then_inc(hidden_stored, 16)
            load_expert(nc, sp, m, layer, 0, (("down", 0), ("down", 1)))
            sp.wait_ge(hidden_stored, 16)

        @block.tensor
        def _(pe):
            for n in range(2 * NT):
                t, half = n // 2, n % 2
                if n >= 4:
                    pe.wait_ge(copied_dve if n % 2 else copied_act, n // 2 - 1)
                for j in range(4):
                    k = 4 * half + j
                    last = nc.tensor.transpose(psum_T[n % 4][:, j * P:(j + 1) * P], m.stream[:, t, k * P:(k + 1) * P], m.ident[:])
                last.then_inc(transposed, 1)
            pe.wait_ge(router_loaded, 32)
            for t in range(NT):
                pe.wait_ge(copied_act, t + 1)
                pe.wait_ge(copied_dve, t + 1)
                for k in range(KD):
                    last = nc.tensor.matmul(psum_logits[:, t, :], hidden_T[:, k, t * P:(t + 1) * P], router_w[:, k, :],
                                            start=(k == 0), stop=(k == KD - 1))
            last.then_inc(logits_ready, 1)
            pe.wait_ge(chosen_ready, 1)
            for t in range(NT):
                for j in range(t + 1):
                    nc.tensor.matmul(psum_rank[:, t, :], (m.earlier if j == t else m.ones)[:], chosen_any[:, j, :],
                                     start=(j == 0), stop=(j == t))
            for j in range(NT):
                last = nc.tensor.matmul(psum_rank[:, NT, :], m.ones[:], chosen_any[:, j, :], start=(j == 0), stop=(j == NT - 1))
            last.then_inc(rank_ready, 1)

        @block.scalar
        def _(act):
            for t in range(NT):
                act.wait_ge(transposed, 2 * t + 1)
                nc.scalar.copy(hidden_T[:, 0:4, t * P:(t + 1) * P], psum_T[2 * t % 4][:].rearrange("p (j n) -> p j n", j=4)).then_inc(copied_act, 1)
            act.wait_ge(logits_ready, 1)
            nc.scalar.activation(scores[:], psum_logits[:], ACT.Sigmoid).then_inc(scores_ready, 1)

        @block.vector
        def _(dve):
            c = Chain(dve, dve_steps)
            c.link(nc.vector.memset(group_score[:], -BIG))
            for t in range(NT):
                dve.wait_ge(transposed, 2 * t + 2)
                nc.vector.tensor_copy(hidden_T[:, 4:8, t * P:(t + 1) * P], psum_T[(2 * t + 1) % 4][:].rearrange("p (j n) -> p j n", j=4)).then_inc(copied_dve, 1)
            dve.wait_ge(scores_ready, 1)
            dve.wait_ge(router_loaded, 32)
            c.link(nc.vector.tensor_tensor(select[:], scores[:], router_b[:].unsqueeze(1).to_broadcast([P, NT, N_EXPERTS]), ALU.add))
            for t in range(NT):
                for g in range(N_GROUPS):
                    c.mark(nc.vector.max(group_top[:, t, g, :], select[:, t, g * PER_GROUP:(g + 1) * PER_GROUP]))
            c.wait()
            c.link(nc.vector.tensor_tensor(group_score[:, :, 0:N_GROUPS], group_top[:, :, :, 0], group_top[:, :, :, 1], ALU.add))
            for t in range(NT):
                c.mark(nc.vector.max(group_best[:, t, :], group_score[:, t, :]))
            c.wait()
            for t in range(NT):
                c.mark(nc.vector.max_index(group_index[:, t, :], group_best[:, t, :], group_score[:, t, :]))
            c.wait()
            c.link(nc.vector.tensor_copy(group_of_token[:], group_index[:, :, 0]))
            for t in range(NT):
                c.mark(nc.vector.tensor_scalar(penalty[:, t, :], m.group_iota[:], group_of_token[:, t:t + 1], -BIG, ALU.not_equal, ALU.mult))
            c.wait()
            c.link(nc.vector.tensor_tensor(select[:], select[:], penalty[:], ALU.add))
            for t in range(NT):
                c.mark(nc.vector.max(expert_best[:, t, :], select[:, t, :]))
            c.wait()
            for t in range(NT):
                c.mark(nc.vector.max_index(expert_index[:, t, :], expert_best[:, t, :], select[:, t, :]))
            c.wait()
            c.link(nc.vector.tensor_copy(expert_of_token[:], expert_index[:, :, 0:TOP_K]))
            for t in range(NT):
                for k in range(TOP_K):
                    c.mark(nc.vector.tensor_scalar(chosen[:, t, k, :], m.expert_iota[:], expert_of_token[:, t, k:k + 1], None, ALU.is_equal))
            c.wait()
            nc.vector.tensor_tensor(chosen_any[:], chosen[:, :, 0, :], chosen[:, :, 1, :], ALU.add).then_inc(chosen_ready, 1)
            for k in range(TOP_K):
                c.mark(nc.vector.tensor_tensor(product[:, :, k, :], chosen[:, :, k, :], scores[:], ALU.mult))
            c.wait()
            c.link(nc.vector.tensor_reduce(gate_raw[:], product[:], AX.X, ALU.add))
            c.link(nc.vector.tensor_tensor(gate_sum[:], gate_raw[:, :, 0], gate_raw[:, :, 1], ALU.add))
            c.link(nc.vector.reciprocal(gate_sum[:], gate_sum[:]))
            for k in range(TOP_K):
                c.mark(nc.vector.tensor_tensor(m.gates[:, :, k], gate_raw[:, :, k], gate_sum[:], ALU.mult))
            dve.wait_ge(rank_ready, 1)
            c.link(nc.vector.tensor_tensor(slot_value[:], psum_rank[:, 0:NT, :], m.expert_base[:].unsqueeze(1).to_broadcast([P, NT, N_EXPERTS]), ALU.add))
            for k in range(TOP_K):
                c.mark(nc.vector.tensor_tensor(product[:, :, k, :], chosen[:, :, k, :], slot_value[:], ALU.mult))
            c.wait()
            c.link(nc.vector.tensor_reduce(slot_f[:], product[:], AX.X, ALU.add))
            nc.vector.tensor_copy(slot_u[:], slot_f[:]).then_inc(slots_ready, 1)
            c.link(nc.vector.tensor_reduce(most_f[:], psum_rank[0:1, NT, :], AX.X, ALU.max))
            c.link(nc.vector.tensor_copy(m.most_tokens[:], most_f[:]))

        @block.gpsimd
        def _(pool):
            for rows in m.x_rows:
                pool.memset(rows[:], 0.0)
            pool.wait_ge(table_empty, 16)
            pool.wait_ge(slots_ready, 1)
            for t in range(NT):
                for k in range(TOP_K):
                    nc.gpsimd.indirect_dma_start(
                        m.table[:, :], bass.IndirectOffsetOnAxis(ap=slot_u[:, t, k:k + 1], axis=0),
                        m.entries[:, t, k, :], None, bounds_check=N_EXPERTS * SEQ - 1, oob_is_err=False).then_inc(table_entry, 16)
            pool.wait_ge(table_entry, 16 * NT * TOP_K)
    clear_semaphores(nc, S)


def load_expert(nc, engine, m, layer, e, parts):
    for part, half in parts:
        raw = m.w_raw[part]
        k = raw.shape[1] // 2
        rows = m.a[f"moe_w_{part}"][layer, e].rearrange("(p k) n -> p k n", p=P)
        engine.dma_start(raw[:, half * k:(half + 1) * k, :], rows[:, half * k:(half + 1) * k, :]).then_inc(m.w_loaded[part][half], 16)


def moe_experts(nc, m, layer):
    with ExitStack() as ctx:
        def ring(name, n, shape, dt=F32):
            return [ctx.enter_context(nc.sbuf_tensor(f"{name}{i}_e{layer}", shape, dt)) for i in range(n)]

        def bank(name):
            return ctx.enter_context(nc.psum_tensor(f"{name}_e{layer}", [P, 512], F32))

        x_high, x_low = ring("x_high", 2, [P, KD, SLOTS], F32R), ring("x_low", 2, [P, KD, SLOTS], F32R)
        silu = ring("silu", 1, [P, D_EXPERT])[0]
        u = ring("u", 1, [P, D_EXPERT])[0]
        u_high, u_low = [ring(name, 1, [P, KE, SLOTS], F32R)[0] for name in ("u_high", "u_low")]
        y = ring("y", 2, [P, D_MODEL])
        w_high, w_low = [{part: ring(f"{name}_{part}", 1, m.w_raw[part].shape, F32R)[0] for part in ("gate", "up", "down")} for name in ("w_high", "w_low")]
        x, slots = m.x_rows, m.slot_rows
        psum_gate, psum_up, psum_uT = bank("psum_gate"), bank("psum_up"), bank("psum_uT")
        psum_xT = [bank("psum_xT0"), bank("psum_xT1")]
        psum_y = [bank("psum_y0"), bank("psum_y1")]
        names = ("x_transposed", "x_high_made", "x_low_made", "gate_done", "up_done", "silu_done", "u_done", "u_transposed", "u_high_made",
                 "u_low_made", "down_done", "y_copied", "high_made", "low_made", "slots_loaded0", "slots_loaded1", "slots_loaded2", "slots_loaded3",
                 "gathers_begun", "scatters_begun")
        S = [ctx.enter_context(nc.semaphore(f"{name}_e{layer}")) for name in names]
        (x_transposed, x_high_made, x_low_made, gate_done, up_done, silu_done, u_done, u_transposed,
         u_high_made, u_low_made, down_done, y_copied, high_made, low_made) = S[:14]
        slots_loaded = S[14:18]
        gathers_begun, scatters_begun = S[18:20]
        x_gathered, y_scattered = m.x_gathered[layer], m.y_scattered[layer]

        def is_main(j):
            return isinstance(j, int)

        def one_pass(engine, begin, body, turns_done, j):
            begin(turns_done, j)
            peeled = 1 if is_main(j) else 0
            for i in range(UNROLL * peeled):
                body(turns_done, i, i, j, False)
            with engine.Fori(peeled, TURNS - 1) as turn:
                for i in range(UNROLL):
                    body(turns_done + turn, i, turn * UNROLL + i, j, False)
            for i in range(UNROLL):
                body(turns_done + (TURNS - 1), i, N_EXPERTS - UNROLL + i, j, True)

        def run(engine, begin, body):
            one_pass(engine, begin, body, 0, 0)
            most = engine.value_load(m.most_tokens[0:1, 0:1], min_val=0, max_val=SEQ)
            with engine.If(most > SLOTS):
                with engine.Fori(1, SEQ // SLOTS) as again:
                    one_pass(engine, begin, body, again * TURNS, again)

        FIRST_GATE, UP, NEXT_GATE, DOWN, LAST_DOWN, NEXT_UP = 0, 2, 4, 6, 4, 8

        def piece(part, half):
            k = m.w_raw[part].shape[1] // 2
            return [t[part][:, half * k:(half + 1) * k, :] for t in (m.w_raw, w_high, w_low)]

        def make_high(act, part, n, halves=(0, 1)):
            for half in halves:
                raw, high, low = piece(part, half)
                act.wait_ge(m.w_loaded[part][half], 16 * (n + 1))
                nc.scalar.copy(high, raw).then_inc(high_made, 1)

        def make_low(dve, part, n, where, halves=(0, 1)):
            for half in halves:
                raw, high, low = piece(part, half)
                dve.wait_ge(high_made, 6 * n + where + half + 1)
                nc.vector.tensor_tensor(low, raw, high.bitcast(F32), ALU.subtract).then_inc(low_made, 1)

        def product(pe, outs, high, low, part, n, where):
            k_tiles = m.w_raw[part].shape[1]
            for half in range(2):
                raw, piece_high, piece_low = piece(part, half)
                pe.wait_ge(low_made, 6 * n + where + half + 1)
                for q, out in enumerate(outs):
                    cols = slice(q * 512, (q + 1) * 512)
                    for j in range(k_tiles // 2):
                        k = half * (k_tiles // 2) + j
                        for x_part, w_part, first in ((high, piece_high, True), (high, piece_low, False), (low, piece_high, False)):
                            mm = nc.tensor.matmul(out[:], x_part[:, k, :], w_part[:, j, cols],
                                                  start=(k == 0 and first), stop=(k == k_tiles - 1 and x_part is low))
            return mm

        block = ctx.enter_context(nc.Block())

        @block.sync
        def _(sp):
            lists = m.table.rearrange("(n s) c -> n s c", s=SLOTS)

            def load_slots(e, i, j):
                sp.dma_start(slots[i][:], lists[e * (SEQ // SLOTS) + j]).then_inc(slots_loaded[i], 16)

            def begin(T, j):
                for i in range(UNROLL - 1):
                    if not is_main(j):
                        sp.wait_ge(y_scattered[i % 2], 16 * 2 * T)
                    load_slots(i, i, j)
                if not is_main(j):
                    sp.wait_ge(low_made, 6 * UNROLL * T)
                    load_expert(nc, sp, m, layer, 0, [(part, half) for part in ("gate", "up", "down") for half in range(2)])
                refill(1, "gate", T * UNROLL, FIRST_GATE)
                refill(1, "up", T * UNROLL, UP)

            def refill(e, part, n, where):
                for half in range(2):
                    sp.wait_ge(low_made, 6 * n + where + half + 1)
                    load_expert(nc, sp, m, layer, e, ((part, half),))

            def body(T, i, e, j, last):
                n = T * UNROLL + i
                ahead = not (last and i == UNROLL - 1)
                if not (last and i >= 2):
                    refill(e + 2, "gate", n, NEXT_GATE)
                if ahead:
                    refill(e + 1, "down", n, DOWN)
                if not (last and i >= 2):
                    refill(e + 2, "up", n, NEXT_UP)
                if not last or i == 0:
                    sp.wait_ge(y_scattered[(i + 1) % 2], 16 * (2 * T + (i + 1) // 2))
                    load_slots(e + UNROLL - 1, (i + UNROLL - 1) % UNROLL, j)
            run(sp, begin, body)

        @block.gpsimd
        def _(pool):
            def gather(i, times):
                pool.wait_ge(slots_loaded[i], 16 * times)
                pool.sem_inc(gathers_begun, 1)
                nc.gpsimd.indirect_dma_start(x[i % 2][:], None, m.h_dram[:, :], bass.IndirectOffsetOnAxis(ap=slots[i][:, 0:1], axis=0),
                                             bounds_check=SEQ - 1, oob_is_err=False).then_inc(x_gathered[i], 16)

            def begin(T, j):
                if not is_main(j):
                    pool.wait_ge(x_transposed, UNROLL * T)
                for i in range(AHEAD):
                    gather(i, T + 1)

            def body(T, i, e, j, last):
                n = T * UNROLL + i
                if not (last and i >= UNROLL - AHEAD):
                    pool.wait_ge(x_transposed, n + 1)
                    gather((i + AHEAD) % UNROLL, T + 1 + (i + AHEAD) // UNROLL)
                pool.wait_ge(y_copied, 2 * n + 2)
                pool.sem_inc(scatters_begun, 1)
                nc.gpsimd.indirect_dma_start(m.y_dram[:, :], bass.IndirectOffsetOnAxis(ap=slots[i][:, 1:2], axis=0), y[i % 2][:], None,
                                             bounds_check=SEQ * TOP_K - 1, oob_is_err=False).then_inc(y_scattered[i % 2], 16)
                if last and i == UNROLL - 1:
                    for b in range(2):
                        pool.wait_ge(y_scattered[b], 16 * (2 * T + 2))
            run(pool, begin, body)

        @block.tensor
        def _(pe):
            def transpose_x(n, b, times):
                pe.wait_ge(x_gathered[b], 16 * times)
                pe.wait_ge(x_low_made, n)
                for half in range(2):
                    for q in range(4):
                        k = 4 * half + q
                        last = nc.tensor.transpose(psum_xT[half][:, q * SLOTS:(q + 1) * SLOTS], x[b % 2][:].rearrange("s (p k) -> s k p", k=KD)[:, k, :], m.ident[:])
                last.then_inc(x_transposed, 1)

            def gate(n, b, body_n, where):
                pe.wait_ge(x_low_made, n + 1)
                pe.wait_ge(silu_done, n)
                mm = product(pe, [psum_gate], x_high[b], x_low[b], "gate", body_n, where)
                mm.then_inc(gate_done, 1)

            def begin(T, j):
                transpose_x(T * UNROLL, 0, T + 1)
                gate(T * UNROLL, 0, T * UNROLL, FIRST_GATE)

            def body(T, i, e, j, last):
                n, b = T * UNROLL + i, i % 2
                ahead = not (last and i == UNROLL - 1)
                if ahead:
                    transpose_x(n + 1, (i + 1) % UNROLL, T + 1 + (i + 1) // UNROLL)
                pe.wait_ge(u_done, n)
                product(pe, [psum_up], x_high[b], x_low[b], "up", n, UP).then_inc(up_done, 1)
                pe.wait_ge(u_done, n + 1)
                pe.wait_ge(u_low_made, n)
                for q in range(KE):
                    mm = nc.tensor.transpose(psum_uT[:, q * SLOTS:(q + 1) * SLOTS], u[:].rearrange("s (p q) -> s q p", q=KE)[:, q, :], m.ident[:])
                mm.then_inc(u_transposed, 1)
                if ahead:
                    gate(n + 1, 1 - b, n, NEXT_GATE)
                pe.wait_ge(u_low_made, n + 1)
                pe.wait_ge(y_copied, 2 * n)
                product(pe, psum_y, u_high, u_low, "down", n, DOWN if ahead else LAST_DOWN).then_inc(down_done, 1)
            run(pe, begin, body)

        @block.scalar
        def _(act):
            def split_x(n, b):
                act.wait_ge(x_transposed, n + 1)
                for half in range(2):
                    nc.scalar.copy(x_high[b][:, 4 * half:4 * half + 4, :], psum_xT[half][:].rearrange("p (q s) -> p q s", q=4)).then_inc(x_high_made, 1)

            def begin(T, j):
                split_x(T * UNROLL, 0)
                make_high(act, "gate", T * UNROLL)
                make_high(act, "up", T * UNROLL)

            def body(T, i, e, j, last):
                n, b = T * UNROLL + i, i % 2
                ahead = not (last and i == UNROLL - 1)
                if ahead:
                    split_x(n + 1, 1 - b)
                    act.wait_ge(gate_done, n + 1)
                    make_high(act, "gate", n + 1, halves=(0,))
                act.wait_ge(gate_done, n + 1)
                act.wait_ge(u_done, n)
                nc.scalar.activation(silu[:], psum_gate[:], ACT.Silu).then_inc(silu_done, 1)
                if ahead:
                    make_high(act, "gate", n + 1, halves=(1,))
                act.wait_ge(u_transposed, n + 1)
                act.wait_ge(down_done, n)
                nc.scalar.copy(u_high[:], psum_uT[:].rearrange("p (q s) -> p q s", q=KE)).then_inc(u_high_made, 1)
                make_high(act, "down", n)
                if ahead:
                    act.wait_ge(up_done, n + 1)
                    make_high(act, "up", n + 1)
                act.wait_ge(down_done, n + 1)
                act.wait_ge(y_scattered[i % 2], 16 * (2 * T + i // 2))
                for half in range(2):
                    nc.scalar.copy(y[i % 2][:, half * 512:(half + 1) * 512], psum_y[half][:]).then_inc(y_copied, 1)
            run(act, begin, body)

        @block.vector
        def _(dve):
            def split_x(n, b):
                for half in range(2):
                    dve.wait_ge(x_high_made, 2 * n + half + 1)
                    low = nc.vector.tensor_tensor(x_low[b][:, 4 * half:4 * half + 4, :], psum_xT[half][:].rearrange("p (q s) -> p q s", q=4),
                                                  x_high[b][:, 4 * half:4 * half + 4, :].bitcast(F32), ALU.subtract)
                low.then_inc(x_low_made, 1)

            def begin(T, j):
                split_x(T * UNROLL, 0)
                make_low(dve, "gate", T * UNROLL, FIRST_GATE)
                make_low(dve, "up", T * UNROLL, UP)

            def body(T, i, e, j, last):
                n, b = T * UNROLL + i, i % 2
                ahead = not (last and i == UNROLL - 1)
                if ahead:
                    split_x(n + 1, 1 - b)
                    make_low(dve, "gate", n, NEXT_GATE, halves=(0,))
                dve.wait_ge(silu_done, n + 1)
                dve.wait_ge(up_done, n + 1)
                dve.wait_ge(u_transposed, n)
                nc.vector.tensor_tensor(u[:], silu[:], psum_up[:], ALU.mult).then_inc(u_done, 1)
                if ahead:
                    make_low(dve, "gate", n, NEXT_GATE, halves=(1,))
                dve.wait_ge(u_high_made, n + 1)
                nc.vector.tensor_tensor(u_low[:], psum_uT[:].rearrange("p (q s) -> p q s", q=KE), u_high[:].bitcast(F32), ALU.subtract).then_inc(u_low_made, 1)
                make_low(dve, "down", n, DOWN if ahead else LAST_DOWN)
                if ahead:
                    make_low(dve, "up", n, NEXT_UP)
            run(dve, begin, body)
    clear_semaphores(nc, [*S, *m.w_loaded["gate"], *m.w_loaded["up"], *m.w_loaded["down"]])


def moe_combine(nc, m, layer):
    last_layer = layer == DEPTH - 1
    with ExitStack() as ctx:
        ln_gain, ln_bias = [ctx.enter_context(nc.sbuf_tensor(f"{name}_c{layer}", [P, D_MODEL], F32)) for name in ("ln_gain", "ln_bias")]
        pair = [ctx.enter_context(nc.sbuf_tensor(f"pair{i}_c{layer}", [P, TOP_K, D_MODEL], F32)) for i in range(NT)]
        names = ("norm_loaded", "tile_done", "dve_steps", "stored", "var_ready", "root_ready")
        S = [ctx.enter_context(nc.semaphore(f"{name}_c{layer}")) for name in names]
        norm_loaded, tile_done, dve_steps, stored, var_ready, root_ready = S
        pair_loaded = [ctx.enter_context(nc.semaphore(f"pair_loaded{t}_c{layer}")) for t in range(NT)]
        block = ctx.enter_context(nc.Block())

        @block.sync
        def _(sp):
            rows = m.y_dram.rearrange("(t p k) d -> t p k d", p=P, k=TOP_K)
            for t in range(NT):
                sp.dma_start(pair[t][:], rows[t]).then_inc(pair_loaded[t], 16)
            sp.dma_start(ln_gain[:], m.a["ln_g"][layer, 1].partition_broadcast(P)).then_inc(norm_loaded, 16)
            sp.dma_start(ln_bias[:], m.a["ln_b"][layer, 1].partition_broadcast(P)).then_inc(norm_loaded, 16)
            if last_layer:
                for t in range(NT):
                    sp.wait_ge(tile_done, t + 1)
                    sp.dma_start(m.out.rearrange("b (t p) d -> (b t) p d", p=P)[t], m.stream[:, t, :]).then_inc(stored, 16)
                sp.wait_ge(stored, 16 * NT)

        @block.scalar
        def _(act):
            roots(nc, act, m.moments, m.ln_eps[:], NT, var_ready, root_ready)

        @block.vector
        def _(dve):
            c = Chain(dve, dve_steps)

            def combine(t):
                dve.wait_ge(pair_loaded[t], 16)
                first, second = pair[t][:, 0, :], pair[t][:, 1, :]
                c.link(nc.vector.tensor_scalar(first, first, m.gates[:, t, 0:1], None, ALU.mult))
                c.link(nc.vector.scalar_tensor_tensor(out=first, in0=second, scalar=m.gates[:, t, 1:2], in1=first, op0=ALU.mult, op1=ALU.add))
                c.link(nc.vector.scalar_tensor_tensor(out=first, in0=m.stream[:, t, :], scalar=ALPHA, in1=first, op0=ALU.mult, op1=ALU.add))
                norm_moments(nc, c, first, m.stats, m.moments[:, t, :], var_ready)

            def normalise(t):
                dve.wait_ge(root_ready, t + 1)
                norm_apply(nc, c, pair[t][:, 0, :], m.moments[:, t, :], ln_gain[:], ln_bias[:], m.stream[:, t, :]).then_inc(tile_done, 1)

            combine(0)
            dve.wait_ge(norm_loaded, 32)
            for t in range(NT):
                if t + 1 < NT:
                    combine(t + 1)
                normalise(t)
    clear_semaphores(nc, [*S, *pair_loaded])


def attention_project(nc, m, heads_T, values):
    with ExitStack() as ctx:
        def sb(name, shape, dt=F32):
            return ctx.enter_context(nc.sbuf_tensor(name, shape, dt))

        sems = []

        def sem(name):
            sems.append(ctx.enter_context(nc.semaphore(name)))
            return sems[-1]

        x_T = sb("x_T", [P, KD, SEQ])
        weights = [sb(f"w_in{i}", [P, KD, 512]) for i in range(2)]
        rot_cos, rot_sin, rot_swap = sb("rot_cos", [P, SEQ]), sb("rot_sin", [P, SEQ]), sb("rot_swap", [P, P])
        turned = [sb(f"turned{i}", [P, SEQ]) for i in range(2)]
        banks = [ctx.enter_context(nc.psum_tensor(f"psum_proj{i}", [P, 512], F32)) for i in range(4)]
        swap_banks = [ctx.enter_context(nc.psum_tensor(f"psum_swap{i}", [P, 512], F32)) for i in range(2)]
        x_loaded, rot_loaded = sem("x_loaded"), sem("rot_loaded")
        w_loaded = [sem(f"w_in_loaded{i}") for i in range(2)]
        tile_ready, copied_act, copied_dve = sem("proj_ready"), sem("proj_copied_act"), sem("proj_copied_dve")
        swapped, rotated, dve_steps = sem("swapped"), sem("rotated"), sem("proj_dve_steps")
        w_in = m.a["even_w_in"][0].rearrange("(k p) n -> p k n", p=P)
        columns = [0, 1, 3, 4, 2, 5]
        block = ctx.enter_context(nc.Block())

        @block.sync
        def _(sp):
            for g, col in enumerate(columns):
                if g >= 2:
                    sp.wait_ge(tile_ready, 4 * (g - 1))
                sp.dma_start(weights[g % 2][:], w_in[:, :, col * 512:(col + 1) * 512]).then_inc(w_loaded[g % 2], 16)
                if g == 0:
                    sp.dma_start(x_T[:], m.a["x_T"].rearrange("(k p) t -> p k t", p=P)).then_inc(x_loaded, 16)
                    for tile_, name in ((rot_cos, "rot_cos"), (rot_sin, "rot_sin"), (rot_swap, "rot_swap")):
                        sp.dma_start(tile_[:], m.a[name]).then_inc(rot_loaded, 16)
            load_expert(nc, sp, m, 0, 0, m.first_weights)

        @block.tensor
        def _(pe):
            def tile_of(g, f):
                n = 4 * g + f
                if f == 0:
                    pe.wait_ge(w_loaded[g % 2], 16 * (g // 2 + 1))
                if n >= 4:
                    pe.wait_ge(copied_dve if n % 2 else copied_act, n // 2 - 1)
                for k in range(KD):
                    if g < 4:
                        left, right = weights[g % 2][:, k, f * P:(f + 1) * P], x_T[:, k, :]
                    else:
                        left, right = x_T[:, k, f * P:(f + 1) * P], weights[g % 2][:, k, :]
                    mm = nc.tensor.matmul(banks[f][:], left, right, start=(k == 0), stop=(k == KD - 1))
                mm.then_inc(tile_ready, 1)

            def swap(r):
                if r == 0:
                    pe.wait_ge(rot_loaded, 48)
                pe.wait_ge(copied_dve if r % 2 else copied_act, r // 2 + 1)
                if r >= 2:
                    pe.wait_ge(rotated, r - 1)
                nc.tensor.matmul(swap_banks[r % 2][:], rot_swap[:], heads_T[:, r, :], start=True, stop=True).then_inc(swapped, 1)

            pe.wait_ge(x_loaded, 16)
            for g in range(6):
                for f in range(4):
                    tile_of(g, f)
                    if 1 <= g < 3:
                        swap(4 * (g - 1) + f)

        @block.scalar
        def _(act):
            for n in range(0, 24, 2):
                act.wait_ge(tile_ready, n + 1)
                out = heads_T[:, n, :] if n < 16 else values[:, (n - 16) // 4, n % 4, :]
                scale = A_DIM ** -0.5 if n // 4 in (0, 2) else 1.0
                nc.scalar.activation(out, banks[n % 4][:], ACT.Copy, scale=scale).then_inc(copied_act, 1)

        @block.vector
        def _(dve):
            c = Chain(dve, dve_steps)

            def rotate(r):
                x = heads_T[:, r, :]
                dve.wait_ge(swapped, r + 1)
                c.mark(nc.vector.tensor_tensor(turned[r % 2][:], swap_banks[r % 2][:], rot_sin[:], ALU.mult))
                c.link(nc.vector.tensor_tensor(x, x, rot_cos[:], ALU.mult))
                nc.vector.tensor_tensor(x, x, turned[r % 2][:], ALU.add).then_inc(rotated, 1)

            for n in range(1, 24, 2):
                dve.wait_ge(tile_ready, n + 1)
                out = heads_T[:, n, :] if n < 16 else values[:, (n - 16) // 4, n % 4, :]
                scale = A_DIM ** -0.5 if n // 4 in (0, 2) else 1.0
                nc.vector.tensor_scalar(out, banks[n % 4][:], scale, None, ALU.mult).then_inc(copied_dve, 1)
                if 4 <= n < 12:
                    if n == 5:
                        dve.wait_ge(rot_loaded, 48)
                    rotate(n - 5)
                    rotate(n - 4)
    clear_semaphores(nc, sems)


def attention_heads(nc, m, heads_T, values, mixed):
    units = [(t, group, f) for t in range(NT) for group in range(2) for f in range(4)]
    N = len(units)
    with ExitStack() as ctx:
        def sb(name, shape, dt=F32):
            return ctx.enter_context(nc.sbuf_tensor(name, shape, dt))

        sems = []

        def sem(name):
            sems.append(ctx.enter_context(nc.semaphore(name)))
            return sems[-1]

        def bank(name):
            return ctx.enter_context(nc.psum_tensor(name, [P, 512], F32))

        bias = sb("rel_bias", [P, B_HEADS, SEQ])
        mask_q, mask_k = sb("mask_q", [1, P]), sb("mask_k", [1, P])
        lambda_in, lambda_prod = sb("lambda_in", [P, 4, A_DIM]), sb("lambda_prod", [P, 2, A_DIM])
        lambda_sum, lambda_exp, neg_lambda = sb("lambda_sum", [P, 2]), sb("lambda_exp", [P, 2]), sb("neg_lambda", [P, 1])
        subln_gain, subln_eps = sb("subln_gain", [P, 2 * A_DIM]), sb("subln_eps", [P, 1])
        probs = [sb(f"probs{i}", [P, 2, SEQ]) for i in range(3)]
        probs_T = [sb(f"probs_T{i}", [P, 2, SEQ]) for i in range(2)]
        neg_max = sb("neg_max", [P, N, 2])
        total = sb("total", [P, N, 2])
        inverse = sb("inverse", [P, N, 2])
        ratio = sb("ratio", [P, N])
        squares, square_sum = sb("squares", [P, P]), sb("square_sum", [P, NT * A_HEADS])
        psum_s = [[bank(f"psum_s{i}{c}") for c in range(2)] for i in range(2)]
        psum_t = [bank(f"psum_t{c}") for c in range(2)]
        psum_o = [bank(f"psum_o{i}") for i in range(2)]
        small_loaded, bias_loaded, bias_masked = sem("small_loaded"), sem("bias_loaded"), sem("bias_masked")
        scores_ready, max_ready, probs_ready, mixed_ready = sem("at_scores"), sem("at_max"), sem("at_probs"), sem("at_combined")
        turned_ready, probs_T_act, probs_T_dve = sem("at_turned"), sem("at_copied_act"), sem("at_copied_dve")
        out_ready, out_copied, dve_steps, lambda_ready = sem("at_out"), sem("at_out_copied"), sem("at_dve_steps"), sem("at_lambda")
        square_ready, root_ready = sem("at_squares"), sem("at_root")
        block = ctx.enter_context(nc.Block())

        @block.sync
        def _(sp):
            for tile_, name in ((mask_q, "mask_q"), (mask_k, "mask_k")):
                sp.dma_start(tile_[:], m.a[name]).then_inc(small_loaded, 16)
            sp.dma_start(lambda_in[:], m.a["even_lambda"][0].partition_broadcast(P)).then_inc(small_loaded, 16)
            sp.dma_start(subln_gain[:], m.a["even_subln_g"][0].partition_broadcast(P)).then_inc(small_loaded, 16)
            sp.dma_start(bias[:], m.a["rel_bias_rows"]).then_inc(bias_loaded, 16)
            sp.dma_start(m.w_out[:], m.a["even_w_out"][0].rearrange("(k p) n -> p k n", p=P)).then_inc(m.w_out_loaded, 16)

        @block.gpsimd
        def _(pool):
            pool.memset(subln_eps[:], SUBLN_EPS)
            pool.wait_ge(bias_loaded, 16)
            nc.gpsimd.tensor_scalar(bias[0:CHUNK, :, SEQ - CHUNK:SEQ], bias[0:CHUNK, :, SEQ - CHUNK:SEQ], NEG_INF, None, ALU.add).then_inc(bias_masked, 1)

        @block.tensor
        def _(pe):
            def scores(n):
                t, group, f = units[n]
                keys = P * (t + 1)
                if n >= 2:
                    pe.wait_ge(probs_ready, 2 * (n - 1))
                for c in range(2):
                    rows = slice(64 * c, 64 * c + 64)
                    out = psum_s[n % 2][c]
                    nc.tensor.matmul(out[:, 0:keys], heads_T[rows, 8 * group + f, t * P:(t + 1) * P],
                                     heads_T[rows, 8 * group + 4 + f, 0:keys], start=True, stop=False)
                    if group == 0:
                        mm = nc.tensor.matmul(out[:, keys - P:keys], mask_q[:], mask_k[:], start=False, stop=True)
                    else:
                        if n == 4:
                            pe.wait_ge(bias_masked, 1)
                        mm = nc.tensor.matmul(out[:, 0:keys], m.ident[:], bias[:, 2 * f + c, SEQ - keys:SEQ], start=False, stop=True)
                    mm.then_inc(scores_ready, 1)

            def turn(n):
                t, group, f = units[n]
                if n >= 1:
                    pe.wait_ge(probs_T_act, n)
                    pe.wait_ge(probs_T_dve, n)
                pe.wait_ge(probs_ready, 2 * n + 2)
                pe.wait_ge(mixed_ready, n + 1)
                for c in range(1 + group):
                    for j in range(t + 1):
                        tr = nc.tensor.transpose(psum_t[c][:, j * P:(j + 1) * P], probs[n % 3][:, c, j * P:(j + 1) * P], m.ident[:])
                tr.then_inc(turned_ready, 1)

            def apply(n):
                t, group, f = units[n]
                pe.wait_ge(probs_T_act, n + 1)
                pe.wait_ge(probs_T_dve, n + 1)
                if n >= 2:
                    pe.wait_ge(out_copied, n - 1)
                width = P // (1 + group)
                for c in range(1 + group):
                    for j in range(t + 1):
                        mm = nc.tensor.matmul(psum_o[n % 2][:, c * width:(c + 1) * width], probs_T[n % 2][:, c, j * P:(j + 1) * P],
                                              values[:, group, j, f * P + c * width:f * P + (c + 1) * width], start=(j == 0), stop=(j == t))
                mm.then_inc(out_ready, 1)

            pe.wait_ge(small_loaded, 64)
            for step in range(N + 3):
                if step < N:
                    scores(step)
                if 2 <= step < N + 2:
                    turn(step - 2)
                if step >= 3:
                    apply(step - 3)

        @block.scalar
        def _(act):
            act.wait_ge(lambda_ready, 1)
            nc.scalar.activation(lambda_exp[:], lambda_sum[:], ACT.Exp).then_inc(lambda_ready, 1)

            def exps(n):
                keys = P * (units[n][0] + 1)
                if n >= 3:
                    act.wait_ge(turned_ready, n - 2)
                for c in range(2):
                    act.wait_ge(max_ready, 2 * n + c + 1)
                    nc.scalar.activation(probs[n % 3][:, c, 0:keys], psum_s[n % 2][c][:, 0:keys], ACT.Exp, bias=neg_max[:, n, c:c + 1],
                                         accum_out=total[:, n, c:c + 1]).then_inc(probs_ready, 1)

            def copy_turned(n):
                t, group, f = units[n]
                act.wait_ge(turned_ready, n + 1)
                if n >= 2:
                    act.wait_ge(out_ready, n - 1)
                if group:
                    nc.scalar.copy(probs_T[n % 2][:, 1, 0:(t + 1) * P], psum_t[1][:, 0:(t + 1) * P]).then_inc(probs_T_act, 1)
                else:
                    act.sem_inc(probs_T_act, 1)

            for step in range(N + 2):
                if step < N:
                    exps(step)
                if step >= 2:
                    copy_turned(step - 2)
            act.wait_ge(square_ready, 1)
            nc.scalar.activation(square_sum[:], square_sum[:], ACT.Sqrt, bias=subln_eps[:], scale=1.0 / (2 * A_DIM)).then_inc(root_ready, 1)

        @block.vector
        def _(dve):
            c_ = Chain(dve, dve_steps)
            dve.wait_ge(small_loaded, 64)
            c_.link(nc.vector.tensor_tensor(lambda_prod[:], lambda_in[:].rearrange("p (a b) d -> p a b d", b=2)[:, :, 0, :],
                                            lambda_in[:].rearrange("p (a b) d -> p a b d", b=2)[:, :, 1, :], ALU.mult))
            nc.vector.tensor_reduce(lambda_sum[:], lambda_prod[:], AX.X, ALU.add).then_inc(lambda_ready, 1)
            dve.wait_ge(lambda_ready, 2)
            c_.link(nc.vector.tensor_tensor(neg_lambda[:], lambda_exp[:, 1:2], lambda_exp[:, 0:1], ALU.subtract))
            c_.link(nc.vector.tensor_scalar(neg_lambda[:], neg_lambda[:], -LAMBDA_INIT, None, ALU.add))
            c_.link(nc.vector.tensor_scalar(subln_gain[:], subln_gain[:], 1.0 - LAMBDA_INIT, None, ALU.mult))

            def maxima(n):
                keys = P * (units[n][0] + 1)
                for c in range(2):
                    dve.wait_ge(scores_ready, 2 * n + c + 1)
                    nc.vector.tensor_reduce(neg_max[:, n, c:c + 1], psum_s[n % 2][c][:, 0:keys], AX.X, ALU.max, negate=True).then_inc(max_ready, 1)

            def combine(n):
                t, group, f = units[n]
                keys = P * (t + 1)
                dve.wait_ge(probs_ready, 2 * n + 2)
                if group:
                    nc.vector.reciprocal(inverse[:, n, :], total[:, n, :]).then_inc(mixed_ready, 1)
                    return
                c_.link(nc.vector.reciprocal(inverse[:, n, :], total[:, n, :]))
                c_.link(nc.vector.scalar_tensor_tensor(out=ratio[:, n:n + 1], in0=total[:, n, 0:1], scalar=neg_lambda[:], in1=inverse[:, n, 1:2],
                                                       op0=ALU.mult, op1=ALU.mult))
                p = probs[n % 3]
                nc.vector.scalar_tensor_tensor(out=p[:, 0, 0:keys], in0=p[:, 1, 0:keys], scalar=ratio[:, n:n + 1], in1=p[:, 0, 0:keys],
                                               op0=ALU.mult, op1=ALU.add).then_inc(mixed_ready, 1)

            def copy_turned(n):
                t, group, f = units[n]
                dve.wait_ge(turned_ready, n + 1)
                if n >= 2:
                    dve.wait_ge(out_ready, n - 1)
                nc.vector.tensor_copy(probs_T[n % 2][:, 0, 0:(t + 1) * P], psum_t[0][:, 0:(t + 1) * P]).then_inc(probs_T_dve, 1)

            def copy_out(n):
                t, group, f = units[n]
                dve.wait_ge(out_ready, n + 1)
                out = mixed[:, t, group * 512 + f * P:group * 512 + (f + 1) * P]
                if group:
                    for c in range(2):
                        mv = nc.vector.tensor_scalar(out[:, c * 64:(c + 1) * 64], psum_o[n % 2][:, c * 64:(c + 1) * 64], inverse[:, n, c:c + 1], None, ALU.mult)
                        if c == 0:
                            c_.mark(mv)
                    mv.then_inc(out_copied, 1)
                    return
                c_.link(nc.vector.tensor_scalar(out, psum_o[n % 2][:, 0:P], inverse[:, n, 0:1], None, ALU.mult))
                nc.vector.scalar_tensor_tensor(out=squares[:], in0=out, scalar=1.0, in1=out, op0=ALU.mult, op1=ALU.mult,
                                               accum_out=square_sum[:, t * A_HEADS + f:t * A_HEADS + f + 1]).then_inc(out_copied, 1)

            for step in range(N + 3):
                if step < N:
                    maxima(step)
                if 1 <= step < N + 1:
                    combine(step - 1)
                if 2 <= step < N + 2:
                    copy_turned(step - 2)
                if step >= 3:
                    copy_out(step - 3)
            dve.wait_ge(out_copied, N)
            dve.sem_inc(square_ready, 1)
            dve.wait_ge(root_ready, 1)
            c_.link(nc.vector.reciprocal(square_sum[:], square_sum[:]))
            for t in range(NT):
                for f in range(A_HEADS):
                    o = mixed[:, t, f * P:(f + 1) * P]
                    c_.mark(nc.vector.scalar_tensor_tensor(out=o, in0=o, scalar=square_sum[:, t * A_HEADS + f:t * A_HEADS + f + 1], in1=subln_gain[:],
                                                           op0=ALU.mult, op1=ALU.mult))
    clear_semaphores(nc, sems)


def mixer_output(nc, m, layer, mixed_T, sources, residual):
    with ExitStack() as ctx:
        sems = []

        def sem(name):
            sems.append(ctx.enter_context(nc.semaphore(f"{name}_w{layer}")))
            return sems[-1]

        pre = ctx.enter_context(nc.sbuf_tensor(f"pre_w{layer}", [P, 2, D_MODEL], F32))
        banks = [ctx.enter_context(nc.psum_tensor(f"psum_turn{i}_w{layer}", [P, 512], F32)) for i in range(4)]
        out_banks = [ctx.enter_context(nc.psum_tensor(f"psum_out{i}_w{layer}", [P, 512], F32)) for i in range(4)]
        transposed, copied_act, copied_dve, product_ready = sem("turned"), sem("copied_act"), sem("copied_dve"), sem("product")
        norm_loaded, added, dve_steps, var_ready, root_ready = sem("norm_loaded"), sem("added"), sem("dve_steps"), sem("var"), sem("root")
        block = ctx.enter_context(nc.Block())

        @block.sync
        def _(sp):
            sp.dma_start(m.ln_gain, m.a["ln_g"][layer, 0].partition_broadcast(P)).then_inc(norm_loaded, 16)
            sp.dma_start(m.ln_bias, m.a["ln_b"][layer, 0].partition_broadcast(P)).then_inc(norm_loaded, 16)
            x = m.a["x"][0] if layer == 0 else m.x_dram
            sp.dma_start(residual[:], x.rearrange("(t p) d -> p t d", p=P)).then_inc(norm_loaded, 16)
            if sources is None:
                load_expert(nc, sp, m, layer, 0, m.first_weights)

        @block.tensor
        def _(pe):
            def turn(t):
                for half in range(2):
                    n = 2 * t + half
                    if n >= 4:
                        pe.wait_ge(copied_dve if half else copied_act, t - 1)
                    for q in range(4):
                        k = 4 * half + q
                        tr = nc.tensor.transpose(banks[n % 4][:, q * P:(q + 1) * P], sources[:, t, k * P:(k + 1) * P], m.ident[:])
                    tr.then_inc(transposed, 1)

            pe.wait_ge(m.w_out_loaded, 16 * (layer + 1))
            if sources is not None:
                turn(0)
            for t in range(NT):
                if sources is not None:
                    if t + 1 < NT:
                        turn(t + 1)
                    pe.wait_ge(copied_act, t + 1)
                    pe.wait_ge(copied_dve, t + 1)
                if t >= 2:
                    pe.wait_ge(added, 2 * (t - 1))
                for half in range(2):
                    for k in range(KD):
                        mm = nc.tensor.matmul(out_banks[2 * (t % 2) + half][:], mixed_T[:, k, t * P:(t + 1) * P], m.w_out[:, k, half * 512:(half + 1) * 512],
                                              start=(k == 0), stop=(k == KD - 1))
                    mm.then_inc(product_ready, 1)

        @block.scalar
        def _(act):
            def copy(t):
                act.wait_ge(transposed, 2 * t + 1)
                nc.scalar.copy(mixed_T[:, 0:4, t * P:(t + 1) * P], banks[2 * t % 4][:].rearrange("p (q n) -> p q n", q=4)).then_inc(copied_act, 1)
            if sources is not None:
                copy(0)
            for t in range(NT):
                if sources is not None and t + 1 < NT:
                    copy(t + 1)
                act.wait_ge(var_ready, t + 1)
                nc.scalar.activation(m.moments[:, t, 2:3], m.moments[:, t, 1:2], ACT.Sqrt, bias=m.ln_eps[:]).then_inc(root_ready, 1)

        @block.vector
        def _(dve):
            c = Chain(dve, dve_steps)

            def copy(t):
                dve.wait_ge(transposed, 2 * t + 2)
                nc.vector.tensor_copy(mixed_T[:, 4:8, t * P:(t + 1) * P], banks[(2 * t + 1) % 4][:].rearrange("p (q n) -> p q n", q=4)).then_inc(copied_dve, 1)

            def add(t):
                for half in range(2):
                    dve.wait_ge(product_ready, 2 * t + half + 1)
                    cols = slice(half * 512, (half + 1) * 512)
                    nc.vector.scalar_tensor_tensor(out=pre[:, t % 2, cols], in0=residual[:, t, cols], scalar=ALPHA, in1=out_banks[2 * (t % 2) + half][:],
                                                   op0=ALU.mult, op1=ALU.add).then_inc(added, 1)
                dve.wait_ge(added, 2 * t + 2)
                norm_moments(nc, c, pre[:, t % 2, :], m.stats, m.moments[:, t, :], var_ready)

            if sources is not None:
                copy(0)
                copy(1)
            dve.wait_ge(norm_loaded, 48)
            add(0)
            for t in range(NT):
                if sources is not None and t + 2 < NT:
                    copy(t + 2)
                if t + 1 < NT:
                    add(t + 1)
                dve.wait_ge(root_ready, t + 1)
                c.link(norm_apply(nc, c, pre[:, t % 2, :], m.moments[:, t, :], m.ln_gain, m.ln_bias, m.stream[:, t, :]))
    clear_semaphores(nc, sems)


def rwkv_project(nc, m, r_T, k_T, value, logit, a_T, g_T, x_T, dx_T, mixes, weights):
    with ExitStack() as ctx:
        sems = []

        def sem(name):
            sems.append(ctx.enter_context(nc.semaphore(name)))
            return sems[-1]

        banks = [ctx.enter_context(nc.psum_tensor(f"psum_rp{i}", [P, 512], F32)) for i in range(4)]
        turn_banks = [ctx.enter_context(nc.psum_tensor(f"psum_rt{i}", [P, 512], F32)) for i in range(4)]
        x_saved, params_loaded, w_loaded = sem("x_saved"), sem("params_loaded"), [sem("rw_loaded0"), sem("rw_loaded1")]
        turned, copied_act, copied_dve, mixed, steps = sem("rx_turned"), sem("rx_copied_act"), sem("rx_copied_dve"), sem("mixed"), sem("rp_steps")
        unit_done, unit_copied, v_stored, ones_set = sem("rp_unit"), sem("rp_copied"), sem("v_stored"), sem("ones_set")
        tanh_w, inner_a = m.ln_gain[:, 0:512], m.ln_gain[:, 512:1024]
        inner_g = [m.ln_bias[:, 0:512], m.ln_bias[0:LORA_G - P, 512:1024]]
        low_in = weights[0]
        low_out = weights[1][:].rearrange("p (a b) n -> p a (b n)", b=2)
        streams = [("r", 0), ("k", 2), ("v", 3), ("w", 1), ("a", 4), ("g", 5)]
        units = [("r", f) for f in range(KD)] + [("k", f) for f in range(KD)] + [("v", n) for n in range(2 * NT)]
        units += [("w in", 0), ("a in", 0), ("g in", 0), ("g in", 1)]
        units += [("w", n) for n in range(2 * NT)] + [("a", f) for f in range(KD)] + [("g", f) for f in range(KD)]
        at = {u: n for n, u in enumerate(units)}
        last_use = [at["r", 7], at["k", 7], at["v", 7], at["w in", 0], at["a in", 0], at["g in", 1]]
        block = ctx.enter_context(nc.Block())

        @block.sync
        def _(sp):
            sp.dma_start(m.params[:], m.a["params"]).then_inc(params_loaded, 16)
            sp.dma_start(m.x_dram.rearrange("(t p) d -> p t d", p=P), m.stream[:]).then_inc(x_saved, 16)
            for n in range(6):
                s, half = n // 2, n % 2
                if n >= 2:
                    sp.wait_ge(unit_done, 8 * (s - 1) + (4 * half + 4 if s < 3 else 0))
                w = m.a["odd_w_rkv"][0, s].rearrange("(k p) n -> p k n", p=P)
                sp.dma_start(weights[half][:], w[:, :, half * 512:(half + 1) * 512]).then_inc(w_loaded[half], 16)
            sp.wait_ge(unit_done, at["v", 7] + 1)
            for name, col in (("odd_w1", 0), ("odd_a1", LORA_W), ("odd_g1", LORA_W + LORA_A)):
                w = m.a[name][0].rearrange("(k p) n -> p k n", p=P)
                sp.dma_start(low_in[:, :, col:col + w.shape[2]], w).then_inc(w_loaded[0], 16)
            sp.dma_start(low_out[0:LORA_W, 0, :], m.a["odd_w2"][0]).then_inc(w_loaded[1], 16)
            sp.dma_start(low_out[LORA_W:LORA_W + 1, 0, :], m.a["odd_w0"]).then_inc(w_loaded[1], 16)
            sp.dma_start(low_out[0:LORA_A, 1, :], m.a["odd_a2"][0]).then_inc(w_loaded[1], 16)
            sp.dma_start(low_out[:, 2, :], m.a["odd_g2"][0, 0:P]).then_inc(w_loaded[1], 16)
            sp.dma_start(low_out[0:LORA_G - P, 3, :], m.a["odd_g2"][0, P:LORA_G]).then_inc(w_loaded[1], 16)
            sp.wait_ge(unit_copied, at["v", 7] + 1)
            sp.dma_start(m.v_dram.rearrange("(t p) d -> p t d", p=P), value[:]).then_inc(v_stored, 16)
            sp.wait_ge(v_stored, 16)

        @block.gpsimd
        def _(pool):
            pool.memset(tanh_w[LORA_W:LORA_W + 1, :], 1.0).then_inc(ones_set, 1)

        @block.tensor
        def _(pe):
            for n in range(2 * NT):
                t, half = n // 2, n % 2
                if n >= 4:
                    pe.wait_ge(copied_dve if half else copied_act, t - 1)
                for q in range(4):
                    k = 4 * half + q
                    tr = nc.tensor.transpose(turn_banks[n % 4][:, q * P:(q + 1) * P], m.stream[:, t, k * P:(k + 1) * P], m.ident[:])
                tr.then_inc(turned, 1)
            for n, (name, i) in enumerate(units):
                if n >= 4:
                    pe.wait_ge(unit_copied, n - 3)
                stream = name[0]
                s = "rkvwag".index(stream)
                x = mixes[s % 2]
                if i == 0 and (len(name) > 1 or s < 3):
                    pe.wait_ge(mixed, KD * (s + 1))
                if s < 3:
                    half = i % 2 if stream == "v" else i // 4
                    if i == (0 if half == 0 else (1 if stream == "v" else 4)):
                        pe.wait_ge(w_loaded[half], 16 * (s + 1))
                    w = weights[half]
                    for k in range(KD):
                        if stream == "v":
                            left, right = x[:, k, (i // 2) * P:(i // 2 + 1) * P], w[:, k, :]
                        else:
                            left, right = w[:, k, (i % 4) * P:(i % 4 + 1) * P], x[:, k, :]
                        mm = nc.tensor.matmul(banks[n % 4][:], left, right, start=(k == 0), stop=(k == KD - 1))
                elif len(name) > 1:
                    if name == "w in":
                        pe.wait_ge(w_loaded[0], 16 * 6)
                    first = {"w in": 0, "a in": LORA_W, "g in": LORA_W + LORA_A + i * P}[name]
                    width = {"w in": LORA_W, "a in": LORA_A, "g in": (P, LORA_G - P)[i]}[name]
                    for k in range(KD):
                        mm = nc.tensor.matmul(banks[n % 4][0:width, :], low_in[:, k, first:first + width], x[:, k, :], start=(k == 0), stop=(k == KD - 1))
                elif stream == "w":
                    if i == 0:
                        pe.wait_ge(w_loaded[1], 16 * 8)
                        pe.wait_ge(ones_set, 1)
                        pe.wait_ge(unit_copied, at["w in", 0] + 1)
                    t, half = i // 2, i % 2
                    mm = nc.tensor.matmul(banks[n % 4][:], tanh_w[0:LORA_W + 1, t * P:(t + 1) * P], low_out[0:LORA_W + 1, 0, half * 512:(half + 1) * 512],
                                          start=True, stop=True)
                elif stream == "a":
                    mm = nc.tensor.matmul(banks[n % 4][:], low_out[0:LORA_A, 1, i * P:(i + 1) * P], inner_a[0:LORA_A, :], start=True, stop=True)
                else:
                    nc.tensor.matmul(banks[n % 4][:], low_out[:, 2, i * P:(i + 1) * P], inner_g[0], start=True, stop=False)
                    mm = nc.tensor.matmul(banks[n % 4][:], low_out[0:LORA_G - P, 3, i * P:(i + 1) * P], inner_g[1], start=False, stop=True)
                mm.then_inc(unit_done, 1)

        @block.scalar
        def _(act):
            for t in range(NT):
                act.wait_ge(turned, 2 * t + 1)
                nc.scalar.copy(x_T[:, 0:4, t * P:(t + 1) * P], turn_banks[2 * t % 4][:].rearrange("p (q n) -> p q n", q=4)).then_inc(copied_act, 1)
            act.wait_ge(params_loaded, 16)
            for n, (name, i) in enumerate(units):
                act.wait_ge(unit_done, n + 1)
                src = banks[n % 4]
                if name in ("r", "k"):
                    e = nc.scalar.copy((r_T if name == "r" else k_T)[:, i, :], src[:])
                elif name == "v":
                    e = nc.scalar.copy(value[:, i // 2, (i % 2) * 512:(i % 2 + 1) * 512], src[:])
                elif name == "w in":
                    e = nc.scalar.activation(tanh_w[0:LORA_W, :], src[0:LORA_W, :], ACT.Tanh)
                elif name == "a in":
                    e = nc.scalar.copy(inner_a[0:LORA_A, :], src[0:LORA_A, :])
                elif name == "g in":
                    e = nc.scalar.activation(inner_g[i], src[0:inner_g[i].shape[0], :], ACT.Sigmoid)
                elif name == "w":
                    e = nc.scalar.activation(logit[:, i // 2, (i % 2) * 512:(i % 2 + 1) * 512], src[:], ACT.Sigmoid)
                elif name == "a":
                    e = nc.scalar.activation(a_T[:, i, :], src[:], ACT.Sigmoid, bias=m.params[:, PARAM["a0"], i:i + 1])
                else:
                    e = nc.scalar.copy(g_T[:, i, :], src[:])
                e.then_inc(unit_copied, 1)

        @block.vector
        def _(dve):
            c = Chain(dve, steps)
            for t in range(NT):
                dve.wait_ge(turned, 2 * t + 2)
                nc.vector.tensor_copy(x_T[:, 4:8, t * P:(t + 1) * P], turn_banks[(2 * t + 1) % 4][:].rearrange("p (q n) -> p q n", q=4)).then_inc(copied_dve, 1)
            dve.wait_ge(x_saved, 16)
            dve.wait_ge(copied_act, NT)
            dve.wait_ge(copied_dve, NT)
            c.mark(nc.vector.tensor_scalar(dx_T[:, :, 0:1], x_T[:, :, 0:1], -1.0, None, ALU.mult))
            c.link(nc.vector.tensor_tensor(dx_T[:, :, 1:SEQ], x_T[:, :, 0:SEQ - 1], x_T[:, :, 1:SEQ], ALU.subtract))
            dve.wait_ge(params_loaded, 16)
            for s, (name, row) in enumerate(streams):
                if s >= 2:
                    dve.wait_ge(unit_done, last_use[s - 2] + 1)
                for k in range(KD):
                    nc.vector.scalar_tensor_tensor(out=mixes[s % 2][:, k, :], in0=dx_T[:, k, :], scalar=m.params[:, PARAM["mix"] + row, k:k + 1],
                                                   in1=x_T[:, k, :], op0=ALU.mult, op1=ALU.add).then_inc(mixed, 1)
    clear_semaphores(nc, sems)


def rwkv_prepare(nc, m, r_T, k_T, value, logit, a_T, decay_T, kk_T, bonus_T):
    with ExitStack() as ctx:
        sems = []

        def sem(name):
            sems.append(ctx.enter_context(nc.semaphore(name)))
            return sems[-1]

        def sb(name, shape):
            return ctx.enter_context(nc.sbuf_tensor(name, shape, F32))

        def banks(name):
            return [ctx.enter_context(nc.psum_tensor(f"{name}{i}", [P, SEQ], F32)) for i in range(2)]

        square, norm, product, v_T = sb("kk_square", [P, 2, SEQ]), sb("kk_norm", [P, 2, SEQ]), sb("rk_product", [P, 2, SEQ]), sb("v_T", [P, 2, SEQ])
        one_less = sb("one_less_k_a", [P, KD])
        sum_decay, pair_ones = sb("sum_decay", [P, P]), sb("pair_ones", [P, P])
        psum_decay, psum_norm, psum_bonus, psum_v = banks("psum_decay"), banks("psum_norm"), banks("psum_bonus"), banks("psum_v")
        consts, steps = sem("pr_consts"), sem("pr_steps")
        kk_ready, square_ready, norm_summed, norm_ready, kk_done = sem("kk_ready"), sem("kk_square_ready"), sem("norm_summed"), sem("norm_ready"), sem("kk_done")
        decay_summed, decay_copied, product_ready, bonus_summed = sem("decay_summed"), sem("decay_copied"), sem("product_ready"), sem("bonus_summed")
        v_turned, v_copied, bonus_ready = sem("v_turned"), sem("v_copied"), sem("bonus_ready")
        block = ctx.enter_context(nc.Block())

        @block.sync
        def _(sp):
            sp.dma_start(sum_decay[:], m.a["sum_decay"]).then_inc(consts, 16)
            sp.dma_start(pair_ones[:], m.a["pair_ones"]).then_inc(consts, 16)

        @block.tensor
        def _(pe):
            pe.wait_ge(consts, 32)
            for f in range(KD):
                b = f % 2
                if f >= 2:
                    pe.wait_ge(decay_copied, f - 1)
                    pe.wait_ge(v_copied, f - 1)
                for t in range(NT):
                    mm = nc.tensor.matmul(psum_decay[b][:, t * P:(t + 1) * P], logit[:, t, f * P:(f + 1) * P], sum_decay[:], start=True, stop=True)
                mm.then_inc(decay_summed, 1)
                for t in range(NT):
                    tr = nc.tensor.transpose(psum_v[b][:, t * P:(t + 1) * P], value[:, t, f * P:(f + 1) * P], m.ident[:])
                tr.then_inc(v_turned, 1)
                pe.wait_ge(square_ready, f + 1)
                if f >= 2:
                    pe.wait_ge(norm_ready, f - 1)
                nc.tensor.matmul(psum_norm[b][:], pair_ones[:], square[:, b, :], start=True, stop=True).then_inc(norm_summed, 1)
                pe.wait_ge(product_ready, f + 1)
                if f >= 2:
                    pe.wait_ge(bonus_ready, f - 1)
                nc.tensor.matmul(psum_bonus[b][:], pair_ones[:], product[:, b, :], start=True, stop=True).then_inc(bonus_summed, 1)

        @block.scalar
        def _(act):
            def first(f):
                b = f % 2
                act.wait_ge(kk_ready, f + 1)
                if f >= 2:
                    act.wait_ge(norm_summed, f - 1)
                nc.scalar.activation(square[:, b, :], kk_T[:, f, :], ACT.Square).then_inc(square_ready, 1)
            first(0)
            for f in range(KD):
                b = f % 2
                if f + 1 < KD:
                    first(f + 1)
                act.wait_ge(decay_summed, f + 1)
                nc.scalar.copy(decay_T[:, f, :], psum_decay[b][:]).then_inc(decay_copied, 1)
                act.wait_ge(v_turned, f + 1)
                if f >= 2:
                    act.wait_ge(bonus_ready, f - 1)
                nc.scalar.copy(v_T[:, b, :], psum_v[b][:]).then_inc(v_copied, 1)
                act.wait_ge(norm_summed, f + 1)
                if f >= 2:
                    act.wait_ge(kk_done, f - 1)
                nc.scalar.activation(norm[:, b, :], psum_norm[b][:], ACT.Sqrt).then_inc(norm_ready, 1)

        @block.vector
        def _(dve):
            c = Chain(dve, steps)
            par = m.params
            c.link(nc.vector.tensor_scalar(one_less[:], par[:, PARAM["k_a"], :], -1.0, 1.0, ALU.mult, ALU.add))

            def keys(f):
                b = f % 2
                nc.vector.tensor_scalar(kk_T[:, f, :], k_T[:, f, :], par[:, PARAM["k_k"], f:f + 1], None, ALU.mult).then_inc(kk_ready, 1)
                if f >= 2:
                    dve.wait_ge(bonus_summed, f - 1)
                c.link(nc.vector.tensor_scalar(product[:, b, :], a_T[:, f, :], par[:, PARAM["k_a"], f:f + 1], one_less[:, f:f + 1], ALU.mult, ALU.add))
                dve.wait_ge(kk_ready, f + 1)
                c.link(nc.vector.tensor_tensor(k_T[:, f, :], k_T[:, f, :], product[:, b, :], ALU.mult))
                nc.vector.scalar_tensor_tensor(out=product[:, b, :], in0=r_T[:, f, :], scalar=par[:, PARAM["r_k"], f:f + 1], in1=k_T[:, f, :],
                                               op0=ALU.mult, op1=ALU.mult).then_inc(product_ready, 1)

            keys(0)
            for f in range(KD):
                b = f % 2
                if f + 1 < KD:
                    keys(f + 1)
                dve.wait_ge(norm_ready, f + 1)
                c.link(nc.vector.tensor_scalar(norm[:, b, :], norm[:, b, :], 1e-12, None, ALU.max))
                c.link(nc.vector.reciprocal(norm[:, b, :], norm[:, b, :]))
                dve.wait_ge(square_ready, f + 1)
                nc.vector.tensor_tensor(kk_T[:, f, :], kk_T[:, f, :], norm[:, b, :], ALU.mult).then_inc(kk_done, 1)
                dve.wait_ge(kk_done, f + 1)
                c.mark(nc.vector.tensor_tensor(a_T[:, f, :], a_T[:, f, :], kk_T[:, f, :], ALU.mult))
                dve.wait_ge(bonus_summed, f + 1)
                dve.wait_ge(v_copied, f + 1)
                nc.vector.tensor_tensor(bonus_T[:, f, :], psum_bonus[b][:], v_T[:, b, :], ALU.mult).then_inc(bonus_ready, 1)
    clear_semaphores(nc, sems)


def rwkv_scan(nc, m, r_T, k_T, kka_T, decay_T, kk_T, y_T):
    with ExitStack() as ctx:
        sems = []

        def sem(name):
            sems.append(ctx.enter_context(nc.semaphore(name)))
            return sems[-1]

        def sb(name, shape=(P, PAIRS, CHUNK)):
            return ctx.enter_context(nc.sbuf_tensor(f"{name}_scan", list(shape), F32))

        def two(name):
            return [sb(f"{name}{i}") for i in range(2)]

        def bank(name):
            return ctx.enter_context(nc.psum_tensor(f"{name}_scan", [P, PAIRS, CHUNK], F32))

        masks = sb("masks", (P, N_MASKS, CHUNK))
        growth, decline = sb("growth"), sb("decline", (P, PAIRS, CHUNK + 1))
        end_decay = sb("end_decay", (P, 2, PAIRS))
        A, B, K, R, V = two("A"), two("B"), two("K"), two("R"), two("V")
        AK, RB, RK = two("AK"), two("RB"), two("RK")
        B_rows, K_rows = two("B_rows"), two("K_rows")
        L, L_level, X, T, Z = sb("L"), two("L_level"), two("X"), sb("T"), sb("Z")
        W, U, S = sb("W"), sb("U"), sb("S")
        bank_W, bank_U, bank_Y, bank_S = bank("bW"), bank("bU"), bank("bY"), bank("bS")
        bank_Z, bank_X, bank_T, bank_K = bank("bZ"), bank("bX"), bank("bT"), bank("bK")

        masks_loaded, v_loaded, state_zero, edge_set = sem("masks_loaded"), [sem("v_loaded0"), sem("v_loaded1")], sem("state_zero"), sem("edge_set")
        exps_ready, a_made, b_made, kr_made, end_copied = sem("exps"), sem("a_made"), sem("b_made"), sem("kr_made"), sem("end_copied")
        l_ready, inter_ready, ak_used, rk_used, rb_used = sem("l_ready"), sem("inter_ready"), sem("ak_used"), sem("rk_used"), sem("rb_used")
        nt_used, l_copied, l_level_ready = sem("nt_used"), sem("l_copied"), sem("l_level_ready")
        rows_ready, k_rows_copied, b_rows_copied = sem("rows_ready"), sem("k_rows_copied"), sem("b_rows_copied")
        z_ready, z_copied, xt_ready, x_added, t_added = sem("z_ready"), sem("z_copied"), sem("xt_ready"), sem("x_added"), sem("t_added")
        w_ready, w_copied, u_ready, u_copied = sem("w_ready"), sem("w_copied"), sem("u_ready"), sem("u_copied")
        y_ready, y_copied, s_ready, s_updated = sem("y_ready"), sem("y_copied"), sem("s_ready"), sem("s_updated")
        t_begun, s_added, products_begun = sem("t_begun"), sem("s_added"), sem("products_begun")
        block = ctx.enter_context(nc.Block())

        def mask(i):
            return masks[:, i, :].unsqueeze(1).to_broadcast([P, PAIRS, CHUNK])

        def run(engine, first, body):
            first()
            for i in range(2):
                body(i, i, True, 0)
            with engine.Fori(1, N_CHUNKS // 2 - 1) as turn:
                for i in range(2):
                    body(turn * 2 + i, i, True, turn)
            for i in range(2):
                body(N_CHUNKS - 2 + i, i, i == 0, N_CHUNKS // 2 - 1)

        def chunk(x, n):
            return x[:, :, bass.ds(n * CHUNK, CHUNK)]

        @block.sync
        def _(sp):
            v_rows = m.v_dram.rearrange("(c s) (q h v) -> c h s q v", s=CHUNK, h=2, v=CHUNK)

            def load_v(n, i):
                for h in range(2):
                    sp.dma_start(V[i][h * CHUNK:(h + 1) * CHUNK, :, :], v_rows[n, h]).then_inc(v_loaded[i], 16)

            def first():
                sp.dma_start(masks[:], m.a["scan_masks"]).then_inc(masks_loaded, 16)
                load_v(0, 0)

            def body(n, i, ahead, turn):
                if ahead:
                    sp.wait_ge(y_ready, n)
                    sp.wait_ge(s_ready, n)
                    load_v(n + 1, 1 - i)
            run(sp, first, body)

        @block.gpsimd
        def _(pool):
            pool.memset(decline[:, :, 0:1], 1.0).then_inc(edge_set, 1)
            pool.memset(S[:], 0.0).then_inc(state_zero, 1)

            def make_kr(n, i):
                pool.wait_ge(exps_ready, 2 * n + 2)
                nc.gpsimd.tensor_tensor(K[i][:], chunk(k_T, n), growth[:], ALU.mult).then_inc(kr_made, 1)
                nc.gpsimd.tensor_tensor(R[i][:], chunk(r_T, n), decline[:, :, 1:CHUNK + 1], ALU.mult).then_inc(kr_made, 1)

            def levels(n, i):
                pool.wait_ge(l_copied, n + 1)
                for j in range(1, LEVELS):
                    if j >= 3:
                        pool.wait_ge(z_ready, n * (LEVELS - 1) + j - 2)
                    nc.gpsimd.tensor_tensor(L_level[j % 2][:], L[:], mask(MASK_LEVEL + j), ALU.mult).then_inc(l_level_ready, 1)

            def first():
                pool.wait_ge(masks_loaded, 16)
                make_kr(0, 0)
                levels(0, 0)

            def body(n, i, ahead, turn):
                if ahead:
                    pool.wait_ge(y_ready, n)
                    pool.wait_ge(z_ready, (n + 1) * (LEVELS - 1))
                    make_kr(n + 1, 1 - i)
                    levels(n + 1, 1 - i)
            run(pool, first, body)

        @block.scalar
        def _(act):
            def exps(n):
                act.wait_ge(a_made, n)
                act.wait_ge(b_made, n)
                act.wait_ge(kr_made, 2 * n)
                act.wait_ge(end_copied, n)
                nc.scalar.activation(decline[:, :, 1:CHUNK + 1], chunk(decay_T, n), ACT.Exp).then_inc(exps_ready, 1)
                nc.scalar.activation(growth[:], chunk(decay_T, n), ACT.Exp, scale=-1.0).then_inc(exps_ready, 1)

            def copy_l(n):
                act.wait_ge(t_begun, n + 1)
                act.wait_ge(l_level_ready, n * (LEVELS - 1))
                nc.scalar.copy(L[:], bank_X[:]).then_inc(l_copied, 1)

            def copy_z(n, j):
                act.wait_ge(z_ready, n * (LEVELS - 1) + j)
                act.wait_ge(xt_ready, n * (LEVELS - 1) + j - 1)
                nc.scalar.copy(Z[:], bank_Z[:]).then_inc(z_copied, 1)

            def copy_rows(n, i):
                act.wait_ge(rows_ready, 2 * n + 1)
                nc.scalar.copy(K_rows[i][:], bank_K[:]).then_inc(k_rows_copied, 1)
                act.wait_ge(rows_ready, 2 * n + 2)
                nc.scalar.copy(B_rows[i][:], bank_W[:]).then_inc(b_rows_copied, 1)

            def first():
                exps(0)
                copy_l(0)
                copy_z(0, 1)
                copy_rows(0, 0)
                for j in range(2, LEVELS):
                    copy_z(0, j)

            def body(n, i, ahead, turn):
                if ahead:
                    exps(n + 1)
                act.wait_ge(w_ready, n + 1)
                act.wait_ge(u_ready, n)
                nc.scalar.copy(W[:], bank_W[:]).then_inc(w_copied, 1)
                act.wait_ge(u_ready, n + 1)
                act.wait_ge(y_ready, n)
                act.wait_ge(s_ready, n)
                nc.scalar.copy(U[:], bank_U[:]).then_inc(u_copied, 1)
                if ahead:
                    copy_l(n + 1)
                    copy_z(n + 1, 1)
                    copy_rows(n + 1, 1 - i)
                    copy_z(n + 1, 2)
                act.wait_ge(y_ready, n + 1)
                nc.scalar.copy(chunk(y_T, n), bank_Y[:]).then_inc(y_copied, 1)
                if ahead:
                    for j in range(3, LEVELS):
                        copy_z(n + 1, j)
            run(act, first, body)

        @block.vector
        def _(dve):
            def make_ab(n, i):
                dve.wait_ge(exps_ready, 2 * n + 1)
                nc.vector.scalar_tensor_tensor(out=A[i][:], in0=chunk(kk_T, n), scalar=-1.0, in1=decline[:, :, 0:CHUNK], op0=ALU.mult, op1=ALU.mult).then_inc(a_made, 1)
                nc.vector.tensor_copy(end_decay[:, i, :], decline[:, :, CHUNK]).then_inc(end_copied, 1)
                dve.wait_ge(exps_ready, 2 * n + 2)
                nc.vector.tensor_tensor(B[i][:], chunk(kka_T, n), growth[:], ALU.mult).then_inc(b_made, 1)

            def start_inverse(n, i):
                dve.wait_ge(l_ready, 2 * n + 1)
                nc.vector.tensor_tensor(X[i][:], bank_Z[:], mask(MASK_FIRST_T), ALU.mult).then_inc(nt_used, 1)
                dve.wait_ge(l_ready, 2 * n + 2)
                nc.vector.tensor_tensor(T[:], bank_X[:], mask(MASK_LEVEL), ALU.mult).then_inc(t_begun, 1)
                dve.wait_ge(nt_used, n + 1)
                nc.vector.tensor_tensor(X[i][:], X[i][:], mask(MASK_IDENT), ALU.add).then_inc(x_added, 1)
                dve.wait_ge(t_begun, n + 1)
                nc.vector.tensor_tensor(T[:], T[:], mask(MASK_IDENT), ALU.add).then_inc(t_added, 1)

            def inter(n, i):
                for q, (out, src, which, used) in enumerate(((AK[i], bank_T, MASK_BEFORE, ak_used), (RK[i], bank_K, MASK_UP_TO, rk_used), (RB[i], bank_U, MASK_UP_TO, rb_used))):
                    dve.wait_ge(inter_ready, 3 * n + q + 1)
                    nc.vector.tensor_tensor(out[:], src[:], mask(which), ALU.mult).then_inc(used, 1)

            def add(n, i, j):
                done = n * (LEVELS - 1) + j
                dve.wait_ge(xt_ready, done)
                dve.wait_ge(x_added, n * LEVELS + j)
                nc.vector.tensor_tensor(X[i][:], X[i][:], bank_X[:], ALU.add).then_inc(x_added, 1)
                if j < LEVELS - 1:
                    dve.wait_ge(t_added, n * (LEVELS - 1) + j)
                    nc.vector.tensor_tensor(T[:], T[:], bank_T[:], ALU.add).then_inc(t_added, 1)

            def first():
                dve.wait_ge(edge_set, 1)
                dve.wait_ge(state_zero, 1)
                dve.wait_ge(masks_loaded, 16)
                make_ab(0, 0)
                start_inverse(0, 0)
                inter(0, 0)
                for j in range(1, LEVELS):
                    add(0, 0, j)

            def body(n, i, ahead, turn):
                if ahead:
                    dve.wait_ge(w_ready, n)
                    dve.wait_ge(s_updated, n)
                    make_ab(n + 1, 1 - i)
                    start_inverse(n + 1, 1 - i)
                    dve.wait_ge(y_ready, n)
                    inter(n + 1, 1 - i)
                    add(n + 1, 1 - i, 1)
                    add(n + 1, 1 - i, 2)
                dve.wait_ge(s_ready, n + 1)
                dve.wait_ge(w_ready, n + 1)
                dve.wait_ge(y_ready, n + 1)
                nc.vector.tensor_tensor(S[:], S[:], bank_S[:], ALU.add).then_inc(s_added, 1)
                dve.wait_ge(s_added, n + 1)
                nc.vector.tensor_tensor(S[:], S[:], end_decay[:, i, :].unsqueeze(2).to_broadcast([P, PAIRS, CHUNK]), ALU.mult).then_inc(s_updated, 1)
                if ahead:
                    for j in range(3, LEVELS):
                        add(n + 1, 1 - i, j)
            run(dve, first, body)

        @block.tensor
        def _(pe):
            def heads(out, *terms, pairs=range(PAIRS)):
                pe.sem_inc(products_begun, 1)
                for q in pairs:
                    for k, (left, right) in enumerate(terms):
                        for h in range(2):
                            rows = slice(h * CHUNK, (h + 1) * CHUNK)
                            mm = nc.tensor.matmul(out[rows, q, :], left[rows, q, :], right[rows, q, :], start=(k == 0), stop=(k == len(terms) - 1))
                return mm

            def rows_of(out, x):
                pe.sem_inc(products_begun, 1)
                for q in range(PAIRS):
                    for h in range(2):
                        rows = slice(h * CHUNK, (h + 1) * CHUNK)
                        mm = nc.tensor.matmul(out[rows, q, :], x[rows, q, :], masks[rows, MASK_IDENT, :], start=True, stop=True)
                return mm

            def products(n, i):
                pe.wait_ge(a_made, n + 1)
                pe.wait_ge(b_made, n + 1)
                pe.wait_ge(x_added, n * LEVELS)
                pe.wait_ge(t_added, n * (LEVELS - 1))
                heads(bank_Z, (B[i], A[i])).then_inc(l_ready, 1)
                heads(bank_X, (A[i], B[i])).then_inc(l_ready, 1)
                pe.wait_ge(kr_made, 2 * n + 2)
                heads(bank_T, (K[i], A[i])).then_inc(inter_ready, 1)
                pe.wait_ge(k_rows_copied, n)
                heads(bank_K, (K[i], R[i])).then_inc(inter_ready, 1)
                pe.wait_ge(u_copied, n)
                heads(bank_U, (B[i], R[i])).then_inc(inter_ready, 1)

            def z(n, i, j):
                pe.wait_ge(l_level_ready, n * (LEVELS - 1) + j)
                pe.wait_ge(x_added, n * LEVELS + j)
                if j == 1:
                    pe.wait_ge(nt_used, n + 1)
                heads(bank_Z, (L_level[j % 2], X[i])).then_inc(z_ready, 1)

            def xt(n, i, j):
                pe.wait_ge(z_copied, n * (LEVELS - 1) + j)
                pe.wait_ge(t_added, n * (LEVELS - 1) + j)
                if j == 1:
                    pe.wait_ge(l_copied, n + 1)
                    pe.wait_ge(ak_used, n + 1)
                mm = heads(bank_X, (T, Z))
                if j < LEVELS - 1:
                    mm = heads(bank_T, (Z, T))
                mm.then_inc(xt_ready, 1)

            def key_rows(n, i):
                pe.wait_ge(rk_used, n + 1)
                rows_of(bank_K, K[i]).then_inc(rows_ready, 1)

            def b_rows(n, i):
                pe.wait_ge(w_copied, n)
                pe.wait_ge(b_rows_copied, n)
                rows_of(bank_W, B[i]).then_inc(rows_ready, 1)

            def out_y(n, i):
                pe.wait_ge(rb_used, n + 1)
                pe.wait_ge(u_copied, n + 1)
                pe.wait_ge(y_copied, n)
                heads(bank_Y, (S, R[i]), (U, RB[i]), (V[i], RK[i])).then_inc(y_ready, 1)

            def out_s(n, i):
                pe.wait_ge(k_rows_copied, n + 1)
                pe.wait_ge(b_rows_copied, n + 1)
                pe.wait_ge(u_copied, n + 1)
                pe.wait_ge(s_updated, n)
                heads(bank_S, (B_rows[i], U), (K_rows[i], V[i])).then_inc(s_ready, 1)

            def first():
                pe.wait_ge(masks_loaded, 16)
                pe.wait_ge(state_zero, 1)
                products(0, 0)
                z(0, 0, 1)
                key_rows(0, 0)
                b_rows(0, 0)
                xt(0, 0, 1)
                for j in range(2, LEVELS):
                    z(0, 0, j)
                    xt(0, 0, j)

            def body(n, i, ahead, turn):
                pe.wait_ge(s_updated, n)
                pe.wait_ge(ak_used, n + 1)
                pe.wait_ge(b_rows_copied, n + 1)
                pe.wait_ge(v_loaded[i], 32 * (turn + 1))
                heads(bank_W, (A[i], S), (AK[i], V[i])).then_inc(w_ready, 1)
                pe.wait_ge(w_copied, n + 1)
                pe.wait_ge(x_added, (n + 1) * LEVELS)
                pe.wait_ge(rb_used, n + 1)
                heads(bank_U, (X[i], W)).then_inc(u_ready, 1)
                o = 1 - i
                if ahead:
                    products(n + 1, o)
                    z(n + 1, o, 1)
                    key_rows(n + 1, o)
                    b_rows(n + 1, o)
                    xt(n + 1, o, 1)
                out_s(n, i)
                if ahead:
                    z(n + 1, o, 2)
                out_y(n, i)
                if ahead:
                    xt(n + 1, o, 2)
                    for j in range(3, LEVELS):
                        z(n + 1, o, j)
                        xt(n + 1, o, j)
            run(pe, first, body)
    clear_semaphores(nc, sems)


def rwkv_finish(nc, m, y_T, g_T, bonus_T, mixed_T):
    with ExitStack() as ctx:
        sems = []

        def sem(name):
            sems.append(ctx.enter_context(nc.semaphore(name)))
            return sems[-1]

        def sb(name, shape):
            return ctx.enter_context(nc.sbuf_tensor(name, shape, F32))

        pair_mean, eps = sb("pair_mean", [P, P]), sb("lnx_eps", [P, 1])
        centred, square, root = sb("gn_centred", [P, 2, SEQ]), sb("gn_square", [P, 2, SEQ]), sb("gn_root", [P, 2, SEQ])
        psum_mean = [ctx.enter_context(nc.psum_tensor(f"psum_mean{i}", [P, SEQ], F32)) for i in range(2)]
        psum_var = [ctx.enter_context(nc.psum_tensor(f"psum_var{i}", [P, SEQ], F32)) for i in range(2)]
        loaded, eps_set, steps = sem("gn_loaded"), sem("gn_eps"), sem("gn_steps")
        mean_ready, centred_ready, square_ready, var_ready, root_ready, done = (sem("gn_mean"), sem("gn_centred"), sem("gn_square"), sem("gn_var"),
                                                                               sem("gn_root"), sem("gn_done"))
        block = ctx.enter_context(nc.Block())

        @block.sync
        def _(sp):
            sp.dma_start(pair_mean[:], m.a["pair_mean"]).then_inc(loaded, 16)
            sp.dma_start(m.w_out[:], m.a["odd_w_out"][0].rearrange("(k p) n -> p k n", p=P)).then_inc(m.w_out_loaded, 16)

        @block.gpsimd
        def _(pool):
            pool.memset(eps[:], LNX_EPS).then_inc(eps_set, 1)

        @block.tensor
        def _(pe):
            def mean(f):
                if f >= 2:
                    pe.wait_ge(centred_ready, f - 1)
                nc.tensor.matmul(psum_mean[f % 2][:], pair_mean[:], y_T[:, f, :], start=True, stop=True).then_inc(mean_ready, 1)

            pe.wait_ge(loaded, 16)
            mean(0)
            for f in range(KD):
                if f + 1 < KD:
                    mean(f + 1)
                pe.wait_ge(square_ready, f + 1)
                if f >= 2:
                    pe.wait_ge(root_ready, f - 1)
                nc.tensor.matmul(psum_var[f % 2][:], pair_mean[:], square[:, f % 2, :], start=True, stop=True).then_inc(var_ready, 1)

        @block.scalar
        def _(act):
            act.wait_ge(eps_set, 1)
            for f in range(KD):
                act.wait_ge(centred_ready, f + 1)
                if f >= 2:
                    act.wait_ge(var_ready, f - 1)
                nc.scalar.activation(square[:, f % 2, :], centred[:, f % 2, :], ACT.Square).then_inc(square_ready, 1)
                act.wait_ge(var_ready, f + 1)
                if f >= 2:
                    act.wait_ge(done, f - 1)
                nc.scalar.activation(root[:, f % 2, :], psum_var[f % 2][:], ACT.Sqrt, bias=eps[:]).then_inc(root_ready, 1)

        @block.vector
        def _(dve):
            c = Chain(dve, steps)

            def centre(f):
                dve.wait_ge(mean_ready, f + 1)
                if f >= 2:
                    dve.wait_ge(done, f - 1)
                nc.vector.tensor_tensor(centred[:, f % 2, :], y_T[:, f, :], psum_mean[f % 2][:], ALU.subtract).then_inc(centred_ready, 1)

            centre(0)
            for f in range(KD):
                b = f % 2
                if f + 1 < KD:
                    centre(f + 1)
                dve.wait_ge(root_ready, f + 1)
                dve.wait_ge(square_ready, f + 1)
                x = centred[:, b, :]
                c.link(nc.vector.reciprocal(root[:, b, :], root[:, b, :]))
                c.link(nc.vector.tensor_tensor(x, x, root[:, b, :], ALU.mult))
                c.link(nc.vector.tensor_scalar(x, x, m.params[:, PARAM["lnx_g"], f:f + 1], m.params[:, PARAM["lnx_b"], f:f + 1], ALU.mult, ALU.add))
                c.link(nc.vector.tensor_tensor(x, x, bonus_T[:, f, :], ALU.add))
                nc.vector.tensor_tensor(mixed_T[:, f, :], x, g_T[:, f, :], ALU.mult).then_inc(done, 1)
    clear_semaphores(nc, sems)


def trunk(nc, a, out):
    m = Shared(a, out)
    with ExitStack() as ctx:
        def sb(name, shape, dt=F32):
            return ctx.enter_context(nc.sbuf_tensor(name, shape, dt))

        def sem(name):
            return ctx.enter_context(nc.semaphore(name))

        def big(name, scope):
            return scope.enter_context(nc.sbuf_tensor(name, [P, KD, SEQ], F32))

        m.stream = sb("stream", [P, NT, D_MODEL])
        gate0, up0 = big("w_gate0", ctx), big("w_up0", ctx)
        m.ident, m.earlier, m.ones = sb("ident", [P, P]), sb("earlier", [P, P]), sb("ones", [P, P])
        m.expert_iota, m.group_iota, m.expert_base = sb("expert_iota", [P, N_EXPERTS]), sb("group_iota", [P, N_EXPERTS]), sb("expert_base", [P, N_EXPERTS])
        m.entries = sb("entries", [P, NT, TOP_K, 2], U32)
        m.ln_eps, m.stats, m.moments = sb("ln_eps", [P, 1]), sb("stats", [P, 2, 6]), sb("moments", [P, NT, 3])
        m.gates, m.most_tokens = sb("gates", [P, NT, TOP_K]), sb("most_tokens", [1, 1], I32)
        m.params = sb("vector_params", [P, len(PARAM) + 5, KD])

        def scratch(name, shape, dt=F32):
            return nc.dram_tensor(name, shape, dt, kind="Internal").ap()

        m.table = scratch("table", [N_EXPERTS * SEQ, 2], U32)
        m.h_dram, m.y_dram = scratch("h_dram", [SEQ, D_MODEL]), scratch("y_dram", [SEQ * TOP_K, D_MODEL])
        m.x_dram, m.v_dram = scratch("x_dram", [SEQ, D_MODEL]), scratch("v_dram", [SEQ, D_MODEL])

        m.w_loaded = {part: [sem(f"{part}_loaded{half}") for half in range(2)] for part in ("gate", "up", "down")}
        m.first_weights = [(part, half) for part in ("gate", "up") for half in range(2)]
        m.w_out_loaded, consts_loaded = sem("w_out_loaded"), sem("consts_loaded")
        m.table_entry = [sem(f"table_entry{layer}") for layer in range(DEPTH)]
        m.x_gathered = [[sem(f"x_gathered{i}_{layer}") for i in range(UNROLL)] for layer in range(DEPTH)]
        m.y_scattered = [[sem(f"y_scattered{i}_{layer}") for i in range(2)] for layer in range(DEPTH)]

        with nc.Block() as block:
            @block.sync
            def _(sp):
                consts = {"ident": m.ident, "earlier": m.earlier, "ones": m.ones, "expert_iota": m.expert_iota,
                          "group_iota": m.group_iota, "expert_base": m.expert_base, "entries": m.entries}
                for name, tile in consts.items():
                    sp.dma_start(tile[:], a[name]).then_inc(consts_loaded, 16)
                sp.wait_ge(consts_loaded, 16 * len(consts))

            @block.gpsimd
            def _(pool):
                pool.memset(m.ln_eps[:], LN_EPS)

        for layer in range(DEPTH):
            m.w_raw = {"gate": gate0, "up": up0}
            with ExitStack() as scope:
                m.ln_gain, m.ln_bias = [scope.enter_context(nc.sbuf_tensor(f"{name}{layer}", [P, D_MODEL], F32))[:] for name in ("ln_gain", "ln_bias")]
                if layer % 2 == 0:
                    heads_T = scope.enter_context(nc.sbuf_tensor("heads_T", [P, 16, SEQ], F32))
                    values = scope.enter_context(nc.sbuf_tensor("values", [P, 2, NT, 512], F32))
                    attention_project(nc, m, heads_T, values)
                    m.w_out = scope.enter_context(nc.sbuf_tensor("w_out0", [P, KD, D_MODEL], F32))
                    attention_heads(nc, m, heads_T, values, m.stream)
                    residual = values[:].rearrange("p a t n -> p (a t n)").rearrange("p (t d) -> p t d", t=NT)
                    mixer_output(nc, m, layer, heads_T[:, 0:KD, :], m.stream, residual)
                else:
                    as_features = lambda t: t[:].rearrange("p t (h n) -> p (t h) n", n=SEQ)
                    r_T, k_T, decay_T, kk_T = [big(name, scope) for name in ("r_T", "k_T", "decay_T", "kk_T")]
                    value = scope.enter_context(nc.sbuf_tensor("value", [P, NT, D_MODEL], F32))
                    bonus_T, a_T, g_T, y_T = as_features(m.stream), up0, gate0, as_features(value)
                    with ExitStack() as inner:
                        logit = inner.enter_context(nc.sbuf_tensor("logit", [P, NT, D_MODEL], F32))
                        with ExitStack() as first:
                            mixes, weights = [kk_T, big("mix1", first)], [big("w_rwkv0", first), big("w_rwkv1", first)]
                            rwkv_project(nc, m, r_T, k_T, value, logit, a_T, g_T, decay_T, as_features(m.stream), mixes, weights)
                        rwkv_prepare(nc, m, r_T, k_T, value, logit, a_T, decay_T, kk_T, bonus_T)
                    rwkv_scan(nc, m, r_T, k_T, a_T, decay_T, kk_T, y_T)
                    m.w_out = scope.enter_context(nc.sbuf_tensor("w_out1", [P, KD, D_MODEL], F32))
                    rwkv_finish(nc, m, y_T, g_T, bonus_T, r_T)
                    mixer_output(nc, m, layer, r_T, None, value)
            with ExitStack() as scope:
                m.w_raw["down"] = scope.enter_context(nc.sbuf_tensor(f"w_down_{layer}", [P, KE, D_MODEL], F32))
                m.x_rows = [scope.enter_context(nc.sbuf_tensor(f"x_rows{i}_{layer}", [SLOTS, D_MODEL], F32)) for i in range(2)]
                m.slot_rows = [scope.enter_context(nc.sbuf_tensor(f"slot_rows{i}_{layer}", [SLOTS, 2], U32)) for i in range(UNROLL)]
                moe_route(nc, m, layer)
                moe_experts(nc, m, layer)
                moe_combine(nc, m, layer)


_INPUTS = ["x", "ln_g", "ln_b", "even_w_in", "even_w_out", "even_lambda", "even_subln_g", "odd_w_rkv", "odd_w0", "odd_w1", "odd_w2",
           "odd_a1", "odd_a2", "odd_g1", "odd_g2", "odd_w_out", "router_w", "router_b", "moe_w_gate", "moe_w_up", "moe_w_down"]


def kernel(**inputs):
    import concourse.bacc as bacc
    from concourse.bass_utils import run_bass_kernel_spmd

    nc = bacc.Bacc("TRN2", target_bir_lowering=False, num_devices=1)
    given = {name: np.ascontiguousarray(inputs[name]) for name in _INPUTS}
    given.update(laid_out(inputs))
    given.update(shape_constants())
    arrays, aps = {}, {}
    for name, array in given.items():
        arrays[f"in_{name}"] = array
        aps[name] = nc.dram_tensor(f"in_{name}", array.shape, mybir.dt.from_np(array.dtype), kind="ExternalInput").ap()
    out = nc.dram_tensor("out", (1, SEQ, D_MODEL), F32, kind="ExternalOutput").ap()
    trunk(nc, aps, out)
    result = run_bass_kernel_spmd(nc, [arrays], core_ids=[0])
    return result.results[0]["out"]
```

```python
import math
from contextlib import ExitStack

import numpy as np

import concourse.bass as bass
from concourse import mybir

F32 = mybir.dt.float32
F32R = mybir.dt.float32r
U32 = mybir.dt.uint32
I32 = mybir.dt.int32
ALU = mybir.AluOpType
ACT = mybir.ActivationFunctionType
AX = mybir.AxisListType

P = 128
D_MODEL, SEQ, DEPTH = 1024, 512, 2
KD = D_MODEL // P
NT = SEQ // P
CHUNK = 64
N_EXPERTS, N_GROUPS, TOP_K = 32, 4, 2
PER_GROUP = N_EXPERTS // N_GROUPS
D_EXPERT = D_MODEL // 2
KE = D_EXPERT // P
SLOTS = 128
UNROLL = 4
AHEAD = 2
TURNS = N_EXPERTS // UNROLL
LN_EPS = 1e-5
DVE_SHARE, POOL_SHARE = slice(0, 640), slice(640, D_MODEL)
ALPHA = (2 * DEPTH) ** 0.25
BIG = 3e38
NOWHERE = 1 << 20
A_HEADS, A_DIM, B_HEADS = D_MODEL // 256, 64, D_MODEL // 128
ROPE_DIM, ROPE_THETA, SUBLN_EPS, REL_CLIP = A_DIM // 4, 500000.0, 1e-5, 128
LAMBDA_INIT = 0.8 - 0.6 * math.exp(-0.3 * 0)
NEG_INF = -1e30
N_CHUNKS, PAIRS = SEQ // CHUNK, D_MODEL // 128
LORA_W, LORA_A, LORA_G = 64, 64, 160
LNX_EPS = 1e-5 * CHUNK
PARAM = {"mix": 0, "a0": 6, "k_k": 7, "k_a": 8, "r_k": 9, "lnx_g": 10, "lnx_b": 11}
LEVELS = 6
MASK_IDENT, MASK_BEFORE, MASK_UP_TO, MASK_FIRST_T, MASK_LEVEL = 0, 1, 2, 3, 4
N_MASKS = MASK_LEVEL + LEVELS


class Shared:

    def __init__(self, a, out):
        self.a, self.out = a, out


def shape_constants():
    i = np.arange(P)
    c = {
        "ident": np.eye(P, dtype=np.float32),
        "earlier": (i[:, None] < i[None, :]).astype(np.float32),
        "ones": np.ones((P, P), np.float32),
    }
    e = np.arange(N_EXPERTS)
    c["expert_iota"] = np.tile(e, (P, 1)).astype(np.float32)
    c["group_iota"] = np.tile(e // PER_GROUP, (P, 1)).astype(np.float32)
    c["expert_base"] = np.tile(e * SEQ, (P, 1)).astype(np.float32)
    token = np.arange(SEQ).reshape(NT, P).T
    c["entries"] = np.stack([np.stack([token, TOP_K * token + k], -1) for k in range(TOP_K)], 2).astype(np.uint32)
    c["nowhere"] = np.full((P, 2 * N_EXPERTS * SEQ // P), NOWHERE, np.uint32)
    half = ROPE_DIM // 2
    inv = np.float32(ROPE_THETA) ** (-np.arange(half, dtype=np.float32) / half)
    angle = np.arange(SEQ, dtype=np.float32)[None, :] * inv.astype(np.float32)[:, None]
    cos, sin = np.ones((A_DIM, SEQ), np.float32), np.zeros((A_DIM, SEQ), np.float32)
    cos[:ROPE_DIM], sin[:ROPE_DIM] = np.tile(np.cos(angle), (2, 1)), np.tile(np.sin(angle), (2, 1))
    c["rot_cos"], c["rot_sin"] = np.tile(cos, (2, 1)), np.tile(sin, (2, 1))
    swap = np.zeros((P, P), np.float32)
    for base in (0, A_DIM):
        for d in range(half):
            swap[base + half + d, base + d] = -1.0
            swap[base + d, base + half + d] = 1.0
    c["rot_swap"] = swap
    c["mask_q"] = (i < CHUNK).astype(np.float32)[None, :]
    c["mask_k"] = np.where(i >= CHUNK, np.float32(NEG_INF), np.float32(0.0)).astype(np.float32)[None, :]
    same = i[:, None] // CHUNK == i[None, :] // CHUNK
    c["sum_decay"] = np.where(same & (i[:, None] <= i[None, :]), np.float32(-math.exp(-0.5)), np.float32(0.0)).astype(np.float32)
    c["pair_ones"] = same.astype(np.float32)
    c["pair_centre"] = c["ident"] - (same / CHUNK).astype(np.float32)
    of_head = np.arange(2 * PAIRS)[None, None, :] == (2 * np.arange(KD)[None, :, None] + i[:, None, None] // CHUNK)
    c["head_mean"] = (of_head / CHUNK).astype(np.float32)
    c["head_spread"] = np.ascontiguousarray(of_head.transpose(2, 1, 0)).astype(np.float32)
    r, q = np.arange(CHUNK)[:, None], np.arange(CHUNK)[None, :]
    masks = [r == q, r < q, r <= q, (r % 2 == 0) & (q == r + 1)]
    for level in range(LEVELS):
        size = 2 ** level
        masks.append((r // (2 * size) == q // (2 * size)) & (r // size == q // size + 1))
    c["scan_masks"] = np.tile(np.stack(masks, 1).astype(np.float32), (2, 1, 1))
    return c


def laid_out(inputs):
    query, key = np.arange(P)[:, None] + SEQ - P, np.arange(SEQ)[None, :]
    distance = np.clip(query - key, -REL_CLIP, REL_CLIP) + REL_CLIP
    vectors = [*np.asarray(inputs["odd_mix"])[0]]
    vectors += [np.asarray(inputs[name])[0].reshape(-1) for name in ("odd_a0", "odd_k_k", "odd_k_a", "odd_r_k", "odd_lnx_g", "odd_lnx_b")]
    return {
        "params": np.ascontiguousarray(np.stack(vectors).reshape(len(vectors), KD, P).transpose(2, 0, 1)),
        "x_T": np.ascontiguousarray(np.asarray(inputs["x"])[0].T),
        "rel_bias_rows": np.ascontiguousarray(np.asarray(inputs["even_rel_bias"])[0][:, distance].transpose(1, 0, 2)),
    }


class Chain:

    def __init__(self, engine, steps_done):
        self.engine, self.steps_done = engine, steps_done
        self.count, self.ahead = 0, 0

    def link(self, instruction):
        self.mark(instruction)
        self.wait()

    def mark(self, instruction):
        instruction.then_inc(self.steps_done, 1)
        self.count += 1

    def wait(self):
        self.engine.wait_ge(self.steps_done, self.ahead + self.count)


def norm_moments(nc, chain, pre, stats, moments, var_ready):
    for half in range(2):
        chain.mark(nc.vector.bn_stats(stats[:, half, :], pre[:, half * 512:(half + 1) * 512]))
    chain.wait()
    nc.vector.bn_aggr(moments[:, 0:2], stats[:, :, :]).then_inc(var_ready, 1)


def norm_root(nc, act, moments, eps, t, var_ready, root_ready):
    act.wait_ge(var_ready, t + 1)
    nc.scalar.activation(moments[:, 2:3], moments[:, 1:2], ACT.Sqrt, bias=eps).then_inc(root_ready, 1)


def norm_shift(nc, chain, moments, shift_ready):
    chain.link(nc.vector.reciprocal(moments[:, 2:3], moments[:, 2:3]))
    nc.vector.scalar_tensor_tensor(out=moments[:, 3:4], in0=moments[:, 0:1], scalar=-1.0, in1=moments[:, 2:3],
                                   op0=ALU.mult, op1=ALU.mult).then_inc(shift_ready, 1)


def norm_scale(nc, act, pre, moments, t, shift_ready, scaled):
    act.wait_ge(shift_ready, t + 1)
    nc.scalar.activation(pre, pre, ACT.Identity, bias=moments[:, 3:4], scale=moments[:, 2:3]).then_inc(scaled, 1)


def norm_finish(engine, pre, gain, bias, out, share, t, scaled, multiplied, finished):
    engine.wait_ge(scaled, t + 1)
    engine.tensor_tensor(pre[:, share], pre[:, share], gain[:, share], ALU.mult).then_inc(multiplied, 1)
    engine.wait_ge(multiplied, t + 1)
    engine.tensor_tensor(out[:, share], pre[:, share], bias[:, share], ALU.add).then_inc(finished, 1)


def clear_semaphores(nc, semaphores):
    with nc.Block() as block:
        @block.gpsimd
        def _(pool):
            for s in semaphores:
                pool.sem_clear(s)


def moe_route(nc, m, layer):
    with ExitStack() as ctx:
        def sb(name, shape, dt=F32):
            return ctx.enter_context(nc.sbuf_tensor(f"{name}_r{layer}", shape, dt))

        hidden_T = sb("hidden_T", [P, KD, SEQ])
        scores = sb("scores", [P, NT, N_EXPERTS])
        select = sb("select", [P, NT, N_EXPERTS])
        group_top = sb("group_top", [P, NT, N_GROUPS, 8])
        group_score = sb("group_score", [P, NT, 8])
        group_best = sb("group_best", [P, NT, 8])
        group_index = sb("group_index", [P, NT, 8], U32)
        group_of_token = sb("group_of_token", [P, NT])
        penalty = sb("penalty", [P, NT, N_EXPERTS])
        expert_best = sb("expert_best", [P, NT, 8])
        expert_index = sb("expert_index", [P, NT, 8], U32)
        expert_of_token = sb("expert_of_token", [P, NT, TOP_K])
        chosen = sb("chosen", [P, NT, TOP_K, N_EXPERTS])
        product = sb("product", [P, NT, TOP_K, N_EXPERTS])
        chosen_any = sb("chosen_any", [P, NT, N_EXPERTS])
        slot_value = sb("slot_value", [P, NT, N_EXPERTS])
        gate_raw = sb("gate_raw", [P, NT, TOP_K])
        gate_sum = sb("gate_sum", [P, NT])
        slot_f = sb("slot_f", [P, NT, TOP_K])
        slot_u = sb("slot_u", [P, NT, TOP_K], U32)
        most_f = sb("most_f", [1, 1])
        psum_T = [ctx.enter_context(nc.psum_tensor(f"psum_T{i}_r{layer}", [P, 512], F32)) for i in range(4)]
        psum_logits = ctx.enter_context(nc.psum_tensor(f"psum_logits_r{layer}", [P, NT, N_EXPERTS], F32))
        psum_rank = ctx.enter_context(nc.psum_tensor(f"psum_rank_r{layer}", [P, NT + 1, N_EXPERTS], F32))
        table_entry = m.table_entry[layer]
        nowhere = sb("nowhere", [P, 2 * N_EXPERTS * SEQ // P], U32)
        router_w, router_b = sb("router_w", [P, KD, N_EXPERTS]), sb("router_b", [P, N_EXPERTS])
        names = ("hidden_stored", "table_empty", "transposed", "copied_act", "copied_dve", "logits", "scores", "chosen", "rank", "slots",
                 "dve_steps", "router_loaded", "nowhere_loaded")
        S = [ctx.enter_context(nc.semaphore(f"{name}_r{layer}")) for name in names]
        (hidden_stored, table_empty, transposed, copied_act, copied_dve, logits_ready,
         scores_ready, chosen_ready, rank_ready, slots_ready, dve_steps, router_loaded, nowhere_loaded) = S
        block = ctx.enter_context(nc.Block())

        @block.sync
        def _(sp):
            sp.dma_start(router_w[:], m.a["router_w"].rearrange("(k p) e -> p k e", p=P)).then_inc(router_loaded, 16)
            sp.dma_start(router_b[:], m.a["router_b"].partition_broadcast(P)).then_inc(router_loaded, 16)
            sp.dma_start(nowhere[:], m.a["nowhere"]).then_inc(nowhere_loaded, 16)
            sp.wait_ge(nowhere_loaded, 16)
            sp.dma_start(m.table.rearrange("(p n) c -> p (n c)", p=P), nowhere[:]).then_inc(table_empty, 16)
            sp.dma_start(m.h_dram.rearrange("(t p) d -> p t d", p=P), m.stream[:]).then_inc(hidden_stored, 16)
            load_expert(nc, sp, m, layer, 0, (("down", 0), ("down", 1)))
            sp.wait_ge(hidden_stored, 16)

        @block.tensor
        def _(pe):
            for n in range(2 * NT):
                t, half = n // 2, n % 2
                if n >= 4:
                    pe.wait_ge(copied_dve if n % 2 else copied_act, n // 2 - 1)
                for j in range(4):
                    k = 4 * half + j
                    last = nc.tensor.transpose(psum_T[n % 4][:, j * P:(j + 1) * P], m.stream[:, t, k * P:(k + 1) * P], m.ident[:])
                last.then_inc(transposed, 1)
            pe.wait_ge(router_loaded, 32)
            for t in range(NT):
                pe.wait_ge(copied_act, t + 1)
                pe.wait_ge(copied_dve, t + 1)
                for k in range(KD):
                    last = nc.tensor.matmul(psum_logits[:, t, :], hidden_T[:, k, t * P:(t + 1) * P], router_w[:, k, :],
                                            start=(k == 0), stop=(k == KD - 1))
            last.then_inc(logits_ready, 1)
            pe.wait_ge(chosen_ready, 1)
            for t in range(NT):
                for j in range(t + 1):
                    nc.tensor.matmul(psum_rank[:, t, :], (m.earlier if j == t else m.ones)[:], chosen_any[:, j, :],
                                     start=(j == 0), stop=(j == t))
            for j in range(NT):
                last = nc.tensor.matmul(psum_rank[:, NT, :], m.ones[:], chosen_any[:, j, :], start=(j == 0), stop=(j == NT - 1))
            last.then_inc(rank_ready, 1)

        @block.scalar
        def _(act):
            for t in range(NT):
                act.wait_ge(transposed, 2 * t + 1)
                nc.scalar.copy(hidden_T[:, 0:4, t * P:(t + 1) * P], psum_T[2 * t % 4][:].rearrange("p (j n) -> p j n", j=4)).then_inc(copied_act, 1)
            act.wait_ge(logits_ready, 1)
            nc.scalar.activation(scores[:], psum_logits[:], ACT.Sigmoid).then_inc(scores_ready, 1)

        @block.vector
        def _(dve):
            c = Chain(dve, dve_steps)
            c.link(nc.vector.memset(group_score[:], -BIG))
            for t in range(NT):
                dve.wait_ge(transposed, 2 * t + 2)
                nc.vector.tensor_copy(hidden_T[:, 4:8, t * P:(t + 1) * P], psum_T[(2 * t + 1) % 4][:].rearrange("p (j n) -> p j n", j=4)).then_inc(copied_dve, 1)
            dve.wait_ge(scores_ready, 1)
            dve.wait_ge(router_loaded, 32)
            c.link(nc.vector.tensor_tensor(select[:], scores[:], router_b[:].unsqueeze(1).to_broadcast([P, NT, N_EXPERTS]), ALU.add))
            for t in range(NT):
                for g in range(N_GROUPS):
                    c.mark(nc.vector.max(group_top[:, t, g, :], select[:, t, g * PER_GROUP:(g + 1) * PER_GROUP]))
            c.wait()
            c.link(nc.vector.tensor_tensor(group_score[:, :, 0:N_GROUPS], group_top[:, :, :, 0], group_top[:, :, :, 1], ALU.add))
            for t in range(NT):
                c.mark(nc.vector.max(group_best[:, t, :], group_score[:, t, :]))
            c.wait()
            for t in range(NT):
                c.mark(nc.vector.max_index(group_index[:, t, :], group_best[:, t, :], group_score[:, t, :]))
            c.wait()
            c.link(nc.vector.tensor_copy(group_of_token[:], group_index[:, :, 0]))
            for t in range(NT):
                c.mark(nc.vector.tensor_scalar(penalty[:, t, :], m.group_iota[:], group_of_token[:, t:t + 1], -BIG, ALU.not_equal, ALU.mult))
            c.wait()
            c.link(nc.vector.tensor_tensor(select[:], select[:], penalty[:], ALU.add))
            for t in range(NT):
                c.mark(nc.vector.max(expert_best[:, t, :], select[:, t, :]))
            c.wait()
            for t in range(NT):
                c.mark(nc.vector.max_index(expert_index[:, t, :], expert_best[:, t, :], select[:, t, :]))
            c.wait()
            c.link(nc.vector.tensor_copy(expert_of_token[:], expert_index[:, :, 0:TOP_K]))
            for t in range(NT):
                for k in range(TOP_K):
                    c.mark(nc.vector.tensor_scalar(chosen[:, t, k, :], m.expert_iota[:], expert_of_token[:, t, k:k + 1], None, ALU.is_equal))
            c.wait()
            nc.vector.tensor_tensor(chosen_any[:], chosen[:, :, 0, :], chosen[:, :, 1, :], ALU.add).then_inc(chosen_ready, 1)
            for k in range(TOP_K):
                c.mark(nc.vector.tensor_tensor(product[:, :, k, :], chosen[:, :, k, :], scores[:], ALU.mult))
            c.wait()
            c.link(nc.vector.tensor_reduce(gate_raw[:], product[:], AX.X, ALU.add))
            c.link(nc.vector.tensor_tensor(gate_sum[:], gate_raw[:, :, 0], gate_raw[:, :, 1], ALU.add))
            c.link(nc.vector.reciprocal(gate_sum[:], gate_sum[:]))
            for k in range(TOP_K):
                c.mark(nc.vector.tensor_tensor(m.gates[:, :, k], gate_raw[:, :, k], gate_sum[:], ALU.mult))
            dve.wait_ge(rank_ready, 1)
            c.link(nc.vector.tensor_tensor(slot_value[:], psum_rank[:, 0:NT, :], m.expert_base[:].unsqueeze(1).to_broadcast([P, NT, N_EXPERTS]), ALU.add))
            for k in range(TOP_K):
                c.mark(nc.vector.tensor_tensor(product[:, :, k, :], chosen[:, :, k, :], slot_value[:], ALU.mult))
            c.wait()
            c.link(nc.vector.tensor_reduce(slot_f[:], product[:], AX.X, ALU.add))
            nc.vector.tensor_copy(slot_u[:], slot_f[:]).then_inc(slots_ready, 1)
            c.link(nc.vector.tensor_reduce(most_f[:], psum_rank[0:1, NT, :], AX.X, ALU.max))
            c.link(nc.vector.tensor_copy(m.most_tokens[:], most_f[:]))

        @block.gpsimd
        def _(pool):
            for rows in m.x_rows:
                pool.memset(rows[:], 0.0)
            pool.wait_ge(table_empty, 16)
            pool.wait_ge(slots_ready, 1)
            for t in range(NT):
                for k in range(TOP_K):
                    nc.gpsimd.indirect_dma_start(
                        m.table[:, :], bass.IndirectOffsetOnAxis(ap=slot_u[:, t, k:k + 1], axis=0),
                        m.entries[:, t, k, :], None, bounds_check=N_EXPERTS * SEQ - 1, oob_is_err=False).then_inc(table_entry, 16)
            pool.wait_ge(table_entry, 16 * NT * TOP_K)
    clear_semaphores(nc, S)


def load_expert(nc, engine, m, layer, e, parts):
    for part, half in parts:
        raw = m.w_raw[part]
        k = raw.shape[1] // 2
        rows = m.a[f"moe_w_{part}"][layer, e].rearrange("(p k) n -> p k n", p=P)
        engine.dma_start(raw[:, half * k:(half + 1) * k, :], rows[:, half * k:(half + 1) * k, :]).then_inc(m.w_loaded[part][half], 16)


def moe_experts(nc, m, layer):
    with ExitStack() as ctx:
        def ring(name, n, shape, dt=F32):
            return [ctx.enter_context(nc.sbuf_tensor(f"{name}{i}_e{layer}", shape, dt)) for i in range(n)]

        def bank(name):
            return ctx.enter_context(nc.psum_tensor(f"{name}_e{layer}", [P, 512], F32))

        x_high, x_low = ring("x_high", 2, [P, KD, SLOTS], F32R), ring("x_low", 2, [P, KD, SLOTS], F32R)
        silu = ring("silu", 1, [P, D_EXPERT])[0]
        u = ring("u", 1, [P, D_EXPERT])[0]
        u_high, u_low = [ring(name, 1, [P, KE, SLOTS], F32R)[0] for name in ("u_high", "u_low")]
        y = ring("y", 2, [P, D_MODEL])
        w_high, w_low = [{part: ring(f"{name}_{part}", 1, m.w_raw[part].shape, F32R)[0] for part in ("gate", "up", "down")} for name in ("w_high", "w_low")]
        x, slots = m.x_rows, m.slot_rows
        psum_gate, psum_up, psum_uT = bank("psum_gate"), bank("psum_up"), bank("psum_uT")
        psum_xT = [bank("psum_xT0"), bank("psum_xT1")]
        psum_y = [bank("psum_y0"), bank("psum_y1")]
        names = ("x_transposed", "x_high_made", "x_low_made", "gate_done", "up_done", "silu_done", "u_done", "u_transposed", "u_high_made",
                 "u_low_made", "down_done", "y_copied", "high_made", "low_made", "slots_loaded0", "slots_loaded1", "slots_loaded2", "slots_loaded3",
                 "gathers_begun", "scatters_begun")
        S = [ctx.enter_context(nc.semaphore(f"{name}_e{layer}")) for name in names]
        (x_transposed, x_high_made, x_low_made, gate_done, up_done, silu_done, u_done, u_transposed,
         u_high_made, u_low_made, down_done, y_copied, high_made, low_made) = S[:14]
        slots_loaded = S[14:18]
        gathers_begun, scatters_begun = S[18:20]
        x_gathered, y_scattered = m.x_gathered[layer], m.y_scattered[layer]

        def is_main(j):
            return isinstance(j, int)

        def one_pass(engine, begin, body, turns_done, j):
            begin(turns_done, j)
            peeled = 1 if is_main(j) else 0
            for i in range(UNROLL * peeled):
                body(turns_done, i, i, j, False)
            with engine.Fori(peeled, TURNS - 1) as turn:
                for i in range(UNROLL):
                    body(turns_done + turn, i, turn * UNROLL + i, j, False)
            for i in range(UNROLL):
                body(turns_done + (TURNS - 1), i, N_EXPERTS - UNROLL + i, j, True)

        def run(engine, begin, body):
            one_pass(engine, begin, body, 0, 0)
            most = engine.value_load(m.most_tokens[0:1, 0:1], min_val=0, max_val=SEQ)
            with engine.If(most > SLOTS):
                with engine.Fori(1, SEQ // SLOTS) as again:
                    one_pass(engine, begin, body, again * TURNS, again)

        FIRST_GATE, UP, NEXT_GATE, DOWN, LAST_DOWN, NEXT_UP = 0, 2, 4, 6, 4, 8

        def piece(part, half):
            k = m.w_raw[part].shape[1] // 2
            return [t[part][:, half * k:(half + 1) * k, :] for t in (m.w_raw, w_high, w_low)]

        def make_high(act, part, n, halves=(0, 1)):
            for half in halves:
                raw, high, low = piece(part, half)
                act.wait_ge(m.w_loaded[part][half], 16 * (n + 1))
                nc.scalar.copy(high, raw).then_inc(high_made, 1)

        def make_low(dve, part, n, where, halves=(0, 1)):
            for half in halves:
                raw, high, low = piece(part, half)
                dve.wait_ge(high_made, 6 * n + where + half + 1)
                nc.vector.tensor_tensor(low, raw, high.bitcast(F32), ALU.subtract).then_inc(low_made, 1)

        def product(pe, outs, high, low, part, n, where):
            k_tiles = m.w_raw[part].shape[1]
            for half in range(2):
                raw, piece_high, piece_low = piece(part, half)
                pe.wait_ge(low_made, 6 * n + where + half + 1)
                for q, out in enumerate(outs):
                    cols = slice(q * 512, (q + 1) * 512)
                    for j in range(k_tiles // 2):
                        k = half * (k_tiles // 2) + j
                        for x_part, w_part, first in ((high, piece_high, True), (high, piece_low, False), (low, piece_high, False)):
                            mm = nc.tensor.matmul(out[:], x_part[:, k, :], w_part[:, j, cols],
                                                  start=(k == 0 and first), stop=(k == k_tiles - 1 and x_part is low))
            return mm

        block = ctx.enter_context(nc.Block())

        @block.sync
        def _(sp):
            lists = m.table.rearrange("(n s) c -> n s c", s=SLOTS)

            def load_slots(e, i, j):
                sp.dma_start(slots[i][:], lists[e * (SEQ // SLOTS) + j]).then_inc(slots_loaded[i], 16)

            def begin(T, j):
                for i in range(UNROLL - 1):
                    if not is_main(j):
                        sp.wait_ge(y_scattered[i % 2], 16 * 2 * T)
                    load_slots(i, i, j)
                if not is_main(j):
                    sp.wait_ge(low_made, 6 * UNROLL * T)
                    load_expert(nc, sp, m, layer, 0, [(part, half) for part in ("gate", "up", "down") for half in range(2)])
                refill(1, "gate", T * UNROLL, FIRST_GATE)
                refill(1, "up", T * UNROLL, UP)

            def refill(e, part, n, where):
                for half in range(2):
                    sp.wait_ge(low_made, 6 * n + where + half + 1)
                    load_expert(nc, sp, m, layer, e, ((part, half),))

            def body(T, i, e, j, last):
                n = T * UNROLL + i
                ahead = not (last and i == UNROLL - 1)
                if not (last and i >= 2):
                    refill(e + 2, "gate", n, NEXT_GATE)
                if ahead:
                    refill(e + 1, "down", n, DOWN)
                if not (last and i >= 2):
                    refill(e + 2, "up", n, NEXT_UP)
                if not last or i == 0:
                    sp.wait_ge(y_scattered[(i + 1) % 2], 16 * (2 * T + (i + 1) // 2))
                    load_slots(e + UNROLL - 1, (i + UNROLL - 1) % UNROLL, j)
            run(sp, begin, body)

        @block.gpsimd
        def _(pool):
            def gather(i, times):
                pool.wait_ge(slots_loaded[i], 16 * times)
                pool.sem_inc(gathers_begun, 1)
                nc.gpsimd.indirect_dma_start(x[i % 2][:], None, m.h_dram[:, :], bass.IndirectOffsetOnAxis(ap=slots[i][:, 0:1], axis=0),
                                             bounds_check=SEQ - 1, oob_is_err=False).then_inc(x_gathered[i], 16)

            def begin(T, j):
                if not is_main(j):
                    pool.wait_ge(x_transposed, UNROLL * T)
                for i in range(AHEAD):
                    gather(i, T + 1)

            def body(T, i, e, j, last):
                n = T * UNROLL + i
                if not (last and i >= UNROLL - AHEAD):
                    pool.wait_ge(x_transposed, n + 1)
                    gather((i + AHEAD) % UNROLL, T + 1 + (i + AHEAD) // UNROLL)
                pool.wait_ge(y_copied, 2 * n + 2)
                pool.sem_inc(scatters_begun, 1)
                nc.gpsimd.indirect_dma_start(m.y_dram[:, :], bass.IndirectOffsetOnAxis(ap=slots[i][:, 1:2], axis=0), y[i % 2][:], None,
                                             bounds_check=SEQ * TOP_K - 1, oob_is_err=False).then_inc(y_scattered[i % 2], 16)
                if last and i == UNROLL - 1:
                    for b in range(2):
                        pool.wait_ge(y_scattered[b], 16 * (2 * T + 2))
            run(pool, begin, body)

        @block.tensor
        def _(pe):
            def transpose_x(n, b, times):
                pe.wait_ge(x_gathered[b], 16 * times)
                pe.wait_ge(x_low_made, n)
                for half in range(2):
                    for q in range(4):
                        k = 4 * half + q
                        last = nc.tensor.transpose(psum_xT[half][:, q * SLOTS:(q + 1) * SLOTS], x[b % 2][:].rearrange("s (p k) -> s k p", k=KD)[:, k, :], m.ident[:])
                last.then_inc(x_transposed, 1)

            def gate(n, b, body_n, where):
                pe.wait_ge(x_low_made, n + 1)
                pe.wait_ge(silu_done, n)
                mm = product(pe, [psum_gate], x_high[b], x_low[b], "gate", body_n, where)
                mm.then_inc(gate_done, 1)

            def begin(T, j):
                transpose_x(T * UNROLL, 0, T + 1)
                gate(T * UNROLL, 0, T * UNROLL, FIRST_GATE)

            def body(T, i, e, j, last):
                n, b = T * UNROLL + i, i % 2
                ahead = not (last and i == UNROLL - 1)
                if ahead:
                    transpose_x(n + 1, (i + 1) % UNROLL, T + 1 + (i + 1) // UNROLL)
                pe.wait_ge(u_done, n)
                product(pe, [psum_up], x_high[b], x_low[b], "up", n, UP).then_inc(up_done, 1)
                pe.wait_ge(u_done, n + 1)
                pe.wait_ge(u_low_made, n)
                for q in range(KE):
                    mm = nc.tensor.transpose(psum_uT[:, q * SLOTS:(q + 1) * SLOTS], u[:].rearrange("s (p q) -> s q p", q=KE)[:, q, :], m.ident[:])
                mm.then_inc(u_transposed, 1)
                if ahead:
                    gate(n + 1, 1 - b, n, NEXT_GATE)
                pe.wait_ge(u_low_made, n + 1)
                pe.wait_ge(y_copied, 2 * n)
                product(pe, psum_y, u_high, u_low, "down", n, DOWN if ahead else LAST_DOWN).then_inc(down_done, 1)
            run(pe, begin, body)

        @block.scalar
        def _(act):
            def split_x(n, b):
                act.wait_ge(x_transposed, n + 1)
                for half in range(2):
                    nc.scalar.copy(x_high[b][:, 4 * half:4 * half + 4, :], psum_xT[half][:].rearrange("p (q s) -> p q s", q=4)).then_inc(x_high_made, 1)

            def begin(T, j):
                split_x(T * UNROLL, 0)
                make_high(act, "gate", T * UNROLL)
                make_high(act, "up", T * UNROLL)

            def body(T, i, e, j, last):
                n, b = T * UNROLL + i, i % 2
                ahead = not (last and i == UNROLL - 1)
                if ahead:
                    split_x(n + 1, 1 - b)
                    act.wait_ge(gate_done, n + 1)
                    make_high(act, "gate", n + 1, halves=(0,))
                act.wait_ge(gate_done, n + 1)
                act.wait_ge(u_done, n)
                nc.scalar.activation(silu[:], psum_gate[:], ACT.Silu).then_inc(silu_done, 1)
                if ahead:
                    make_high(act, "gate", n + 1, halves=(1,))
                act.wait_ge(u_transposed, n + 1)
                act.wait_ge(down_done, n)
                nc.scalar.copy(u_high[:], psum_uT[:].rearrange("p (q s) -> p q s", q=KE)).then_inc(u_high_made, 1)
                make_high(act, "down", n)
                if ahead:
                    act.wait_ge(up_done, n + 1)
                    make_high(act, "up", n + 1)
                act.wait_ge(down_done, n + 1)
                act.wait_ge(y_scattered[i % 2], 16 * (2 * T + i // 2))
                for half in range(2):
                    nc.scalar.copy(y[i % 2][:, half * 512:(half + 1) * 512], psum_y[half][:]).then_inc(y_copied, 1)
            run(act, begin, body)

        @block.vector
        def _(dve):
            def split_x(n, b):
                for half in range(2):
                    dve.wait_ge(x_high_made, 2 * n + half + 1)
                    low = nc.vector.tensor_tensor(x_low[b][:, 4 * half:4 * half + 4, :], psum_xT[half][:].rearrange("p (q s) -> p q s", q=4),
                                                  x_high[b][:, 4 * half:4 * half + 4, :].bitcast(F32), ALU.subtract)
                low.then_inc(x_low_made, 1)

            def begin(T, j):
                split_x(T * UNROLL, 0)
                make_low(dve, "gate", T * UNROLL, FIRST_GATE)
                make_low(dve, "up", T * UNROLL, UP)

            def body(T, i, e, j, last):
                n, b = T * UNROLL + i, i % 2
                ahead = not (last and i == UNROLL - 1)
                if ahead:
                    split_x(n + 1, 1 - b)
                    make_low(dve, "gate", n, NEXT_GATE, halves=(0,))
                dve.wait_ge(silu_done, n + 1)
                dve.wait_ge(up_done, n + 1)
                dve.wait_ge(u_transposed, n)
                nc.vector.tensor_tensor(u[:], silu[:], psum_up[:], ALU.mult).then_inc(u_done, 1)
                if ahead:
                    make_low(dve, "gate", n, NEXT_GATE, halves=(1,))
                dve.wait_ge(u_high_made, n + 1)
                nc.vector.tensor_tensor(u_low[:], psum_uT[:].rearrange("p (q s) -> p q s", q=KE), u_high[:].bitcast(F32), ALU.subtract).then_inc(u_low_made, 1)
                make_low(dve, "down", n, DOWN if ahead else LAST_DOWN)
                if ahead:
                    make_low(dve, "up", n, NEXT_UP)
            run(dve, begin, body)
    clear_semaphores(nc, [*S, *m.w_loaded["gate"], *m.w_loaded["up"], *m.w_loaded["down"]])


def moe_combine(nc, m, layer):
    last_layer = layer == DEPTH - 1
    with ExitStack() as ctx:
        ln_gain, ln_bias = [ctx.enter_context(nc.sbuf_tensor(f"{name}_c{layer}", [P, D_MODEL], F32)) for name in ("ln_gain", "ln_bias")]
        pair = [ctx.enter_context(nc.sbuf_tensor(f"pair{i}_c{layer}", [P, TOP_K, D_MODEL], F32)) for i in range(NT)]
        names = ("norm_loaded", "dve_steps", "stored", "var_ready", "root_ready", "gated", "shift_ready", "scaled",
                 "pool_multiplied", "pool_finished", "dve_multiplied", "dve_finished")
        S = [ctx.enter_context(nc.semaphore(f"{name}_c{layer}")) for name in names]
        (norm_loaded, dve_steps, stored, var_ready, root_ready, gated, shift_ready, scaled,
         pool_multiplied, pool_finished, dve_multiplied, dve_finished) = S
        pair_loaded = [ctx.enter_context(nc.semaphore(f"pair_loaded{t}_c{layer}")) for t in range(NT)]
        block = ctx.enter_context(nc.Block())

        @block.sync
        def _(sp):
            rows = m.y_dram.rearrange("(t p k) d -> t p k d", p=P, k=TOP_K)
            for t in range(NT):
                sp.dma_start(pair[t][:], rows[t]).then_inc(pair_loaded[t], 16)
            sp.dma_start(ln_gain[:], m.a["ln_g"][layer, 1].partition_broadcast(P)).then_inc(norm_loaded, 16)
            sp.dma_start(ln_bias[:], m.a["ln_b"][layer, 1].partition_broadcast(P)).then_inc(norm_loaded, 16)
            if last_layer:
                for t in range(NT):
                    sp.wait_ge(dve_finished, t + 1)
                    sp.wait_ge(pool_finished, t + 1)
                    sp.dma_start(m.out.rearrange("b (t p) d -> (b t) p d", p=P)[t], m.stream[:, t, :]).then_inc(stored, 16)
                sp.wait_ge(stored, 16 * NT)

        @block.scalar
        def _(act):
            def gate(t):
                act.wait_ge(pair_loaded[t], 16)
                nc.scalar.activation(pair[t][:, 0, :], pair[t][:, 0, :], ACT.Copy, scale=m.gates[:, t, 0:1]).then_inc(gated, 1)

            gate(0)
            gate(1)
            for t in range(NT):
                norm_root(nc, act, m.moments[:, t, :], m.ln_eps[:], t, var_ready, root_ready)
                norm_scale(nc, act, pair[t][:, 0, :], m.moments[:, t, :], t, shift_ready, scaled)
                if t + 2 < NT:
                    gate(t + 2)

        @block.gpsimd
        def _(pool):
            pool.wait_ge(norm_loaded, 32)
            for t in range(NT):
                norm_finish(nc.gpsimd, pair[t][:, 0, :], ln_gain[:], ln_bias[:], m.stream[:, t, :], POOL_SHARE, t, scaled, pool_multiplied, pool_finished)

        @block.vector
        def _(dve):
            c = Chain(dve, dve_steps)

            def combine(t):
                dve.wait_ge(gated, t + 1)
                first, second = pair[t][:, 0, :], pair[t][:, 1, :]
                c.link(nc.vector.scalar_tensor_tensor(out=first, in0=second, scalar=m.gates[:, t, 1:2], in1=first, op0=ALU.mult, op1=ALU.add))
                c.link(nc.vector.scalar_tensor_tensor(out=first, in0=m.stream[:, t, :], scalar=ALPHA, in1=first, op0=ALU.mult, op1=ALU.add))
                norm_moments(nc, c, first, m.stats, m.moments[:, t, :], var_ready)

            combine(0)
            dve.wait_ge(norm_loaded, 32)
            for t in range(NT):
                dve.wait_ge(root_ready, t + 1)
                norm_shift(nc, c, m.moments[:, t, :], shift_ready)
                if t + 1 < NT:
                    combine(t + 1)
                norm_finish(nc.vector, pair[t][:, 0, :], ln_gain[:], ln_bias[:], m.stream[:, t, :], DVE_SHARE, t, scaled, dve_multiplied, dve_finished)
    clear_semaphores(nc, [*S, *pair_loaded])


def attention_project(nc, m, heads_T, values):
    with ExitStack() as ctx:
        def sb(name, shape, dt=F32):
            return ctx.enter_context(nc.sbuf_tensor(name, shape, dt))

        sems = []

        def sem(name):
            sems.append(ctx.enter_context(nc.semaphore(name)))
            return sems[-1]

        x_raw = m.stream[:].rearrange("p t (h n) -> p (t h) n", n=SEQ)
        w_raw = [m.w_raw["gate"], m.w_raw["up"]]
        x_high, x_low = sb("x_in_high", [P, KD, SEQ], F32R), sb("x_in_low", [P, KD, SEQ], F32R)
        w_high, w_low = [[sb(f"w_in_{name}{i}", [P, KD, 512], F32R) for i in range(2)] for name in ("high", "low")]
        rot_cos, rot_sin, rot_swap = sb("rot_cos", [P, SEQ]), sb("rot_sin", [P, SEQ]), sb("rot_swap", [P, P])
        turned = [sb(f"turned{i}", [P, SEQ]) for i in range(2)]
        banks = [ctx.enter_context(nc.psum_tensor(f"psum_proj{i}", [P, 512], F32)) for i in range(4)]
        swap_banks = [ctx.enter_context(nc.psum_tensor(f"psum_swap{i}", [P, 512], F32)) for i in range(2)]
        x_loaded, rot_loaded = sem("x_loaded"), sem("rot_loaded")
        w_loaded = [sem(f"w_in_loaded{i}") for i in range(2)]
        tile_ready, copied_act, copied_dve = sem("proj_ready"), sem("proj_copied_act"), sem("proj_copied_dve")
        swapped, rotated, dve_steps = sem("swapped"), sem("rotated"), sem("proj_dve_steps")
        x_high_made, x_low_made, w_high_made, w_low_made = sem("x_high_made"), sem("x_low_made"), sem("w_high_made"), sem("w_low_made")
        halves = [slice(0, KD // 2), slice(KD // 2, KD)]
        w_in = m.a["even_w_in"][0].rearrange("(k p) n -> p k n", p=P)
        columns = [0, 1, 3, 4, 2, 5]
        block = ctx.enter_context(nc.Block())

        @block.sync
        def _(sp):
            for g, col in enumerate(columns):
                if g >= 2:
                    sp.wait_ge(w_low_made, 2 * (g - 1))
                sp.dma_start(w_raw[g % 2][:], w_in[:, :, col * 512:(col + 1) * 512]).then_inc(w_loaded[g % 2], 16)
                if g == 0:
                    sp.dma_start(x_raw, m.a["x_T"].rearrange("(k p) t -> p k t", p=P)).then_inc(x_loaded, 16)
                    for tile_, name in ((rot_cos, "rot_cos"), (rot_sin, "rot_sin"), (rot_swap, "rot_swap")):
                        sp.dma_start(tile_[:], m.a[name]).then_inc(rot_loaded, 16)
            sp.wait_ge(w_low_made, 2 * len(columns))
            load_expert(nc, sp, m, 0, 0, m.first_weights)

        @block.tensor
        def _(pe):
            def tile_of(g, f):
                n = 4 * g + f
                if n >= 4:
                    pe.wait_ge(copied_dve if n % 2 else copied_act, n // 2 - 1)
                b, tile_ = g % 2, slice(f * P, (f + 1) * P)
                for k in range(KD):
                    if f == 0 and k % (KD // 2) == 0:
                        half = k // (KD // 2)
                        pe.wait_ge(w_low_made, 2 * g + half + 1)
                        if g == 0:
                            pe.wait_ge(x_low_made, half + 1)
                    w_parts, x_parts = (w_high[b], w_low[b]), (x_high, x_low)
                    stationary, moving = (w_parts, x_parts) if g < 4 else (x_parts, w_parts)
                    for i, j in ((0, 0), (0, 1), (1, 0)):
                        mm = nc.tensor.matmul(banks[f][:], stationary[i][:, k, tile_], moving[j][:, k, :], start=(k == 0 and i + j == 0),
                                              stop=(k == KD - 1 and i == 1))
                mm.then_inc(tile_ready, 1)

            def swap(r):
                if r == 0:
                    pe.wait_ge(rot_loaded, 48)
                pe.wait_ge(copied_dve if r % 2 else copied_act, r // 2 + 1)
                if r >= 2:
                    pe.wait_ge(rotated, r - 1)
                nc.tensor.matmul(swap_banks[r % 2][:], rot_swap[:], heads_T[:, r, :], start=True, stop=True).then_inc(swapped, 1)

            for g in range(6):
                for f in range(4):
                    tile_of(g, f)
                    if 1 <= g < 3:
                        swap(4 * (g - 1) + f)

        @block.scalar
        def _(act):
            def make_high(g):
                act.wait_ge(w_loaded[g % 2], 16 * (g // 2 + 1))
                if g >= 2:
                    act.wait_ge(tile_ready, 4 * (g - 1))
                for half in halves:
                    nc.scalar.copy(w_high[g % 2][:, half, :], w_raw[g % 2][:, half, :]).then_inc(w_high_made, 1)

            make_high(0)
            act.wait_ge(x_loaded, 16)
            for half in halves:
                nc.scalar.copy(x_high[:, half, :], x_raw[:, half, :]).then_inc(x_high_made, 1)
            for n in range(0, 24, 2):
                if n % 4 == 0 and n < 20:
                    make_high(n // 4 + 1)
                act.wait_ge(tile_ready, n + 1)
                out = heads_T[:, n, :] if n < 16 else values[:, (n - 16) // 4, n % 4, :]
                scale = A_DIM ** -0.5 if n // 4 in (0, 2) else 1.0
                nc.scalar.activation(out, banks[n % 4][:], ACT.Copy, scale=scale).then_inc(copied_act, 1)

        @block.vector
        def _(dve):
            c = Chain(dve, dve_steps)

            def rotate(r):
                x = heads_T[:, r, :]
                dve.wait_ge(swapped, r + 1)
                c.mark(nc.vector.tensor_tensor(turned[r % 2][:], swap_banks[r % 2][:], rot_sin[:], ALU.mult))
                c.link(nc.vector.tensor_tensor(x, x, rot_cos[:], ALU.mult))
                nc.vector.tensor_tensor(x, x, turned[r % 2][:], ALU.add).then_inc(rotated, 1)

            def make_low(g, half):
                dve.wait_ge(w_high_made, 2 * g + half + 1)
                cut = halves[half]
                nc.vector.tensor_tensor(w_low[g % 2][:, cut, :], w_raw[g % 2][:, cut, :], w_high[g % 2][:, cut, :].bitcast(F32), ALU.subtract).then_inc(w_low_made, 1)

            for half in range(2):
                make_low(0, half)
            for half in range(2):
                cut = halves[half]
                dve.wait_ge(x_high_made, half + 1)
                nc.vector.tensor_tensor(x_low[:, cut, :], x_raw[:, cut, :], x_high[:, cut, :].bitcast(F32), ALU.subtract).then_inc(x_low_made, 1)
            for n in range(1, 24, 2):
                if n % 4 == 1 and n < 20:
                    make_low(n // 4 + 1, 0)
                    make_low(n // 4 + 1, 1)
                dve.wait_ge(tile_ready, n + 1)
                out = heads_T[:, n, :] if n < 16 else values[:, (n - 16) // 4, n % 4, :]
                scale = A_DIM ** -0.5 if n // 4 in (0, 2) else 1.0
                nc.vector.tensor_scalar(out, banks[n % 4][:], scale, None, ALU.mult).then_inc(copied_dve, 1)
                if 4 <= n < 12:
                    if n == 5:
                        dve.wait_ge(rot_loaded, 48)
                    rotate(n - 5)
                    rotate(n - 4)
    clear_semaphores(nc, sems)


def attention_heads(nc, m, heads_T, values, mixed):
    units = [(t, group, f) for t in range(NT) for group in range(2) for f in range(4)]
    N = len(units)
    with ExitStack() as ctx:
        def sb(name, shape, dt=F32):
            return ctx.enter_context(nc.sbuf_tensor(name, shape, dt))

        sems = []

        def sem(name):
            sems.append(ctx.enter_context(nc.semaphore(name)))
            return sems[-1]

        def bank(name):
            return ctx.enter_context(nc.psum_tensor(name, [P, 512], F32))

        bias = sb("rel_bias", [P, B_HEADS, SEQ])
        mask_q, mask_k = sb("mask_q", [1, P]), sb("mask_k", [1, P])
        lambda_in, lambda_prod = sb("lambda_in", [P, 4, A_DIM]), sb("lambda_prod", [P, 2, A_DIM])
        lambda_sum, lambda_exp, neg_lambda = sb("lambda_sum", [P, 2]), sb("lambda_exp", [P, 2]), sb("neg_lambda", [P, 1])
        subln_gain, subln_eps = sb("subln_gain", [P, 2 * A_DIM]), sb("subln_eps", [P, 1])
        probs = [sb(f"probs{i}", [P, 2, SEQ]) for i in range(3)]
        probs_T = [sb(f"probs_T{i}", [P, 2, SEQ]) for i in range(2)]
        neg_max = sb("neg_max", [P, N, 2])
        total = sb("total", [P, N, 2])
        inverse = sb("inverse", [P, N, 2])
        ratio = sb("ratio", [P, N])
        squares, square_sum = sb("squares", [P, P]), sb("square_sum", [P, NT * A_HEADS])
        psum_s = [[bank(f"psum_s{i}{c}") for c in range(2)] for i in range(2)]
        psum_t = [bank(f"psum_t{c}") for c in range(2)]
        psum_o = [bank(f"psum_o{i}") for i in range(2)]
        small_loaded, bias_loaded, bias_masked = sem("small_loaded"), sem("bias_loaded"), sem("bias_masked")
        scores_ready, max_ready, probs_ready, mixed_ready = sem("at_scores"), sem("at_max"), sem("at_probs"), sem("at_combined")
        turned_ready, probs_T_act, probs_T_dve = sem("at_turned"), sem("at_copied_act"), sem("at_copied_dve")
        out_ready, out_copied, dve_steps, lambda_ready = sem("at_out"), sem("at_out_copied"), sem("at_dve_steps"), sem("at_lambda")
        square_ready, root_ready = sem("at_squares"), sem("at_root")
        block = ctx.enter_context(nc.Block())

        @block.sync
        def _(sp):
            for tile_, name in ((mask_q, "mask_q"), (mask_k, "mask_k")):
                sp.dma_start(tile_[:], m.a[name]).then_inc(small_loaded, 16)
            sp.dma_start(lambda_in[:], m.a["even_lambda"][0].partition_broadcast(P)).then_inc(small_loaded, 16)
            sp.dma_start(subln_gain[:], m.a["even_subln_g"][0].partition_broadcast(P)).then_inc(small_loaded, 16)
            sp.dma_start(bias[:], m.a["rel_bias_rows"]).then_inc(bias_loaded, 16)
            sp.dma_start(m.w_out[:], m.a["even_w_out"][0].rearrange("(k p) n -> p k n", p=P)).then_inc(m.w_out_loaded, 16)

        @block.gpsimd
        def _(pool):
            pool.memset(subln_eps[:], SUBLN_EPS)
            pool.wait_ge(bias_loaded, 16)
            nc.gpsimd.tensor_scalar(bias[0:CHUNK, :, SEQ - CHUNK:SEQ], bias[0:CHUNK, :, SEQ - CHUNK:SEQ], NEG_INF, None, ALU.add).then_inc(bias_masked, 1)

        @block.tensor
        def _(pe):
            def scores(n):
                t, group, f = units[n]
                keys = P * (t + 1)
                if n >= 2:
                    pe.wait_ge(probs_ready, 2 * (n - 1))
                for c in range(2):
                    rows = slice(64 * c, 64 * c + 64)
                    out = psum_s[n % 2][c]
                    nc.tensor.matmul(out[:, 0:keys], heads_T[rows, 8 * group + f, t * P:(t + 1) * P],
                                     heads_T[rows, 8 * group + 4 + f, 0:keys], start=True, stop=False)
                    if group == 0:
                        mm = nc.tensor.matmul(out[:, keys - P:keys], mask_q[:], mask_k[:], start=False, stop=True)
                    else:
                        if n == 4:
                            pe.wait_ge(bias_masked, 1)
                        mm = nc.tensor.matmul(out[:, 0:keys], m.ident[:], bias[:, 2 * f + c, SEQ - keys:SEQ], start=False, stop=True)
                    mm.then_inc(scores_ready, 1)

            def turn(n):
                t, group, f = units[n]
                if n >= 1:
                    pe.wait_ge(probs_T_act, n)
                    pe.wait_ge(probs_T_dve, n)
                pe.wait_ge(probs_ready, 2 * n + 2)
                pe.wait_ge(mixed_ready, n + 1)
                for c in range(1 + group):
                    for j in range(t + 1):
                        tr = nc.tensor.transpose(psum_t[c][:, j * P:(j + 1) * P], probs[n % 3][:, c, j * P:(j + 1) * P], m.ident[:])
                tr.then_inc(turned_ready, 1)

            def apply(n):
                t, group, f = units[n]
                pe.wait_ge(probs_T_act, n + 1)
                pe.wait_ge(probs_T_dve, n + 1)
                if n >= 2:
                    pe.wait_ge(out_copied, n - 1)
                width = P // (1 + group)
                for c in range(1 + group):
                    for j in range(t + 1):
                        mm = nc.tensor.matmul(psum_o[n % 2][:, c * width:(c + 1) * width], probs_T[n % 2][:, c, j * P:(j + 1) * P],
                                              values[:, group, j, f * P + c * width:f * P + (c + 1) * width], start=(j == 0), stop=(j == t))
                mm.then_inc(out_ready, 1)

            pe.wait_ge(small_loaded, 64)
            for step in range(N + 3):
                if step < N:
                    scores(step)
                if 2 <= step < N + 2:
                    turn(step - 2)
                if step >= 3:
                    apply(step - 3)

        @block.scalar
        def _(act):
            act.wait_ge(lambda_ready, 1)
            nc.scalar.activation(lambda_exp[:], lambda_sum[:], ACT.Exp).then_inc(lambda_ready, 1)

            def exps(n):
                keys = P * (units[n][0] + 1)
                if n >= 3:
                    act.wait_ge(turned_ready, n - 2)
                for c in range(2):
                    act.wait_ge(max_ready, 2 * n + c + 1)
                    nc.scalar.activation(probs[n % 3][:, c, 0:keys], psum_s[n % 2][c][:, 0:keys], ACT.Exp, bias=neg_max[:, n, c:c + 1],
                                         accum_out=total[:, n, c:c + 1]).then_inc(probs_ready, 1)

            def copy_turned(n):
                t, group, f = units[n]
                act.wait_ge(turned_ready, n + 1)
                if n >= 2:
                    act.wait_ge(out_ready, n - 1)
                if group:
                    nc.scalar.copy(probs_T[n % 2][:, 1, 0:(t + 1) * P], psum_t[1][:, 0:(t + 1) * P]).then_inc(probs_T_act, 1)
                else:
                    act.sem_inc(probs_T_act, 1)

            for step in range(N + 2):
                if step < N:
                    exps(step)
                if step >= 2:
                    copy_turned(step - 2)
            act.wait_ge(square_ready, 1)
            nc.scalar.activation(square_sum[:], square_sum[:], ACT.Sqrt, bias=subln_eps[:], scale=1.0 / (2 * A_DIM)).then_inc(root_ready, 1)

        @block.vector
        def _(dve):
            c_ = Chain(dve, dve_steps)
            dve.wait_ge(small_loaded, 64)
            c_.link(nc.vector.tensor_tensor(lambda_prod[:], lambda_in[:].rearrange("p (a b) d -> p a b d", b=2)[:, :, 0, :],
                                            lambda_in[:].rearrange("p (a b) d -> p a b d", b=2)[:, :, 1, :], ALU.mult))
            nc.vector.tensor_reduce(lambda_sum[:], lambda_prod[:], AX.X, ALU.add).then_inc(lambda_ready, 1)
            dve.wait_ge(lambda_ready, 2)
            c_.link(nc.vector.tensor_tensor(neg_lambda[:], lambda_exp[:, 1:2], lambda_exp[:, 0:1], ALU.subtract))
            c_.link(nc.vector.tensor_scalar(neg_lambda[:], neg_lambda[:], -LAMBDA_INIT, None, ALU.add))
            c_.link(nc.vector.tensor_scalar(subln_gain[:], subln_gain[:], 1.0 - LAMBDA_INIT, None, ALU.mult))

            def maxima(n):
                keys = P * (units[n][0] + 1)
                for c in range(2):
                    dve.wait_ge(scores_ready, 2 * n + c + 1)
                    nc.vector.tensor_reduce(neg_max[:, n, c:c + 1], psum_s[n % 2][c][:, 0:keys], AX.X, ALU.max, negate=True).then_inc(max_ready, 1)

            def combine(n):
                t, group, f = units[n]
                keys = P * (t + 1)
                dve.wait_ge(probs_ready, 2 * n + 2)
                if group:
                    nc.vector.reciprocal(inverse[:, n, :], total[:, n, :]).then_inc(mixed_ready, 1)
                    return
                c_.link(nc.vector.reciprocal(inverse[:, n, :], total[:, n, :]))
                c_.link(nc.vector.scalar_tensor_tensor(out=ratio[:, n:n + 1], in0=total[:, n, 0:1], scalar=neg_lambda[:], in1=inverse[:, n, 1:2],
                                                       op0=ALU.mult, op1=ALU.mult))
                p = probs[n % 3]
                nc.vector.scalar_tensor_tensor(out=p[:, 0, 0:keys], in0=p[:, 1, 0:keys], scalar=ratio[:, n:n + 1], in1=p[:, 0, 0:keys],
                                               op0=ALU.mult, op1=ALU.add).then_inc(mixed_ready, 1)

            def copy_turned(n):
                t, group, f = units[n]
                dve.wait_ge(turned_ready, n + 1)
                if n >= 2:
                    dve.wait_ge(out_ready, n - 1)
                nc.vector.tensor_copy(probs_T[n % 2][:, 0, 0:(t + 1) * P], psum_t[0][:, 0:(t + 1) * P]).then_inc(probs_T_dve, 1)

            def copy_out(n):
                t, group, f = units[n]
                dve.wait_ge(out_ready, n + 1)
                out = mixed[:, t, group * 512 + f * P:group * 512 + (f + 1) * P]
                if group:
                    for c in range(2):
                        mv = nc.vector.tensor_scalar(out[:, c * 64:(c + 1) * 64], psum_o[n % 2][:, c * 64:(c + 1) * 64], inverse[:, n, c:c + 1], None, ALU.mult)
                        if c == 0:
                            c_.mark(mv)
                    mv.then_inc(out_copied, 1)
                    return
                c_.link(nc.vector.tensor_scalar(out, psum_o[n % 2][:, 0:P], inverse[:, n, 0:1], None, ALU.mult))
                nc.vector.scalar_tensor_tensor(out=squares[:], in0=out, scalar=1.0, in1=out, op0=ALU.mult, op1=ALU.mult,
                                               accum_out=square_sum[:, t * A_HEADS + f:t * A_HEADS + f + 1]).then_inc(out_copied, 1)

            for step in range(N + 3):
                if step < N:
                    maxima(step)
                if 1 <= step < N + 1:
                    combine(step - 1)
                if 2 <= step < N + 2:
                    copy_turned(step - 2)
                if step >= 3:
                    copy_out(step - 3)
            dve.wait_ge(out_copied, N)
            dve.sem_inc(square_ready, 1)
            dve.wait_ge(root_ready, 1)
            c_.link(nc.vector.reciprocal(square_sum[:], square_sum[:]))
            for t in range(NT):
                for f in range(A_HEADS):
                    o = mixed[:, t, f * P:(f + 1) * P]
                    c_.mark(nc.vector.scalar_tensor_tensor(out=o, in0=o, scalar=square_sum[:, t * A_HEADS + f:t * A_HEADS + f + 1], in1=subln_gain[:],
                                                           op0=ALU.mult, op1=ALU.mult))
    clear_semaphores(nc, sems)


def mixer_output(nc, m, layer, mixed_T, sources, residual):
    with ExitStack() as ctx:
        sems = []

        def sem(name):
            sems.append(ctx.enter_context(nc.semaphore(f"{name}_w{layer}")))
            return sems[-1]

        pre = ctx.enter_context(nc.sbuf_tensor(f"pre_w{layer}", [P, 2, D_MODEL], F32))
        ln_gain, ln_bias = [ctx.enter_context(nc.sbuf_tensor(f"{name}_w{layer}", [P, D_MODEL], F32))[:] for name in ("ln_gain", "ln_bias")]
        banks = [ctx.enter_context(nc.psum_tensor(f"psum_turn{i}_w{layer}", [P, 512], F32)) for i in range(4)]
        out_banks = [ctx.enter_context(nc.psum_tensor(f"psum_out{i}_w{layer}", [P, 512], F32)) for i in range(4)]
        transposed, copied_act, copied_dve, product_ready = sem("turned"), sem("copied_act"), sem("copied_dve"), sem("product")
        norm_loaded, added, dve_steps, var_ready, root_ready = sem("norm_loaded"), sem("added"), sem("dve_steps"), sem("var"), sem("root")
        shift_ready, scaled = sem("shift_ready"), sem("scaled")
        pool_multiplied, pool_finished, dve_multiplied, dve_finished = sem("pool_multiplied"), sem("pool_finished"), sem("dve_multiplied"), sem("dve_finished")
        block = ctx.enter_context(nc.Block())

        @block.sync
        def _(sp):
            sp.dma_start(ln_gain, m.a["ln_g"][layer, 0].partition_broadcast(P)).then_inc(norm_loaded, 16)
            sp.dma_start(ln_bias, m.a["ln_b"][layer, 0].partition_broadcast(P)).then_inc(norm_loaded, 16)
            x = m.a["x"][0] if layer == 0 else m.x_dram
            sp.dma_start(residual[:], x.rearrange("(t p) d -> p t d", p=P)).then_inc(norm_loaded, 16)
            if sources is None:
                load_expert(nc, sp, m, layer, 0, m.first_weights)

        @block.tensor
        def _(pe):
            def turn(t):
                for half in range(2):
                    n = 2 * t + half
                    if n >= 4:
                        pe.wait_ge(copied_dve if half else copied_act, t - 1)
                    for q in range(4):
                        k = 4 * half + q
                        tr = nc.tensor.transpose(banks[n % 4][:, q * P:(q + 1) * P], sources[:, t, k * P:(k + 1) * P], m.ident[:])
                    tr.then_inc(transposed, 1)

            pe.wait_ge(m.w_out_loaded, 16 * (layer + 1))
            if sources is not None:
                turn(0)
            for t in range(NT):
                if sources is not None:
                    if t + 1 < NT:
                        turn(t + 1)
                    pe.wait_ge(copied_act, t + 1)
                    pe.wait_ge(copied_dve, t + 1)
                if t >= 2:
                    pe.wait_ge(added, 2 * (t - 1))
                for half in range(2):
                    for k in range(KD):
                        mm = nc.tensor.matmul(out_banks[2 * (t % 2) + half][:], mixed_T[:, k, t * P:(t + 1) * P], m.w_out[:, k, half * 512:(half + 1) * 512],
                                              start=(k == 0), stop=(k == KD - 1))
                    mm.then_inc(product_ready, 1)

        @block.scalar
        def _(act):
            def copy(t):
                act.wait_ge(transposed, 2 * t + 1)
                nc.scalar.copy(mixed_T[:, 0:4, t * P:(t + 1) * P], banks[2 * t % 4][:].rearrange("p (q n) -> p q n", q=4)).then_inc(copied_act, 1)
            if sources is not None:
                copy(0)
            for t in range(NT):
                if sources is not None and t + 1 < NT:
                    copy(t + 1)
                norm_root(nc, act, m.moments[:, t, :], m.ln_eps[:], t, var_ready, root_ready)
                norm_scale(nc, act, pre[:, t % 2, :], m.moments[:, t, :], t, shift_ready, scaled)

        @block.gpsimd
        def _(pool):
            pool.wait_ge(norm_loaded, 48)
            for t in range(NT):
                norm_finish(nc.gpsimd, pre[:, t % 2, :], ln_gain, ln_bias, m.stream[:, t, :], POOL_SHARE, t, scaled, pool_multiplied, pool_finished)

        @block.vector
        def _(dve):
            c = Chain(dve, dve_steps)

            def copy(t):
                dve.wait_ge(transposed, 2 * t + 2)
                nc.vector.tensor_copy(mixed_T[:, 4:8, t * P:(t + 1) * P], banks[(2 * t + 1) % 4][:].rearrange("p (q n) -> p q n", q=4)).then_inc(copied_dve, 1)

            def add(t):
                for half in range(2):
                    dve.wait_ge(product_ready, 2 * t + half + 1)
                    cols = slice(half * 512, (half + 1) * 512)
                    nc.vector.scalar_tensor_tensor(out=pre[:, t % 2, cols], in0=residual[:, t, cols], scalar=ALPHA, in1=out_banks[2 * (t % 2) + half][:],
                                                   op0=ALU.mult, op1=ALU.add).then_inc(added, 1)
                dve.wait_ge(added, 2 * t + 2)
                norm_moments(nc, c, pre[:, t % 2, :], m.stats, m.moments[:, t, :], var_ready)

            if sources is not None:
                copy(0)
                copy(1)
            dve.wait_ge(norm_loaded, 48)
            add(0)
            for t in range(NT):
                if sources is not None and t + 2 < NT:
                    copy(t + 2)
                dve.wait_ge(root_ready, t + 1)
                norm_shift(nc, c, m.moments[:, t, :], shift_ready)
                if t + 1 < NT:
                    if t >= 1:
                        dve.wait_ge(pool_finished, t)
                        dve.wait_ge(dve_finished, t)
                    add(t + 1)
                norm_finish(nc.vector, pre[:, t % 2, :], ln_gain, ln_bias, m.stream[:, t, :], DVE_SHARE, t, scaled, dve_multiplied, dve_finished)
    clear_semaphores(nc, sems)


def rwkv_project(nc, m, r_T, k_T, value, logit, a_T, g_T, x_T, dx_T, mixes, weights):
    with ExitStack() as ctx:
        sems = []

        def sem(name):
            sems.append(ctx.enter_context(nc.semaphore(name)))
            return sems[-1]

        banks = [ctx.enter_context(nc.psum_tensor(f"psum_rp{i}", [P, 512], F32)) for i in range(4)]
        turn_banks = [ctx.enter_context(nc.psum_tensor(f"psum_rt{i}", [P, 512], F32)) for i in range(4)]
        x_saved, params_loaded, w_loaded = sem("x_saved"), sem("params_loaded"), [sem("rw_loaded0"), sem("rw_loaded1")]
        turned, copied_act, copied_dve, mixed, steps = sem("rx_turned"), sem("rx_copied_act"), sem("rx_copied_dve"), sem("mixed"), sem("rp_steps")
        unit_done, unit_copied, v_stored, ones_set = sem("rp_unit"), sem("rp_copied"), sem("v_stored"), sem("ones_set")
        inner = ctx.enter_context(nc.sbuf_tensor("lora_inner", [P, 4, SEQ], F32))
        tanh_w, inner_a = inner[:, 0, :], inner[:, 1, :]
        inner_g = [inner[:, 2, :], inner[0:LORA_G - P, 3, :]]
        low_in = weights[0]
        low_out = weights[1][:].rearrange("p (a b) n -> p a (b n)", b=2)
        streams = [("r", 0), ("k", 2), ("v", 3), ("w", 1), ("a", 4), ("g", 5)]
        units = [("r", f) for f in range(KD)] + [("k", f) for f in range(KD)] + [("v", n) for n in range(2 * NT)]
        units += [("w in", 0), ("a in", 0), ("g in", 0), ("g in", 1)]
        units += [("w", n) for n in range(2 * NT)] + [("a", f) for f in range(KD)] + [("g", f) for f in range(KD)]
        at = {u: n for n, u in enumerate(units)}
        last_use = [at["r", 7], at["k", 7], at["v", 7], at["w in", 0], at["a in", 0], at["g in", 1]]
        block = ctx.enter_context(nc.Block())

        @block.sync
        def _(sp):
            sp.dma_start(m.params[:], m.a["params"]).then_inc(params_loaded, 16)
            sp.dma_start(m.x_dram.rearrange("(t p) d -> p t d", p=P), m.stream[:]).then_inc(x_saved, 16)
            for n in range(6):
                s, half = n // 2, n % 2
                if n >= 2:
                    sp.wait_ge(unit_done, 8 * (s - 1) + (4 * half + 4 if s < 3 else 0))
                w = m.a["odd_w_rkv"][0, s].rearrange("(k p) n -> p k n", p=P)
                sp.dma_start(weights[half][:], w[:, :, half * 512:(half + 1) * 512]).then_inc(w_loaded[half], 16)
            sp.wait_ge(unit_done, at["v", 7] + 1)
            for name, col in (("odd_w1", 0), ("odd_a1", LORA_W), ("odd_g1", LORA_W + LORA_A)):
                w = m.a[name][0].rearrange("(k p) n -> p k n", p=P)
                sp.dma_start(low_in[:, :, col:col + w.shape[2]], w).then_inc(w_loaded[0], 16)
            sp.dma_start(low_out[0:LORA_W, 0, :], m.a["odd_w2"][0]).then_inc(w_loaded[1], 16)
            sp.dma_start(low_out[LORA_W:LORA_W + 1, 0, :], m.a["odd_w0"]).then_inc(w_loaded[1], 16)
            sp.dma_start(low_out[0:LORA_A, 1, :], m.a["odd_a2"][0]).then_inc(w_loaded[1], 16)
            sp.dma_start(low_out[:, 2, :], m.a["odd_g2"][0, 0:P]).then_inc(w_loaded[1], 16)
            sp.dma_start(low_out[0:LORA_G - P, 3, :], m.a["odd_g2"][0, P:LORA_G]).then_inc(w_loaded[1], 16)
            sp.wait_ge(unit_copied, at["v", 7] + 1)
            sp.dma_start(m.v_dram.rearrange("(t p) d -> p t d", p=P), value[:]).then_inc(v_stored, 16)
            sp.wait_ge(v_stored, 16)

        @block.gpsimd
        def _(pool):
            pool.memset(tanh_w[LORA_W:LORA_W + 1, :], 1.0).then_inc(ones_set, 1)

        @block.tensor
        def _(pe):
            for n in range(2 * NT):
                t, half = n // 2, n % 2
                if n >= 4:
                    pe.wait_ge(copied_dve if half else copied_act, t - 1)
                for q in range(4):
                    k = 4 * half + q
                    tr = nc.tensor.transpose(turn_banks[n % 4][:, q * P:(q + 1) * P], m.stream[:, t, k * P:(k + 1) * P], m.ident[:])
                tr.then_inc(turned, 1)
            for n, (name, i) in enumerate(units):
                if n >= 4:
                    pe.wait_ge(unit_copied, n - 3)
                stream = name[0]
                s = "rkvwag".index(stream)
                x = mixes[s % 2]
                if i == 0 and (len(name) > 1 or s < 3):
                    pe.wait_ge(mixed, KD * (s + 1))
                if s < 3:
                    half = i % 2 if stream == "v" else i // 4
                    if i == (0 if half == 0 else (1 if stream == "v" else 4)):
                        pe.wait_ge(w_loaded[half], 16 * (s + 1))
                    w = weights[half]
                    for k in range(KD):
                        if stream == "v":
                            left, right = x[:, k, (i // 2) * P:(i // 2 + 1) * P], w[:, k, :]
                        else:
                            left, right = w[:, k, (i % 4) * P:(i % 4 + 1) * P], x[:, k, :]
                        mm = nc.tensor.matmul(banks[n % 4][:], left, right, start=(k == 0), stop=(k == KD - 1))
                elif len(name) > 1:
                    if name == "w in":
                        pe.wait_ge(w_loaded[0], 16 * 6)
                    first = {"w in": 0, "a in": LORA_W, "g in": LORA_W + LORA_A + i * P}[name]
                    width = {"w in": LORA_W, "a in": LORA_A, "g in": (P, LORA_G - P)[i]}[name]
                    for k in range(KD):
                        mm = nc.tensor.matmul(banks[n % 4][0:width, :], low_in[:, k, first:first + width], x[:, k, :], start=(k == 0), stop=(k == KD - 1))
                elif stream == "w":
                    if i == 0:
                        pe.wait_ge(w_loaded[1], 16 * 8)
                        pe.wait_ge(ones_set, 1)
                        pe.wait_ge(unit_copied, at["w in", 0] + 1)
                    t, half = i // 2, i % 2
                    mm = nc.tensor.matmul(banks[n % 4][:], tanh_w[0:LORA_W + 1, t * P:(t + 1) * P], low_out[0:LORA_W + 1, 0, half * 512:(half + 1) * 512],
                                          start=True, stop=True)
                elif stream == "a":
                    mm = nc.tensor.matmul(banks[n % 4][:], low_out[0:LORA_A, 1, i * P:(i + 1) * P], inner_a[0:LORA_A, :], start=True, stop=True)
                else:
                    nc.tensor.matmul(banks[n % 4][:], low_out[:, 2, i * P:(i + 1) * P], inner_g[0], start=True, stop=False)
                    mm = nc.tensor.matmul(banks[n % 4][:], low_out[0:LORA_G - P, 3, i * P:(i + 1) * P], inner_g[1], start=False, stop=True)
                mm.then_inc(unit_done, 1)

        @block.scalar
        def _(act):
            for t in range(NT):
                act.wait_ge(turned, 2 * t + 1)
                nc.scalar.copy(x_T[:, 0:4, t * P:(t + 1) * P], turn_banks[2 * t % 4][:].rearrange("p (q n) -> p q n", q=4)).then_inc(copied_act, 1)
            act.wait_ge(params_loaded, 16)
            for n, (name, i) in enumerate(units):
                act.wait_ge(unit_done, n + 1)
                src = banks[n % 4]
                if name in ("r", "k"):
                    e = nc.scalar.copy((r_T if name == "r" else k_T)[:, i, :], src[:])
                elif name == "v":
                    e = nc.scalar.copy(value[:, i // 2, (i % 2) * 512:(i % 2 + 1) * 512], src[:])
                elif name == "w in":
                    e = nc.scalar.activation(tanh_w[0:LORA_W, :], src[0:LORA_W, :], ACT.Tanh)
                elif name == "a in":
                    e = nc.scalar.copy(inner_a[0:LORA_A, :], src[0:LORA_A, :])
                elif name == "g in":
                    e = nc.scalar.activation(inner_g[i], src[0:inner_g[i].shape[0], :], ACT.Sigmoid)
                elif name == "w":
                    e = nc.scalar.activation(logit[:, i // 2, (i % 2) * 512:(i % 2 + 1) * 512], src[:], ACT.Sigmoid)
                elif name == "a":
                    e = nc.scalar.activation(a_T[:, i, :], src[:], ACT.Sigmoid, bias=m.params[:, PARAM["a0"], i:i + 1])
                else:
                    e = nc.scalar.copy(g_T[:, i, :], src[:])
                e.then_inc(unit_copied, 1)

        @block.vector
        def _(dve):
            c = Chain(dve, steps)
            for t in range(NT):
                dve.wait_ge(turned, 2 * t + 2)
                nc.vector.tensor_copy(x_T[:, 4:8, t * P:(t + 1) * P], turn_banks[(2 * t + 1) % 4][:].rearrange("p (q n) -> p q n", q=4)).then_inc(copied_dve, 1)
            dve.wait_ge(x_saved, 16)
            dve.wait_ge(copied_act, NT)
            dve.wait_ge(copied_dve, NT)
            c.mark(nc.vector.tensor_scalar(dx_T[:, :, 0:1], x_T[:, :, 0:1], -1.0, None, ALU.mult))
            c.link(nc.vector.tensor_tensor(dx_T[:, :, 1:SEQ], x_T[:, :, 0:SEQ - 1], x_T[:, :, 1:SEQ], ALU.subtract))
            dve.wait_ge(params_loaded, 16)
            for s, (name, row) in enumerate(streams):
                if s >= 2:
                    dve.wait_ge(unit_done, last_use[s - 2] + 1)
                for k in range(KD):
                    nc.vector.scalar_tensor_tensor(out=mixes[s % 2][:, k, :], in0=dx_T[:, k, :], scalar=m.params[:, PARAM["mix"] + row, k:k + 1],
                                                   in1=x_T[:, k, :], op0=ALU.mult, op1=ALU.add).then_inc(mixed, 1)
    clear_semaphores(nc, sems)


def rwkv_prepare(nc, m, r_T, k_T, value, logit, a_T, decay_T, kk_T, bonus_T):
    with ExitStack() as ctx:
        sems = []

        def sem(name):
            sems.append(ctx.enter_context(nc.semaphore(name)))
            return sems[-1]

        def sb(name, shape):
            return ctx.enter_context(nc.sbuf_tensor(name, shape, F32))

        def banks(name):
            return [ctx.enter_context(nc.psum_tensor(f"{name}{i}", [P, SEQ], F32)) for i in range(2)]

        square, norm, product, v_T = sb("kk_square", [P, 2, SEQ]), sb("kk_norm", [P, 2, SEQ]), sb("rk_product", [P, 2, SEQ]), sb("v_T", [P, 2, SEQ])
        one_less = sb("one_less_k_a", [P, KD])
        sum_decay, pair_ones = sb("sum_decay", [P, P]), sb("pair_ones", [P, P])
        psum_decay, psum_norm, psum_bonus, psum_v = banks("psum_decay"), banks("psum_norm"), banks("psum_bonus"), banks("psum_v")
        consts, steps = sem("pr_consts"), sem("pr_steps")
        kk_ready, square_ready, norm_summed, norm_ready, kk_done = sem("kk_ready"), sem("kk_square_ready"), sem("norm_summed"), sem("norm_ready"), sem("kk_done")
        decay_summed, decay_copied, product_ready, bonus_summed = sem("decay_summed"), sem("decay_copied"), sem("product_ready"), sem("bonus_summed")
        v_turned, v_copied, bonus_ready = sem("v_turned"), sem("v_copied"), sem("bonus_ready")
        one_less_set, change_ready, norm_inverted = sem("one_less_set"), sem("change_ready"), sem("norm_inverted")
        block = ctx.enter_context(nc.Block())

        @block.sync
        def _(sp):
            sp.dma_start(sum_decay[:], m.a["sum_decay"]).then_inc(consts, 16)
            sp.dma_start(pair_ones[:], m.a["pair_ones"]).then_inc(consts, 16)

        @block.gpsimd
        def _(pool):
            for f in range(KD):
                pool.wait_ge(norm_inverted, f + 1)
                nc.gpsimd.tensor_tensor(kk_T[:, f, :], kk_T[:, f, :], norm[:, f % 2, :], ALU.mult).then_inc(kk_done, 1)
                pool.wait_ge(kk_done, f + 1)
                nc.gpsimd.tensor_tensor(a_T[:, f, :], a_T[:, f, :], kk_T[:, f, :], ALU.mult)

        @block.tensor
        def _(pe):
            pe.wait_ge(consts, 32)
            for f in range(KD):
                b = f % 2
                if f >= 2:
                    pe.wait_ge(decay_copied, f - 1)
                    pe.wait_ge(v_copied, f - 1)
                for t in range(NT):
                    mm = nc.tensor.matmul(psum_decay[b][:, t * P:(t + 1) * P], logit[:, t, f * P:(f + 1) * P], sum_decay[:], start=True, stop=True)
                mm.then_inc(decay_summed, 1)
                for t in range(NT):
                    tr = nc.tensor.transpose(psum_v[b][:, t * P:(t + 1) * P], value[:, t, f * P:(f + 1) * P], m.ident[:])
                tr.then_inc(v_turned, 1)
                pe.wait_ge(square_ready, f + 1)
                if f >= 2:
                    pe.wait_ge(norm_ready, f - 1)
                nc.tensor.matmul(psum_norm[b][:], pair_ones[:], square[:, b, :], start=True, stop=True).then_inc(norm_summed, 1)
                pe.wait_ge(product_ready, f + 1)
                if f >= 2:
                    pe.wait_ge(bonus_ready, f - 1)
                nc.tensor.matmul(psum_bonus[b][:], pair_ones[:], product[:, b, :], start=True, stop=True).then_inc(bonus_summed, 1)

        @block.scalar
        def _(act):
            par = m.params

            def first(f):
                b = f % 2
                nc.scalar.activation(kk_T[:, f, :], k_T[:, f, :], ACT.Copy, scale=par[:, PARAM["k_k"], f:f + 1]).then_inc(kk_ready, 1)
                if f >= 2:
                    act.wait_ge(bonus_summed, f - 1)
                nc.scalar.activation(product[:, b, :], a_T[:, f, :], ACT.Identity, bias=one_less[:, f:f + 1],
                                     scale=par[:, PARAM["k_a"], f:f + 1]).then_inc(change_ready, 1)
                if f >= 2:
                    act.wait_ge(norm_summed, f - 1)
                act.wait_ge(kk_ready, f + 1)
                nc.scalar.activation(square[:, b, :], kk_T[:, f, :], ACT.Square).then_inc(square_ready, 1)
            act.wait_ge(one_less_set, 1)
            first(0)
            for f in range(KD):
                b = f % 2
                if f + 1 < KD:
                    first(f + 1)
                act.wait_ge(decay_summed, f + 1)
                nc.scalar.copy(decay_T[:, f, :], psum_decay[b][:]).then_inc(decay_copied, 1)
                act.wait_ge(v_turned, f + 1)
                if f >= 2:
                    act.wait_ge(bonus_ready, f - 1)
                nc.scalar.copy(v_T[:, b, :], psum_v[b][:]).then_inc(v_copied, 1)
                act.wait_ge(norm_summed, f + 1)
                if f >= 2:
                    act.wait_ge(kk_done, f - 1)
                nc.scalar.activation(norm[:, b, :], psum_norm[b][:], ACT.Sqrt).then_inc(norm_ready, 1)

        @block.vector
        def _(dve):
            c = Chain(dve, steps)
            par = m.params
            nc.vector.tensor_scalar(one_less[:], par[:, PARAM["k_a"], :], -1.0, 1.0, ALU.mult, ALU.add).then_inc(one_less_set, 1)

            def keys(f):
                b = f % 2
                dve.wait_ge(change_ready, f + 1)
                c.link(nc.vector.tensor_tensor(k_T[:, f, :], k_T[:, f, :], product[:, b, :], ALU.mult))
                nc.vector.scalar_tensor_tensor(out=product[:, b, :], in0=r_T[:, f, :], scalar=par[:, PARAM["r_k"], f:f + 1], in1=k_T[:, f, :],
                                               op0=ALU.mult, op1=ALU.mult).then_inc(product_ready, 1)

            keys(0)
            for f in range(KD):
                b = f % 2
                if f + 1 < KD:
                    keys(f + 1)
                dve.wait_ge(norm_ready, f + 1)
                c.link(nc.vector.tensor_scalar(norm[:, b, :], norm[:, b, :], 1e-12, None, ALU.max))
                nc.vector.reciprocal(norm[:, b, :], norm[:, b, :]).then_inc(norm_inverted, 1)
                dve.wait_ge(bonus_summed, f + 1)
                dve.wait_ge(v_copied, f + 1)
                nc.vector.tensor_tensor(bonus_T[:, f, :], psum_bonus[b][:], v_T[:, b, :], ALU.mult).then_inc(bonus_ready, 1)
    clear_semaphores(nc, sems)


def rwkv_scan(nc, m, r_T, k_T, kka_T, decay_T, kk_T, y_T):
    with ExitStack() as ctx:
        sems = []

        def sem(name):
            sems.append(ctx.enter_context(nc.semaphore(name)))
            return sems[-1]

        def sb(name, shape=(P, PAIRS, CHUNK)):
            return ctx.enter_context(nc.sbuf_tensor(f"{name}_scan", list(shape), F32))

        def two(name):
            return [sb(f"{name}{i}") for i in range(2)]

        def bank(name):
            return ctx.enter_context(nc.psum_tensor(f"{name}_scan", [P, PAIRS, CHUNK], F32))

        masks = sb("masks", (P, N_MASKS, CHUNK))
        growth, decline = sb("growth"), sb("decline", (P, PAIRS, CHUNK + 1))
        end_decay = sb("end_decay", (P, 2, PAIRS))
        joint = (P, PAIRS, 2, CHUNK)
        A_AK, R_RK, rows_BK = [[sb(f"{name}{i}", joint) for i in range(2)] for name in ("A_AK", "R_RK", "rows_BK")]
        S_V, U_V = sb("S_V", joint), sb("U_V", joint)
        B, K, RB = two("B"), two("K"), two("RB")
        L, L_level, X, T, Z = sb("L"), two("L_level"), two("X"), sb("T"), sb("Z")
        W = sb("W")
        own = [slice(h * CHUNK, (h + 1) * CHUNK) for h in range(2)]
        other = own[::-1]
        bank_W, bank_U, bank_Y, bank_S = bank("bW"), bank("bU"), bank("bY"), bank("bS")
        bank_Z, bank_X, bank_T, bank_K = bank("bZ"), bank("bX"), bank("bT"), bank("bK")

        masks_loaded, v_loaded, state_zero, edge_set = sem("masks_loaded"), sem("v_loaded"), sem("state_zero"), sem("edge_set")
        exps_ready, a_made, b_made, k_made, r_made, end_copied = sem("exps"), sem("a_made"), sem("b_made"), sem("k_made"), sem("r_made"), sem("end_copied")
        l_ready, inter_ready, ak_used, rk_used, rb_used = sem("l_ready"), sem("inter_ready"), sem("ak_used"), sem("rk_used"), sem("rb_used")
        nt_used, l_copied, l_level_ready = sem("nt_used"), sem("l_copied"), sem("l_level_ready")
        rows_ready, k_rows_copied, b_rows_copied = sem("rows_ready"), sem("k_rows_copied"), sem("b_rows_copied")
        z_ready, z_copied, xt_ready, x_added, t_added = sem("z_ready"), sem("z_copied"), sem("xt_ready"), sem("x_added"), sem("t_added")
        w_ready, w_copied, u_ready, u_copied = sem("w_ready"), sem("w_copied"), sem("u_ready"), sem("u_copied")
        y_ready, y_copied, s_ready, s_updated = sem("y_ready"), sem("y_copied"), sem("s_ready"), sem("s_updated")
        t_begun, s_added, products_begun = sem("t_begun"), sem("s_added"), sem("products_begun")
        block = ctx.enter_context(nc.Block())

        def mask(i, rows=slice(0, P)):
            return masks[rows, i, :].unsqueeze(1).to_broadcast([rows.stop - rows.start, PAIRS, CHUNK])

        def run(engine, first, body):
            first()
            for i in range(2):
                body(i, i, True, 0)
            with engine.Fori(1, N_CHUNKS // 2 - 1) as turn:
                for i in range(2):
                    body(turn * 2 + i, i, True, turn)
            for i in range(2):
                body(N_CHUNKS - 2 + i, i, i == 0, N_CHUNKS // 2 - 1)

        def chunk(x, n, rows=slice(0, P)):
            return x[rows, :, bass.ds(n * CHUNK, CHUNK)]

        @block.sync
        def _(sp):
            v_rows = m.v_dram.rearrange("(c s) (q h v) -> c h s q v", s=CHUNK, h=2, v=CHUNK)

            def load_v(n):
                for joined in (S_V, U_V):
                    for h in range(2):
                        sp.dma_start(joined[other[h], :, h, :], v_rows[n, h]).then_inc(v_loaded, 16)

            def first():
                sp.dma_start(masks[:], m.a["scan_masks"]).then_inc(masks_loaded, 16)
                sp.wait_ge(state_zero, 1)
                load_v(0)

            def body(n, i, ahead, turn):
                if ahead:
                    sp.wait_ge(y_ready, n + 1)
                    sp.wait_ge(s_ready, n + 1)
                    load_v(n + 1)
            run(sp, first, body)

        @block.gpsimd
        def _(pool):
            pool.memset(decline[:, :, 0:1], 1.0).then_inc(edge_set, 1)
            pool.memset(S_V[:], 0.0).then_inc(state_zero, 1)

            def make_k(n, i):
                pool.wait_ge(exps_ready, 2 * n + 2)
                nc.gpsimd.tensor_tensor(K[i][:], chunk(k_T, n), growth[:], ALU.mult).then_inc(k_made, 1)

            def levels(n, i):
                pool.wait_ge(l_copied, n + 1)
                for j in range(1, LEVELS):
                    if j >= 3:
                        pool.wait_ge(z_ready, n * (LEVELS - 1) + j - 2)
                    nc.gpsimd.tensor_tensor(L_level[j % 2][:], L[:], mask(MASK_LEVEL + j), ALU.mult).then_inc(l_level_ready, 1)

            def first():
                pool.wait_ge(masks_loaded, 16)
                make_k(0, 0)
                levels(0, 0)

            def body(n, i, ahead, turn):
                if ahead:
                    pool.wait_ge(y_ready, n)
                    pool.wait_ge(z_ready, (n + 1) * (LEVELS - 1))
                    make_k(n + 1, 1 - i)
                    levels(n + 1, 1 - i)
            run(pool, first, body)

        @block.scalar
        def _(act):
            def exps(n):
                act.wait_ge(a_made, n)
                act.wait_ge(b_made, n)
                act.wait_ge(k_made, n)
                act.wait_ge(r_made, n)
                act.wait_ge(end_copied, n)
                nc.scalar.activation(decline[:, :, 1:CHUNK + 1], chunk(decay_T, n), ACT.Exp).then_inc(exps_ready, 1)
                nc.scalar.activation(growth[:], chunk(decay_T, n), ACT.Exp, scale=-1.0).then_inc(exps_ready, 1)

            def copy_l(n):
                act.wait_ge(t_begun, n + 1)
                act.wait_ge(l_level_ready, n * (LEVELS - 1))
                nc.scalar.copy(L[:], bank_X[:]).then_inc(l_copied, 1)

            def copy_z(n, j):
                act.wait_ge(z_ready, n * (LEVELS - 1) + j)
                act.wait_ge(xt_ready, n * (LEVELS - 1) + j - 1)
                nc.scalar.copy(Z[:], bank_Z[:]).then_inc(z_copied, 1)

            def copy_k_rows(n, i):
                act.wait_ge(rows_ready, 2 * n + 1)
                for h in range(2):
                    c = nc.scalar.copy(rows_BK[i][other[h], :, h, :], bank_K[other[h]])
                c.then_inc(k_rows_copied, 1)

            def copy_b_rows(n, i):
                act.wait_ge(rows_ready, 2 * n + 2)
                for h in range(2):
                    c = nc.scalar.copy(rows_BK[i][own[h], :, h, :], bank_W[own[h]])
                c.then_inc(b_rows_copied, 1)

            def first():
                exps(0)
                copy_l(0)
                copy_z(0, 1)
                copy_k_rows(0, 0)
                copy_b_rows(0, 0)
                for j in range(2, LEVELS):
                    copy_z(0, j)

            def body(n, i, ahead, turn):
                if ahead:
                    exps(n + 1)
                act.wait_ge(w_ready, n + 1)
                act.wait_ge(u_ready, n)
                nc.scalar.copy(W[:], bank_W[:]).then_inc(w_copied, 1)
                if ahead:
                    copy_l(n + 1)
                act.wait_ge(u_ready, n + 1)
                act.wait_ge(y_ready, n)
                act.wait_ge(s_ready, n)
                for h in range(2):
                    c = nc.scalar.copy(U_V[own[h], :, h, :], bank_U[own[h]])
                c.then_inc(u_copied, 1)
                if ahead:
                    copy_z(n + 1, 1)
                    copy_k_rows(n + 1, 1 - i)
                    copy_b_rows(n + 1, 1 - i)
                    copy_z(n + 1, 2)
                    copy_z(n + 1, 3)
                act.wait_ge(y_ready, n + 1)
                nc.scalar.copy(chunk(y_T, n), bank_Y[:]).then_inc(y_copied, 1)
                if ahead:
                    for j in range(4, LEVELS):
                        copy_z(n + 1, j)
            run(act, first, body)

        @block.vector
        def _(dve):
            def make_ab(n, i):
                dve.wait_ge(exps_ready, 2 * n + 1)
                for h in range(2):
                    a = nc.vector.scalar_tensor_tensor(out=A_AK[i][own[h], :, h, :], in0=chunk(kk_T, n, own[h]), scalar=-1.0, in1=decline[own[h], :, 0:CHUNK],
                                                       op0=ALU.mult, op1=ALU.mult)
                a.then_inc(a_made, 1)
                nc.vector.tensor_copy(end_decay[:, i, :], decline[:, :, CHUNK]).then_inc(end_copied, 1)
                dve.wait_ge(exps_ready, 2 * n + 2)
                nc.vector.tensor_tensor(B[i][:], chunk(kka_T, n), growth[:], ALU.mult).then_inc(b_made, 1)

            def make_r(n, i):
                for h in range(2):
                    r = nc.vector.tensor_tensor(R_RK[i][own[h], :, h, :], chunk(r_T, n, own[h]), decline[own[h], :, 1:CHUNK + 1], ALU.mult)
                r.then_inc(r_made, 1)

            def start_inverse(n, i):
                dve.wait_ge(l_ready, 2 * n + 1)
                nc.vector.tensor_tensor(X[i][:], bank_Z[:], mask(MASK_FIRST_T), ALU.mult).then_inc(nt_used, 1)
                dve.wait_ge(l_ready, 2 * n + 2)
                nc.vector.tensor_tensor(T[:], bank_X[:], mask(MASK_LEVEL), ALU.mult).then_inc(t_begun, 1)
                dve.wait_ge(nt_used, n + 1)
                nc.vector.tensor_tensor(X[i][:], X[i][:], mask(MASK_IDENT), ALU.add).then_inc(x_added, 1)
                dve.wait_ge(t_begun, n + 1)
                nc.vector.tensor_tensor(T[:], T[:], mask(MASK_IDENT), ALU.add).then_inc(t_added, 1)

            def inter(n, i, q):
                joined, src, which, used = ((A_AK[i], bank_T, MASK_BEFORE, ak_used), (R_RK[i], bank_K, MASK_UP_TO, rk_used), (None, bank_U, MASK_UP_TO, rb_used))[q]
                dve.wait_ge(inter_ready, 3 * n + q + 1)
                if joined is None:
                    nc.vector.tensor_tensor(RB[i][:], src[:], mask(which), ALU.mult).then_inc(used, 1)
                    return
                for h in range(2):
                    x = nc.vector.tensor_tensor(joined[other[h], :, h, :], src[other[h]], mask(which, other[h]), ALU.mult)
                x.then_inc(used, 1)

            def add(n, i, j):
                done = n * (LEVELS - 1) + j
                dve.wait_ge(xt_ready, done)
                dve.wait_ge(x_added, n * LEVELS + j)
                nc.vector.tensor_tensor(X[i][:], X[i][:], bank_X[:], ALU.add).then_inc(x_added, 1)
                if j < LEVELS - 1:
                    dve.wait_ge(t_added, n * (LEVELS - 1) + j)
                    nc.vector.tensor_tensor(T[:], T[:], bank_T[:], ALU.add).then_inc(t_added, 1)

            def first():
                dve.wait_ge(edge_set, 1)
                dve.wait_ge(state_zero, 1)
                dve.wait_ge(masks_loaded, 16)
                make_ab(0, 0)
                start_inverse(0, 0)
                make_r(0, 0)
                inter(0, 0, 0)
                for j in range(1, 4):
                    add(0, 0, j)
                inter(0, 0, 1)
                inter(0, 0, 2)
                for j in range(4, LEVELS):
                    add(0, 0, j)

            def body(n, i, ahead, turn):
                if ahead:
                    dve.wait_ge(w_ready, n)
                    dve.wait_ge(s_updated, n)
                    make_ab(n + 1, 1 - i)
                    start_inverse(n + 1, 1 - i)
                    dve.wait_ge(y_ready, n)
                    make_r(n + 1, 1 - i)
                    inter(n + 1, 1 - i, 0)
                    add(n + 1, 1 - i, 1)
                    add(n + 1, 1 - i, 2)
                dve.wait_ge(s_ready, n + 1)
                dve.wait_ge(w_ready, n + 1)
                dve.wait_ge(y_ready, n + 1)
                for h in range(2):
                    state = S_V[own[h], :, h, :]
                    x = nc.vector.tensor_tensor(state, state, bank_S[own[h]], ALU.add)
                x.then_inc(s_added, 1)
                dve.wait_ge(s_added, n + 1)
                for h in range(2):
                    state = S_V[own[h], :, h, :]
                    x = nc.vector.tensor_tensor(state, state, end_decay[own[h], i, :].unsqueeze(2).to_broadcast([CHUNK, PAIRS, CHUNK]), ALU.mult)
                x.then_inc(s_updated, 1)
                if ahead:
                    add(n + 1, 1 - i, 3)
                    inter(n + 1, 1 - i, 1)
                    inter(n + 1, 1 - i, 2)
                    for j in range(4, LEVELS):
                        add(n + 1, 1 - i, j)
            run(dve, first, body)

        @block.tensor
        def _(pe):
            def of_head(x, q, h):
                return x[own[h], q, h, :] if len(x.shape) == 4 else x[own[h], q, :]

            def heads(out, left, right, to=own):
                pe.sem_inc(products_begun, 1)
                for q in range(PAIRS):
                    for h in range(2):
                        mm = nc.tensor.matmul(out[to[h], q, :], of_head(left, q, h), of_head(right, q, h), start=True, stop=True)
                return mm

            def joined(out, left, right, *more, pairs=range(PAIRS)):
                pe.sem_inc(products_begun, 1)
                for q in pairs:
                    for h in range(2):
                        mm = nc.tensor.matmul(out[own[h], q, :], left[:, q, h, :], right[:, q, h, :], start=True, stop=not more)
                        if more:
                            mm = nc.tensor.matmul(out[own[h], q, :], of_head(more[0], q, h), of_head(more[1], q, h), start=False, stop=True)
                return mm

            def rows_of(out, x, to):
                pe.sem_inc(products_begun, 1)
                for q in range(PAIRS):
                    for h in range(2):
                        mm = nc.tensor.matmul(out[to[h], q, :], x[own[h], q, :], masks[own[h], MASK_IDENT, :], start=True, stop=True)
                return mm

            def products(n, i):
                pe.wait_ge(a_made, n + 1)
                pe.wait_ge(b_made, n + 1)
                pe.wait_ge(x_added, n * LEVELS)
                pe.wait_ge(t_added, n * (LEVELS - 1))
                heads(bank_Z, B[i], A_AK[i]).then_inc(l_ready, 1)
                heads(bank_X, A_AK[i], B[i]).then_inc(l_ready, 1)

            def inter_ak(n, i):
                pe.wait_ge(k_made, n + 1)
                heads(bank_T, K[i], A_AK[i], to=other).then_inc(inter_ready, 1)

            def inter_rk(n, i):
                pe.wait_ge(k_rows_copied, n + 1)
                pe.wait_ge(r_made, n + 1)
                heads(bank_K, K[i], R_RK[i], to=other).then_inc(inter_ready, 1)

            def inter_rb(n, i):
                pe.wait_ge(u_copied, n)
                heads(bank_U, B[i], R_RK[i]).then_inc(inter_ready, 1)

            def z(n, i, j):
                pe.wait_ge(l_level_ready, n * (LEVELS - 1) + j)
                pe.wait_ge(x_added, n * LEVELS + j)
                if j == 1:
                    pe.wait_ge(nt_used, n + 1)
                heads(bank_Z, L_level[j % 2], X[i]).then_inc(z_ready, 1)

            def xt(n, i, j):
                pe.wait_ge(z_copied, n * (LEVELS - 1) + j)
                pe.wait_ge(t_added, n * (LEVELS - 1) + j)
                if j == 1:
                    pe.wait_ge(l_copied, n + 1)
                    pe.wait_ge(ak_used, n + 1)
                mm = heads(bank_X, T, Z)
                if j < LEVELS - 1:
                    mm = heads(bank_T, Z, T)
                mm.then_inc(xt_ready, 1)

            def key_rows(n, i):
                pe.wait_ge(rk_used, n)
                rows_of(bank_K, K[i], other).then_inc(rows_ready, 1)

            def b_rows(n, i):
                pe.wait_ge(w_copied, n)
                pe.wait_ge(b_rows_copied, n)
                rows_of(bank_W, B[i], own).then_inc(rows_ready, 1)

            def out_y(n, i, pairs):
                pe.wait_ge(rb_used, n + 1)
                pe.wait_ge(u_copied, n + 1)
                pe.wait_ge(y_copied, n)
                return joined(bank_Y, S_V, R_RK[i], U_V, RB[i], pairs=pairs)

            def out_s(n, i):
                pe.wait_ge(k_rows_copied, n + 1)
                pe.wait_ge(b_rows_copied, n + 1)
                pe.wait_ge(u_copied, n + 1)
                pe.wait_ge(s_updated, n)
                joined(bank_S, rows_BK[i], U_V).then_inc(s_ready, 1)

            def first():
                pe.wait_ge(masks_loaded, 16)
                pe.wait_ge(state_zero, 1)
                products(0, 0)
                inter_ak(0, 0)
                z(0, 0, 1)
                key_rows(0, 0)
                xt(0, 0, 1)
                b_rows(0, 0)
                for j in (2, 3):
                    z(0, 0, j)
                    xt(0, 0, j)
                inter_rk(0, 0)
                z(0, 0, 4)
                inter_rb(0, 0)
                xt(0, 0, 4)
                z(0, 0, 5)
                xt(0, 0, 5)

            def body(n, i, ahead, turn):
                pe.wait_ge(s_updated, n)
                pe.wait_ge(ak_used, n + 1)
                pe.wait_ge(b_rows_copied, n + 1)
                pe.wait_ge(v_loaded, 64 * (n + 1))
                joined(bank_W, A_AK[i], S_V).then_inc(w_ready, 1)
                o = 1 - i
                if ahead:
                    products(n + 1, o)
                pe.wait_ge(w_copied, n + 1)
                pe.wait_ge(x_added, (n + 1) * LEVELS)
                pe.wait_ge(rb_used, n + 1)
                heads(bank_U, X[i], W).then_inc(u_ready, 1)
                if ahead:
                    inter_ak(n + 1, o)
                    z(n + 1, o, 1)
                    key_rows(n + 1, o)
                    xt(n + 1, o, 1)
                    b_rows(n + 1, o)
                    z(n + 1, o, 2)
                out_s(n, i)
                if ahead:
                    xt(n + 1, o, 2)
                out_y(n, i, range(0, PAIRS // 2))
                if ahead:
                    z(n + 1, o, 3)
                out_y(n, i, range(PAIRS // 2, PAIRS)).then_inc(y_ready, 1)
                if ahead:
                    xt(n + 1, o, 3)
                    inter_rk(n + 1, o)
                    z(n + 1, o, 4)
                    inter_rb(n + 1, o)
                    xt(n + 1, o, 4)
                    z(n + 1, o, 5)
                    xt(n + 1, o, 5)
            run(pe, first, body)
    clear_semaphores(nc, sems)


def rwkv_finish(nc, m, y_T, g_T, bonus_T, mixed_T):
    with ExitStack() as ctx:
        sems = []

        def sem(name):
            sems.append(ctx.enter_context(nc.semaphore(name)))
            return sems[-1]

        def sb(name, shape):
            return ctx.enter_context(nc.sbuf_tensor(name, shape, F32))

        heads = 2 * PAIRS
        head_mean, head_spread = sb("head_mean", [P, KD, heads]), sb("head_spread", [heads, KD, P])
        pair_centre, eps = sb("pair_centre", [P, P]), sb("lnx_eps", [P, 1])
        normed, square, root = sb("gn_normed", [P, 2, SEQ]), sb("gn_square", [P, 2, SEQ]), sb("gn_root", [heads, SEQ])
        psum_centred = [ctx.enter_context(nc.psum_tensor(f"psum_centred{i}", [P, SEQ], F32)) for i in range(2)]
        psum_scale = [ctx.enter_context(nc.psum_tensor(f"psum_scale{i}", [P, SEQ], F32)) for i in range(3)]
        psum_var = ctx.enter_context(nc.psum_tensor("psum_var", [heads, SEQ], F32))
        loaded, eps_set, bonus_shifted = sem("gn_loaded"), sem("gn_eps"), sem("bonus_shifted")
        centred_ready, centred_copied, square_ready, squares_summed, root_ready, inverse_ready = (
            sem("gn_centred"), sem("gn_copied"), sem("gn_square"), sem("gn_squares_summed"), sem("gn_root"), sem("gn_inverse"))
        scale_ready, normed_ready, summed, done = sem("gn_scale"), sem("gn_normed"), sem("gn_summed"), sem("gn_done")
        block = ctx.enter_context(nc.Block())

        @block.sync
        def _(sp):
            sp.dma_start(head_mean[:], m.a["head_mean"]).then_inc(loaded, 16)
            sp.dma_start(head_spread[:], m.a["head_spread"]).then_inc(loaded, 16)
            sp.dma_start(pair_centre[:], m.a["pair_centre"]).then_inc(loaded, 16)
            sp.dma_start(m.w_out[:], m.a["odd_w_out"][0].rearrange("(k p) n -> p k n", p=P)).then_inc(m.w_out_loaded, 16)

        @block.gpsimd
        def _(pool):
            pool.memset(eps[:], LNX_EPS).then_inc(eps_set, 1)
            for f in range(KD):
                nc.gpsimd.tensor_scalar(bonus_T[:, f, :], bonus_T[:, f, :], m.params[:, PARAM["lnx_b"], f:f + 1], None, ALU.add).then_inc(bonus_shifted, 1)
            for f in range(KD):
                pool.wait_ge(summed, f + 1)
                nc.gpsimd.tensor_tensor(mixed_T[:, f, :], normed[:, f % 2, :], g_T[:, f, :], ALU.mult).then_inc(done, 1)

        @block.tensor
        def _(pe):
            def centre(f):
                if f >= 2:
                    pe.wait_ge(centred_copied, f - 1)
                nc.tensor.matmul(psum_centred[f % 2][:], pair_centre[:], y_T[:, f, :], start=True, stop=True).then_inc(centred_ready, 1)

            pe.wait_ge(loaded, 48)
            centre(0)
            for f in range(KD):
                if f + 1 < KD:
                    centre(f + 1)
                pe.wait_ge(square_ready, f + 1)
                nc.tensor.matmul(psum_var[:], head_mean[:, f, :], square[:, f % 2, :], start=(f == 0), stop=(f == KD - 1)).then_inc(squares_summed, 1)
            pe.wait_ge(inverse_ready, 1)
            for f in range(KD):
                if f >= 3:
                    pe.wait_ge(normed_ready, f - 2)
                nc.tensor.matmul(psum_scale[f % 3][:], head_spread[:, f, :], root[:], start=True, stop=True).then_inc(scale_ready, 1)

        @block.scalar
        def _(act):
            act.wait_ge(eps_set, 1)
            for f in range(KD):
                act.wait_ge(centred_copied, f + 1)
                if f >= 2:
                    act.wait_ge(squares_summed, f - 1)
                nc.scalar.activation(square[:, f % 2, :], y_T[:, f, :], ACT.Square).then_inc(square_ready, 1)
            act.wait_ge(squares_summed, KD)
            nc.scalar.activation(root[:], psum_var[:], ACT.Sqrt, bias=eps[0:heads]).then_inc(root_ready, 1)

        @block.vector
        def _(dve):
            for f in range(KD):
                dve.wait_ge(centred_ready, f + 1)
                nc.vector.tensor_copy(y_T[:, f, :], psum_centred[f % 2][:]).then_inc(centred_copied, 1)
            dve.wait_ge(root_ready, 1)
            nc.vector.reciprocal(root[:], root[:]).then_inc(inverse_ready, 1)
            for f in range(KD):
                x = normed[:, f % 2, :]
                dve.wait_ge(scale_ready, f + 1)
                dve.wait_ge(centred_copied, f + 1)
                if f >= 2:
                    dve.wait_ge(done, f - 1)
                nc.vector.tensor_tensor(x, y_T[:, f, :], psum_scale[f % 3][:], ALU.mult).then_inc(normed_ready, 1)
                dve.wait_ge(normed_ready, f + 1)
                dve.wait_ge(bonus_shifted, f + 1)
                nc.vector.scalar_tensor_tensor(out=x, in0=x, scalar=m.params[:, PARAM["lnx_g"], f:f + 1], in1=bonus_T[:, f, :],
                                               op0=ALU.mult, op1=ALU.add).then_inc(summed, 1)
    clear_semaphores(nc, sems)


def trunk(nc, a, out):
    m = Shared(a, out)
    with ExitStack() as ctx:
        def sb(name, shape, dt=F32):
            return ctx.enter_context(nc.sbuf_tensor(name, shape, dt))

        def sem(name):
            return ctx.enter_context(nc.semaphore(name))

        def big(name, scope):
            return scope.enter_context(nc.sbuf_tensor(name, [P, KD, SEQ], F32))

        m.stream = sb("stream", [P, NT, D_MODEL])
        gate0, up0 = big("w_gate0", ctx), big("w_up0", ctx)
        m.ident, m.earlier, m.ones = sb("ident", [P, P]), sb("earlier", [P, P]), sb("ones", [P, P])
        m.expert_iota, m.group_iota, m.expert_base = sb("expert_iota", [P, N_EXPERTS]), sb("group_iota", [P, N_EXPERTS]), sb("expert_base", [P, N_EXPERTS])
        m.entries = sb("entries", [P, NT, TOP_K, 2], U32)
        m.ln_eps, m.stats, m.moments = sb("ln_eps", [P, 1]), sb("stats", [P, 2, 6]), sb("moments", [P, NT, 4])
        m.gates, m.most_tokens = sb("gates", [P, NT, TOP_K]), sb("most_tokens", [1, 1], I32)
        m.params = sb("vector_params", [P, len(PARAM) + 5, KD])

        def scratch(name, shape, dt=F32):
            return nc.dram_tensor(name, shape, dt, kind="Internal").ap()

        m.table = scratch("table", [N_EXPERTS * SEQ, 2], U32)
        m.h_dram, m.y_dram = scratch("h_dram", [SEQ, D_MODEL]), scratch("y_dram", [SEQ * TOP_K, D_MODEL])
        m.x_dram, m.v_dram = scratch("x_dram", [SEQ, D_MODEL]), scratch("v_dram", [SEQ, D_MODEL])

        m.w_loaded = {part: [sem(f"{part}_loaded{half}") for half in range(2)] for part in ("gate", "up", "down")}
        m.first_weights = [(part, half) for part in ("gate", "up") for half in range(2)]
        m.w_out_loaded, consts_loaded = sem("w_out_loaded"), sem("consts_loaded")
        m.table_entry = [sem(f"table_entry{layer}") for layer in range(DEPTH)]
        m.x_gathered = [[sem(f"x_gathered{i}_{layer}") for i in range(UNROLL)] for layer in range(DEPTH)]
        m.y_scattered = [[sem(f"y_scattered{i}_{layer}") for i in range(2)] for layer in range(DEPTH)]

        with nc.Block() as block:
            @block.sync
            def _(sp):
                consts = {"ident": m.ident, "earlier": m.earlier, "ones": m.ones, "expert_iota": m.expert_iota,
                          "group_iota": m.group_iota, "expert_base": m.expert_base, "entries": m.entries}
                for name, tile in consts.items():
                    sp.dma_start(tile[:], a[name]).then_inc(consts_loaded, 16)
                sp.wait_ge(consts_loaded, 16 * len(consts))

            @block.gpsimd
            def _(pool):
                pool.memset(m.ln_eps[:], LN_EPS)

        for layer in range(DEPTH):
            m.w_raw = {"gate": gate0, "up": up0}
            with ExitStack() as scope:
                if layer % 2 == 0:
                    heads_T = scope.enter_context(nc.sbuf_tensor("heads_T", [P, 16, SEQ], F32))
                    values = scope.enter_context(nc.sbuf_tensor("values", [P, 2, NT, 512], F32))
                    attention_project(nc, m, heads_T, values)
                    m.w_out = scope.enter_context(nc.sbuf_tensor("w_out0", [P, KD, D_MODEL], F32))
                    attention_heads(nc, m, heads_T, values, m.stream)
                    residual = values[:].rearrange("p a t n -> p (a t n)").rearrange("p (t d) -> p t d", t=NT)
                    mixer_output(nc, m, layer, heads_T[:, 0:KD, :], m.stream, residual)
                else:
                    as_features = lambda t: t[:].rearrange("p t (h n) -> p (t h) n", n=SEQ)
                    r_T, k_T, decay_T, kk_T = [big(name, scope) for name in ("r_T", "k_T", "decay_T", "kk_T")]
                    value = scope.enter_context(nc.sbuf_tensor("value", [P, NT, D_MODEL], F32))
                    bonus_T, a_T, g_T, y_T = as_features(m.stream), up0, gate0, as_features(value)
                    with ExitStack() as inner:
                        logit = inner.enter_context(nc.sbuf_tensor("logit", [P, NT, D_MODEL], F32))
                        with ExitStack() as first:
                            mixes, weights = [kk_T, big("mix1", first)], [big("w_rwkv0", first), big("w_rwkv1", first)]
                            rwkv_project(nc, m, r_T, k_T, value, logit, a_T, g_T, decay_T, as_features(m.stream), mixes, weights)
                        rwkv_prepare(nc, m, r_T, k_T, value, logit, a_T, decay_T, kk_T, bonus_T)
                    rwkv_scan(nc, m, r_T, k_T, a_T, decay_T, kk_T, y_T)
                    m.w_out = scope.enter_context(nc.sbuf_tensor("w_out1", [P, KD, D_MODEL], F32))
                    rwkv_finish(nc, m, y_T, g_T, bonus_T, r_T)
                    mixer_output(nc, m, layer, r_T, None, value)
            with ExitStack() as scope:
                m.w_raw["down"] = scope.enter_context(nc.sbuf_tensor(f"w_down_{layer}", [P, KE, D_MODEL], F32))
                m.x_rows = [scope.enter_context(nc.sbuf_tensor(f"x_rows{i}_{layer}", [SLOTS, D_MODEL], F32)) for i in range(2)]
                m.slot_rows = [scope.enter_context(nc.sbuf_tensor(f"slot_rows{i}_{layer}", [SLOTS, 2], U32)) for i in range(UNROLL)]
                moe_route(nc, m, layer)
                moe_experts(nc, m, layer)
                moe_combine(nc, m, layer)


_INPUTS = ["x", "ln_g", "ln_b", "even_w_in", "even_w_out", "even_lambda", "even_subln_g", "odd_w_rkv", "odd_w0", "odd_w1", "odd_w2",
           "odd_a1", "odd_a2", "odd_g1", "odd_g2", "odd_w_out", "router_w", "router_b", "moe_w_gate", "moe_w_up", "moe_w_down"]


def kernel(**inputs):
    import concourse.bacc as bacc
    from concourse.bass_utils import run_bass_kernel_spmd

    nc = bacc.Bacc("TRN2", target_bir_lowering=False, num_devices=1)
    given = {name: np.ascontiguousarray(inputs[name]) for name in _INPUTS}
    given.update(laid_out(inputs))
    given.update(shape_constants())
    arrays, aps = {}, {}
    for name, array in given.items():
        arrays[f"in_{name}"] = array
        aps[name] = nc.dram_tensor(f"in_{name}", array.shape, mybir.dt.from_np(array.dtype), kind="ExternalInput").ap()
    out = nc.dram_tensor("out", (1, SEQ, D_MODEL), F32, kind="ExternalOutput").ap()
    trunk(nc, aps, out)
    result = run_bass_kernel_spmd(nc, [arrays], core_ids=[0])
    return result.results[0]["out"]
```
